# Optimizing a Trainium2 kernel written in Bass

```python
import jax, jax.numpy as jnp
from jax import lax
import numpy as np
import math
import jax
import jax.numpy as jnp

D_MODEL = 1024
BATCH = 1
SEQ = 256
DEPTH = 2

N_MIXERS = 2
N_A_LAYERS = (DEPTH + 1) // 2
N_B_LAYERS = DEPTH // 2
RMS_EPS = 1e-6
NEG_INF = -1e30

A_GROUPS = ((128, 1), (512, 4), (2048, 16))
A_N_GROUPS = len(A_GROUPS)
A_HEADS = 16
A_HEAD_DIM = D_MODEL // A_HEADS
A_WIDTH = A_HEADS * A_HEAD_DIM
A_IN_WIDTH = A_N_GROUPS * 3 * A_WIDTH
ROPE_THETA = 10000.0

B_HEADS = 4
B_KEY_DIM = D_MODEL // 2 // B_HEADS
B_VAL_DIM = D_MODEL // B_HEADS
B_QK_WIDTH = B_HEADS * B_KEY_DIM
B_V_WIDTH = B_HEADS * B_VAL_DIM
B_GATE_RANK = 16
B_GATE_TAU = 16.0
B_CHUNK = 64
B_IN_WIDTH = 2 * B_QK_WIDTH + 2 * B_V_WIDTH + 2 * B_GATE_RANK

FFN_HIDDEN = -(-8 * D_MODEL // (3 * 256)) * 256


def rms_norm(x, gain):
    xf = x.astype(jnp.float32)
    y = xf * lax.rsqrt(jnp.mean(xf * xf, axis=-1, keepdims=True) + RMS_EPS)
    return (y * gain.astype(jnp.float32)).astype(x.dtype)

def rope(x, positions):
    half = x.shape[-1] // 2
    inv_freq = ROPE_THETA ** (-jnp.arange(half, dtype=jnp.float32) / half)
    ang = positions.astype(jnp.float32)[:, None] * inv_freq[None, :]
    cos = jnp.cos(ang)[:, None, :]
    sin = jnp.sin(ang)[:, None, :]
    xf = x.astype(jnp.float32)
    x1, x2 = xf[..., :half], xf[..., half:]
    return jnp.concatenate([x1 * cos - x2 * sin, x2 * cos + x1 * sin], axis=-1).astype(x.dtype)

def dilated_window_attention(q, k, v, window, dilation):
    bsz, seq, nh, dh = q.shape
    half = window // (2 * dilation)
    L = seq // dilation
    nb = -(-L // half)
    Lp = nb * half

    def to_phase(t):
        t = t.reshape(bsz, L, dilation, nh, dh)
        return jnp.moveaxis(t, 2, 1).reshape(bsz * dilation, L, nh, dh)

    n = bsz * dilation
    qp = jnp.pad(to_phase(q), ((0, 0), (0, Lp - L), (0, 0), (0, 0))).reshape(n, nb, half, nh, dh)

    def key_blocks(t):
        t = jnp.pad(to_phase(t), ((0, 0), (half, Lp - L + half), (0, 0), (0, 0)))
        t = t.reshape(n, nb + 2, half, nh, dh)
        return jnp.concatenate([t[:, :-2], t[:, 1:-1], t[:, 2:]], axis=2)

    kb = key_blocks(k)
    vb = key_blocks(v)
    tq = jnp.arange(nb)[:, None] * half + jnp.arange(half)[None, :]
    tk = jnp.arange(nb)[:, None] * half + jnp.arange(3 * half)[None, :] - half
    dist = tk[:, None, :] - tq[:, :, None]
    valid = (tk[:, None, :] >= 0) & (tk[:, None, :] < L) & (jnp.abs(dist) <= half)

    scores = jnp.einsum("nbqhd,nbkhd->nbhqk", qp.astype(jnp.float32), kb.astype(jnp.float32)) * (dh ** -0.5)
    scores = jnp.where(valid[None, :, None], scores, NEG_INF)
    m = jnp.max(scores, axis=-1, keepdims=True)
    p = jnp.exp(scores - m)
    l = jnp.sum(p, axis=-1)
    o = jnp.einsum("nbhqk,nbkhd->nbqhd", p, vb.astype(jnp.float32))
    o = o / jnp.moveaxis(l, 2, 3)[..., None]
    lse = jnp.moveaxis(m[..., 0] + jnp.log(l), 2, 3)

    def from_phase(t):
        rest = t.shape[4:]
        t = t.reshape(bsz, dilation, Lp, nh, *rest)[:, :, :L]
        return jnp.moveaxis(t, 1, 2).reshape(bsz, seq, nh, *rest)

    return from_phase(o), from_phase(lse)

def dilated_attention_mixer(h, w_in, q_gain, k_gain, w_out, positions):
    bsz, seq, _ = h.shape
    qkv = (h @ w_in).reshape(bsz, seq, A_N_GROUPS, 3, A_HEADS, A_HEAD_DIM)
    outs, lses = [], []
    for g, (window, dilation) in enumerate(A_GROUPS):
        q = rope(rms_norm(qkv[:, :, g, 0], q_gain[g]), positions)
        k = rope(rms_norm(qkv[:, :, g, 1], k_gain[g]), positions)
        v = qkv[:, :, g, 2]
        o, lse = dilated_window_attention(q, k, v, window, dilation)
        outs.append(o)
        lses.append(lse)
    alpha = jax.nn.softmax(jnp.stack(lses, axis=0), axis=0)
    out = jnp.sum(alpha[..., None] * jnp.stack(outs, axis=0), axis=0)
    return out.reshape(bsz, seq, A_WIDTH).astype(h.dtype) @ w_out

def gla_chunk(q, k, v, log_a, strict):
    bsz, nh, seq, dk = q.shape
    dv = v.shape[-1]
    nc = seq // B_CHUNK
    q = q.astype(jnp.float32).reshape(bsz, nh, nc, B_CHUNK, dk)
    k = k.astype(jnp.float32).reshape(bsz, nh, nc, B_CHUNK, dk)
    v = v.astype(jnp.float32).reshape(bsz, nh, nc, B_CHUNK, dv)
    b = jnp.cumsum(log_a.astype(jnp.float32).reshape(bsz, nh, nc, B_CHUNK, dk), axis=3)
    b_last = b[..., -1:, :]
    q_t = q * jnp.exp(b)
    k_t = k * jnp.exp(-b)
    k_end = k * jnp.exp(b_last - b)
    mask = jnp.tril(jnp.ones((B_CHUNK, B_CHUNK), dtype=bool), k=-1 if strict else 0)
    attn = jnp.where(mask, jnp.einsum("bhncd,bhnsd->bhncs", q_t, k_t), 0.0)
    o_intra = jnp.einsum("bhncs,bhnse->bhnce", attn, v)
    chunk_kv = jnp.einsum("bhncd,bhnce->bhnde", k_end, v)
    decay = jnp.exp(b_last[..., 0, :])

    def step(state, inp):
        kv_n, dec_n = inp
        return dec_n[..., None] * state + kv_n, state

    init = jnp.zeros((bsz, nh, dk, dv), jnp.float32)
    _, s_in = lax.scan(step, init, (jnp.moveaxis(chunk_kv, 2, 0), jnp.moveaxis(decay, 2, 0)))
    s_in = jnp.moveaxis(s_in, 0, 2)
    o_inter = jnp.einsum("bhncd,bhnde->bhnce", q_t, s_in)
    return (o_intra + o_inter).reshape(bsz, nh, seq, dv)

def _heads(t, nh):
    bsz, seq, _ = t.shape
    return t.reshape(bsz, seq, nh, -1).transpose(0, 2, 1, 3)

def gla_mixer(h, w_in, w_gate_f, bias_gate_f, w_gate_b, bias_gate_b, out_gain, w_out):
    bsz, seq, _ = h.shape
    proj = h @ w_in
    cuts = np.cumsum([B_QK_WIDTH, B_QK_WIDTH, B_V_WIDTH, B_V_WIDTH, B_GATE_RANK]).tolist()
    q, k, v, r, zf, zb = jnp.split(proj, cuts, axis=-1)
    q = _heads(q, B_HEADS) * (B_KEY_DIM ** -0.5)
    k = _heads(k, B_HEADS)
    v = _heads(v, B_HEADS)
    log_af = jax.nn.log_sigmoid((zf @ w_gate_f + bias_gate_f).astype(jnp.float32)) / B_GATE_TAU
    log_ab = jax.nn.log_sigmoid((zb @ w_gate_b + bias_gate_b).astype(jnp.float32)) / B_GATE_TAU
    log_af = _heads(log_af, B_HEADS)
    log_ab = _heads(log_ab, B_HEADS)
    o_f = gla_chunk(q, k, v, log_af, strict=False)
    flip = lambda t: jnp.flip(t, axis=2)
    o_b = flip(gla_chunk(flip(q), flip(k), flip(v), flip(log_ab), strict=True))
    o = (o_f + o_b).transpose(0, 2, 1, 3)
    o = rms_norm(o, out_gain).reshape(bsz, seq, B_V_WIDTH)
    o = o * jax.nn.silu(r.astype(jnp.float32))
    return o.astype(h.dtype) @ w_out

def swiglu(h, w_gate_up, w_down):
    g, u = jnp.split(h @ w_gate_up, 2, axis=-1)
    return (jax.nn.silu(g) * u) @ w_down

def first_inputs(seed: int = 0) -> dict:
    key = jax.random.key(seed)
    ks = jax.random.split(key, 16)

    def nrm(k, shape, scale):
        return jax.random.normal(k, shape, jnp.float32) * scale

    return {
        "x": nrm(ks[0], (BATCH, SEQ, D_MODEL), 1.0),
        "attn_norm": 1.0 + nrm(ks[1], (DEPTH, D_MODEL), 0.02),
        "ffn_norm": 1.0 + nrm(ks[2], (DEPTH, D_MODEL), 0.02),
        "a_w_in": nrm(ks[3], (N_A_LAYERS, D_MODEL, A_IN_WIDTH), D_MODEL ** -0.5),
        "a_q_norm": 1.0 + nrm(ks[4], (N_A_LAYERS, A_N_GROUPS, A_HEAD_DIM), 0.02),
        "a_k_norm": 1.0 + nrm(ks[5], (N_A_LAYERS, A_N_GROUPS, A_HEAD_DIM), 0.02),
        "a_w_out": nrm(ks[6], (N_A_LAYERS, A_WIDTH, D_MODEL), A_WIDTH ** -0.5),
        "b_w_in": nrm(ks[7], (N_B_LAYERS, D_MODEL, B_IN_WIDTH), D_MODEL ** -0.5),
        "b_w_gate_f": nrm(ks[8], (N_B_LAYERS, B_GATE_RANK, B_QK_WIDTH), B_GATE_RANK ** -0.5),
        "b_gate_bias_f": nrm(ks[9], (N_B_LAYERS, B_QK_WIDTH), 0.1),
        "b_w_gate_b": nrm(ks[10], (N_B_LAYERS, B_GATE_RANK, B_QK_WIDTH), B_GATE_RANK ** -0.5),
        "b_gate_bias_b": nrm(ks[11], (N_B_LAYERS, B_QK_WIDTH), 0.1),
        "b_out_norm": 1.0 + nrm(ks[12], (N_B_LAYERS, B_HEADS, B_VAL_DIM), 0.02),
        "b_w_out": nrm(ks[13], (N_B_LAYERS, B_V_WIDTH, D_MODEL), B_V_WIDTH ** -0.5),
        "ffn_w_gate_up": nrm(ks[14], (DEPTH, D_MODEL, 2 * FFN_HIDDEN), D_MODEL ** -0.5),
        "ffn_w_down": nrm(ks[15], (DEPTH, FFN_HIDDEN, D_MODEL), FFN_HIDDEN ** -0.5),
    }

def first_block(x, attn_norm, ffn_norm, a_w_in, a_q_norm, a_k_norm, a_w_out, b_w_in, b_w_gate_f, b_gate_bias_f, b_w_gate_b, b_gate_bias_b, b_out_norm, b_w_out, ffn_w_gate_up, ffn_w_down):
    positions = jnp.arange(x.shape[1])
    h = x
    for i in range(DEPTH):
        j = i // N_MIXERS
        hn = rms_norm(h, attn_norm[i])
        if i % N_MIXERS == 0:
            mix = dilated_attention_mixer(hn, a_w_in[j], a_q_norm[j], a_k_norm[j], a_w_out[j], positions)
        else:
            mix = gla_mixer(hn, b_w_in[j], b_w_gate_f[j], b_gate_bias_f[j], b_w_gate_b[j], b_gate_bias_b[j], b_out_norm[j], b_w_out[j])
        h = h + mix.astype(h.dtype)
        h = h + swiglu(rms_norm(h, ffn_norm[i]), ffn_w_gate_up[i], ffn_w_down[i]).astype(h.dtype)
    return h


DEPTH_2 = 1

CTX_LEN = 256
GRID_W = 64

ATTN_HEADS = 8
ATTN_KV_HEADS = 2
ATTN_GROUP = ATTN_HEADS // ATTN_KV_HEADS
HEAD_DIM = 128
ROPE_AXIS_DIM = HEAD_DIM // 2
Q_BLOCK = 128

GDN_HEADS = 8
GDN_DK = 128
GDN_DV = 128
GDN_CHUNK = 64
SHORT_CONV = 3

D_FF = 2816
FFN_CONV = 3

NORM_EPS = 1e-6

ATTN_Q_W = ATTN_HEADS * HEAD_DIM
ATTN_KV_W = ATTN_KV_HEADS * HEAD_DIM
GDN_QK_W = GDN_HEADS * GDN_DK
GDN_V_W = GDN_HEADS * GDN_DV
GDN_CONV_W = 2 * GDN_QK_W + GDN_V_W
IN_SPLITS = (ATTN_KV_W, ATTN_KV_W, GDN_CONV_W, 2 * GDN_HEADS, 2 * GDN_HEADS, ATTN_Q_W, GDN_V_W, 2 * D_MODEL)
CTX_COLS = 2 * ATTN_KV_W + GDN_CONV_W + 4 * GDN_HEADS
IN_COLS = CTX_COLS + ATTN_Q_W + GDN_V_W + 2 * D_MODEL


def rms_norm_2(x, gain=None):
    x32 = x.astype(jnp.float32)
    y = x32 * lax.rsqrt(jnp.mean(x32 * x32, axis=-1, keepdims=True) + NORM_EPS)
    if gain is not None:
        y = y * gain.astype(jnp.float32)
    return y.astype(x.dtype)

def l2_normalize(x):
    return x * lax.rsqrt(jnp.sum(x * x, axis=-1, keepdims=True) + NORM_EPS)

def modulate(h, shift, scale):
    return h * (1.0 + scale) + shift

def split_cols(p):
    parts, off = [], 0
    for size in IN_SPLITS:
        if off >= p.shape[-1]:
            break
        parts.append(p[..., off:off + size])
        off += size
    return parts

def dwconv_centred(x, w, b=None):
    width = w.shape[0]
    pad = width // 2
    n = x.shape[1]
    xp = jnp.pad(x, ((0, 0), (pad, pad), (0, 0)))
    y = xp[:, 0:n] * w[0]
    for j in range(1, width):
        y = y + xp[:, j:j + n] * w[j]
    return y if b is None else y + b

def axial_rope_tables(n):
    rows = n // GRID_W
    row_ids = jnp.broadcast_to(jnp.arange(rows, dtype=jnp.float32)[:, None], (rows, GRID_W)).reshape(n)
    col_ids = jnp.broadcast_to(jnp.arange(GRID_W, dtype=jnp.float32)[None, :], (rows, GRID_W)).reshape(n)
    inv_freq = ROPE_THETA ** (-jnp.arange(0, ROPE_AXIS_DIM, 2, dtype=jnp.float32) / ROPE_AXIS_DIM)
    ang = jnp.concatenate([row_ids[:, None] * inv_freq, col_ids[:, None] * inv_freq], axis=-1)
    ang = ang.reshape(n, 2, ROPE_AXIS_DIM // 2)
    return jnp.cos(ang), jnp.sin(ang)

def apply_axial_rope(x, cos, sin):
    x32 = x.astype(jnp.float32).reshape(*x.shape[:-1], 2, 2, ROPE_AXIS_DIM // 2)
    x1, x2 = x32[..., 0, :], x32[..., 1, :]
    cos = cos[None, :, None]
    sin = sin[None, :, None]
    out = jnp.stack([x1 * cos - x2 * sin, x2 * cos + x1 * sin], axis=-2)
    return out.reshape(x.shape).astype(x.dtype)

def sdpa_block(q, k, v):
    s = jnp.einsum('bqhgd,bkhd->bhgqk', q, k).astype(jnp.float32) * (HEAD_DIM ** -0.5)
    p = jax.nn.softmax(s, axis=-1).astype(v.dtype)
    return jnp.einsum('bhgqk,bkhd->bqhgd', p, v)

def latent_attention(q, k_all, v_all):
    b, n = q.shape[:2]
    nb = n // Q_BLOCK
    qb = jnp.moveaxis(q.reshape(b, nb, Q_BLOCK, *q.shape[2:]), 1, 0)
    o = lax.map(lambda q_blk: sdpa_block(q_blk, k_all, v_all), qb)
    return jnp.moveaxis(o, 0, 1).reshape(b, n, ATTN_Q_W)

def gdn_chunked(q, k, v, log_a, beta, s0, with_output):
    b, h, n, dk = q.shape
    dv = v.shape[-1]
    nc = n // GDN_CHUNK
    q = q.reshape(b, h, nc, GDN_CHUNK, dk)
    k = k.reshape(b, h, nc, GDN_CHUNK, dk)
    v = v.reshape(b, h, nc, GDN_CHUNK, dv)
    log_a = log_a.reshape(b, h, nc, GDN_CHUNK)
    beta = beta.reshape(b, h, nc, GDN_CHUNK)
    gam = jnp.cumsum(log_a, axis=-1)
    idx = jnp.arange(GDN_CHUNK)
    strict = idx[:, None] > idx[None, :]
    incl = idx[:, None] >= idx[None, :]
    dec = jnp.exp(jnp.where(incl, gam[..., :, None] - gam[..., None, :], -jnp.inf))
    kk = jnp.einsum('bhncd,bhnsd->bhncs', k, k)
    a_mat = jnp.where(strict, beta[..., :, None] * dec * kk, 0.0) + jnp.eye(GDN_CHUNK, dtype=jnp.float32)
    rhs = jnp.concatenate([beta[..., None] * v, (beta * jnp.exp(gam))[..., None] * k], axis=-1)
    uw = lax.linalg.triangular_solve(a_mat, rhs, left_side=True, lower=True, unit_diagonal=True)
    u, w = uw[..., :dv], uw[..., dv:]
    k_dec = k * jnp.exp(gam[..., -1:] - gam)[..., None]
    g_last = jnp.exp(gam[..., -1])
    xs = [u, w, k_dec, g_last]
    if with_output:
        q_dec = q * jnp.exp(gam)[..., None]
        p = dec * jnp.einsum('bhncd,bhnsd->bhncs', q, k)
        xs = xs + [q_dec, p]
    xs = tuple(jnp.moveaxis(t, 2, 0) for t in xs)

    def step(s, inp):
        u_c, w_c, kd_c, gl_c = inp[:4]
        delta = u_c - jnp.einsum('bhcd,bhde->bhce', w_c, s)
        s_new = gl_c[..., None, None] * s + jnp.einsum('bhcd,bhce->bhde', kd_c, delta)
        if with_output:
            qd_c, p_c = inp[4], inp[5]
            o = jnp.einsum('bhcd,bhde->bhce', qd_c, s) + jnp.einsum('bhcs,bhse->bhce', p_c, delta)
            return s_new, o
        return s_new, None

    s_fin, o = lax.scan(step, s0, xs)
    if with_output:
        o = jnp.moveaxis(o, 0, 2).reshape(b, h, n, dv)
    return o, s_fin

def gdn_prepare(qkv, db, da, conv_w, a_log, dt_bias):
    b, n, _ = qkv.shape
    qkv = jax.nn.silu(dwconv_centred(qkv, conv_w)).astype(jnp.float32)
    q, k, v = jnp.split(qkv, [GDN_QK_W, 2 * GDN_QK_W], axis=-1)
    q = l2_normalize(q.reshape(b, n, GDN_HEADS, GDN_DK)) * (GDN_DK ** -0.5)
    k = l2_normalize(k.reshape(b, n, GDN_HEADS, GDN_DK))
    v = v.reshape(b, n, GDN_HEADS, GDN_DV)
    q, k, v = (t.transpose(0, 2, 1, 3) for t in (q, k, v))
    beta = jax.nn.sigmoid(db.astype(jnp.float32)).reshape(b, n, 2, GDN_HEADS).transpose(2, 0, 3, 1)
    da = da.astype(jnp.float32).reshape(b, n, 2, GDN_HEADS).transpose(2, 0, 3, 1)
    log_a = -jnp.exp(a_log.astype(jnp.float32))[:, None, :, None] * jax.nn.softplus(
        da + dt_bias.astype(jnp.float32)[:, None, :, None])
    return q, k, v, log_a, beta

def gdn_bidirectional(ctx_in, lat_in, with_ctx_output):
    qc, kc, vc, lac, bc = ctx_in
    ql, kl, vl, lal, bl = lat_in
    s0 = jnp.zeros((ql.shape[0], GDN_HEADS, GDN_DK, GDN_DV), jnp.float32)
    o_lat, o_ctx = None, None
    for d in range(2):
        rev = (lambda t: jnp.flip(t, axis=2)) if d == 1 else (lambda t: t)
        oc, sc = gdn_chunked(rev(qc), rev(kc), rev(vc), rev(lac[d]), rev(bc[d]), s0, with_ctx_output)
        ol, _ = gdn_chunked(rev(ql), rev(kl), rev(vl), rev(lal[d]), rev(bl[d]), sc, True)
        o_lat = rev(ol) if o_lat is None else o_lat + rev(ol)
        if with_ctx_output:
            o_ctx = rev(oc) if o_ctx is None else o_ctx + rev(oc)
    return o_lat, o_ctx

def gdn_output(o, z, norm_w):
    b, n = z.shape[:2]
    o = rms_norm_2(o.transpose(0, 2, 1, 3), norm_w)
    y = o * jax.nn.silu(z.astype(jnp.float32).reshape(b, n, GDN_HEADS, GDN_DV))
    return y.reshape(b, n, GDN_V_W).astype(z.dtype)

def merge_branches(attn, gdn, gates, w_pa, w_pd, w_out):
    g_a, g_d = jnp.split(gates, 2, axis=-1)
    y = jax.nn.sigmoid(g_a) * (attn @ w_pa) + jax.nn.sigmoid(g_d) * (gdn @ w_pd)
    return y @ w_out

def conv_ffn(h, w_up, conv_w, conv_b, w_down):
    u = dwconv_centred(h @ w_up, conv_w, conv_b)
    g, val = jnp.split(u, 2, axis=-1)
    return (jax.nn.silu(g) * val) @ w_down

def hybrid_layer(x, ctx, c, c_ctx, w_mod, b_mod, w_in, q_norm_w, k_norm_w, conv_qkv_w, a_log, dt_bias,
                 gdn_norm_w, w_pa, w_pd, w_out, w_up, ffn_conv_w, ffn_conv_b, w_down, update_ctx):
    b, n, _ = x.shape
    cl = ctx.shape[1]
    mod_lat = jax.nn.silu(c) @ w_mod + b_mod
    mod_ctx = jax.nn.silu(c_ctx) @ w_mod + b_mod
    sh1, sc1, g1, sh2, sc2, g2 = [m[:, None, :] for m in jnp.split(mod_lat, 6, axis=-1)]
    csh1, csc1, cg1, csh2, csc2, cg2 = jnp.split(mod_ctx, 6, axis=-1)

    hx = modulate(rms_norm_2(x), sh1, sc1)
    hc = modulate(rms_norm_2(ctx), csh1, csc1)
    ak_x, av_x, qkv_x, db_x, da_x, aq_x, z_x, gate_x = split_cols(hx @ w_in)
    ak_c, av_c, qkv_c, db_c, da_c, *rest_c = split_cols(hc @ (w_in if update_ctx else w_in[:, :CTX_COLS]))

    cos, sin = axial_rope_tables(n)
    q_x = apply_axial_rope(rms_norm_2(aq_x.reshape(b, n, ATTN_HEADS, HEAD_DIM), q_norm_w), cos, sin)
    q_x = q_x.reshape(b, n, ATTN_KV_HEADS, ATTN_GROUP, HEAD_DIM)
    k_x = apply_axial_rope(rms_norm_2(ak_x.reshape(b, n, ATTN_KV_HEADS, HEAD_DIM), k_norm_w), cos, sin)
    v_x = av_x.reshape(b, n, ATTN_KV_HEADS, HEAD_DIM)
    k_c = rms_norm_2(ak_c.reshape(b, cl, ATTN_KV_HEADS, HEAD_DIM), k_norm_w)
    v_c = av_c.reshape(b, cl, ATTN_KV_HEADS, HEAD_DIM)
    attn_x = latent_attention(q_x, jnp.concatenate([k_c, k_x], axis=1), jnp.concatenate([v_c, v_x], axis=1))

    gdn_x_in = gdn_prepare(qkv_x, db_x, da_x, conv_qkv_w, a_log, dt_bias)
    gdn_c_in = gdn_prepare(qkv_c, db_c, da_c, conv_qkv_w, a_log, dt_bias)
    o_x, o_c = gdn_bidirectional(gdn_c_in, gdn_x_in, update_ctx)
    gdn_x = gdn_output(o_x, z_x, gdn_norm_w)

    x = x + g1 * merge_branches(attn_x, gdn_x, gate_x, w_pa, w_pd, w_out)
    x = x + g2 * conv_ffn(modulate(rms_norm_2(x), sh2, sc2), w_up, ffn_conv_w, ffn_conv_b, w_down)

    if update_ctx:
        aq_c, z_c, gate_c = rest_c
        q_c = rms_norm_2(aq_c.reshape(b, cl, ATTN_HEADS, HEAD_DIM), q_norm_w)
        q_c = q_c.reshape(b, cl, ATTN_KV_HEADS, ATTN_GROUP, HEAD_DIM)
        attn_c = sdpa_block(q_c, k_c, v_c).reshape(b, cl, ATTN_Q_W)
        gdn_c = gdn_output(o_c, z_c, gdn_norm_w)
        ctx = ctx + cg1 * merge_branches(attn_c, gdn_c, gate_c, w_pa, w_pd, w_out)
        ctx = ctx + cg2 * conv_ffn(modulate(rms_norm_2(ctx), csh2, csc2), w_up, ffn_conv_w, ffn_conv_b, w_down)
    return x, ctx

def second_inputs(seed: int = 0) -> dict:
    key = jax.random.key(seed)
    ks = jax.random.split(key, 22)
    f32 = jnp.float32

    def dense(k, shape, fan_in, s=1.0):
        return s * (fan_in ** -0.5) * jax.random.normal(k, shape, f32)

    dt = jnp.exp(jax.random.uniform(ks[10], (DEPTH_2, 2, GDN_HEADS), f32,
                                    minval=math.log(1e-3), maxval=math.log(1e-1)))
    return {
        'x': jax.random.normal(ks[0], (BATCH, SEQ, D_MODEL), f32),
        'c': jax.random.normal(ks[1], (BATCH, D_MODEL), f32),
        'ctx': jax.random.normal(ks[2], (BATCH, CTX_LEN, D_MODEL), f32),
        'c_ctx': jax.random.normal(ks[3], (D_MODEL,), f32),
        'w_mod': dense(ks[4], (DEPTH_2, D_MODEL, 6 * D_MODEL), D_MODEL, 0.5),
        'b_mod': 0.02 * jax.random.normal(ks[5], (DEPTH_2, 6 * D_MODEL), f32),
        'w_in': dense(ks[6], (DEPTH_2, D_MODEL, IN_COLS), D_MODEL),
        'q_norm_w': 1.0 + 0.05 * jax.random.normal(ks[7], (DEPTH_2, HEAD_DIM), f32),
        'k_norm_w': 1.0 + 0.05 * jax.random.normal(ks[8], (DEPTH_2, HEAD_DIM), f32),
        'conv_qkv_w': dense(ks[9], (DEPTH_2, SHORT_CONV, GDN_CONV_W), SHORT_CONV),
        'a_log': jnp.log(jax.random.uniform(ks[11], (DEPTH_2, 2, GDN_HEADS), f32, minval=1.0, maxval=16.0)),
        'dt_bias': dt + jnp.log(-jnp.expm1(-dt)),
        'gdn_norm_w': 1.0 + 0.05 * jax.random.normal(ks[12], (DEPTH_2, GDN_DV), f32),
        'w_pa': dense(ks[13], (DEPTH_2, ATTN_Q_W, D_MODEL), ATTN_Q_W),
        'w_pd': dense(ks[14], (DEPTH_2, GDN_V_W, D_MODEL), GDN_V_W),
        'w_out': dense(ks[15], (DEPTH_2, D_MODEL, D_MODEL), D_MODEL),
        'w_up': dense(ks[16], (DEPTH_2, D_MODEL, 2 * D_FF), D_MODEL),
        'ffn_conv_w': dense(ks[17], (DEPTH_2, FFN_CONV, 2 * D_FF), FFN_CONV),
        'ffn_conv_b': 0.02 * jax.random.normal(ks[18], (DEPTH_2, 2 * D_FF), f32),
        'w_down': dense(ks[19], (DEPTH_2, D_FF, D_MODEL), D_FF),
        'final_norm_w': 1.0 + 0.05 * jax.random.normal(ks[20], (D_MODEL,), f32),
    }

def second_block(x, c, ctx, c_ctx, w_mod, b_mod, w_in, q_norm_w, k_norm_w, conv_qkv_w, a_log, dt_bias,
              gdn_norm_w, w_pa, w_pd, w_out, w_up, ffn_conv_w, ffn_conv_b, w_down, final_norm_w):
    for layer in range(DEPTH_2):
        x, ctx = hybrid_layer(
            x, ctx, c, c_ctx, w_mod[layer], b_mod[layer], w_in[layer], q_norm_w[layer], k_norm_w[layer],
            conv_qkv_w[layer], a_log[layer], dt_bias[layer], gdn_norm_w[layer], w_pa[layer], w_pd[layer],
            w_out[layer], w_up[layer], ffn_conv_w[layer], ffn_conv_b[layer], w_down[layer],
            update_ctx=layer < DEPTH_2 - 1)
    return rms_norm_2(x, final_norm_w)


def setup_inputs(seed=0):
    out = dict(first_inputs(seed))
    for name, value in second_inputs(seed + 1).items():
        if name != "x":
            out[name + "_2"] = value
    return out


def reference(
    x, attn_norm, ffn_norm, a_w_in, a_q_norm, a_k_norm, a_w_out, b_w_in, b_w_gate_f,
    b_gate_bias_f, b_w_gate_b, b_gate_bias_b, b_out_norm, b_w_out, ffn_w_gate_up, ffn_w_down,
    c_2, ctx_2, c_ctx_2, w_mod_2, b_mod_2, w_in_2, q_norm_w_2, k_norm_w_2, conv_qkv_w_2,
    a_log_2, dt_bias_2, gdn_norm_w_2, w_pa_2, w_pd_2, w_out_2, w_up_2, ffn_conv_w_2,
    ffn_conv_b_2, w_down_2, final_norm_w_2,
):
    x = first_block(
        x, attn_norm, ffn_norm, a_w_in, a_q_norm, a_k_norm, a_w_out, b_w_in, b_w_gate_f,
        b_gate_bias_f, b_w_gate_b, b_gate_bias_b, b_out_norm, b_w_out, ffn_w_gate_up,
        ffn_w_down,
    )
    return second_block(
        x, c_2, ctx_2, c_ctx_2, w_mod_2, b_mod_2, w_in_2, q_norm_w_2, k_norm_w_2, conv_qkv_w_2,
        a_log_2, dt_bias_2, gdn_norm_w_2, w_pa_2, w_pd_2, w_out_2, w_up_2, ffn_conv_w_2,
        ffn_conv_b_2, w_down_2, final_norm_w_2,
    )


_drawn_inputs = setup_inputs


def setup_inputs(seed=0):
    import zlib

    import numpy as np

    out = dict(_drawn_inputs(seed))
    spreads = {}
    factors = {'a_q_norm': 8.0,
     'a_k_norm': 8.0,
     'b_gate_bias_f': 3.76,
     'b_gate_bias_b': 3.673,
     'b_out_norm': 15.504,
     'ctx_2': 19.087,
     'c_ctx_2': 10.196,
     'b_mod_2': 4.142,
     'q_norm_w_2': 200.0,
     'k_norm_w_2': 200.0,
     'a_log_2': 3.342,
     'gdn_norm_w_2': 41.039,
     'ffn_conv_b_2': 34.761}
    for name, (base, spread) in spreads.items():
        noise = np.random.default_rng([zlib.crc32(name.encode()), seed]).standard_normal(out[name].shape)
        drawn = base * np.exp(spread * noise) if base else spread * noise
        out[name] = jnp.asarray(drawn.astype(out[name].dtype))
    for name, factor in factors.items():
        out[name] = (out[name] * factor).astype(out[name].dtype)
    return out
```

```python
from contextlib import contextmanager

import concourse.bass as bass
from concourse import mybir
import numpy as np

F32 = mybir.dt.float32
F32R = mybir.dt.float32r
I32 = mybir.dt.int32
ALU = mybir.AluOpType
ACT = mybir.ActivationFunctionType
AX = mybir.AxisListType

P = 128
D = 1024
KT = D // P
SEQ = 256
TT = SEQ // P
EPS = 1e-6
CW = 512
HK = 4

A_GROUPS = ((128, 1), (512, 4), (2048, 16))
NG = len(A_GROUPS)
A_HEADS, A_HD = 16, 64
GLA_HEADS, GLA_DK, GLA_DV, GLA_RANK, GLA_TAU = 4, 128, 256, 16, 16.0
CHUNK = 64
NCH = SEQ // CHUNK
FF = 2816
FT = FF // P
N_FFC = FF // 256
NH2, KV2, HD2 = 8, 2, 128
GROUP2 = NH2 // KV2
GDN_HEADS, GDN_D = 8, 128
NT2 = 4
LEVELS = (1, 2, 4, 8, 16, 32)
GDN_PER = dict(pe=80, act=41, dve=51, pool=6)


def constants():
    p = np.arange(P)
    f32 = np.float32
    c = {}
    c["ident"] = np.eye(P, dtype=f32)
    same = p[:, None] // CHUNK == p[None, :] // CHUNK
    c["gla_f"] = (same & (p[:, None] <= p[None, :])).astype(np.int32).view(f32)
    c["gla_b"] = (same & (p[:, None] > p[None, :])).astype(np.int32).view(f32)
    c["cum_f"] = (same & (p[:, None] <= p[None, :])).astype(f32)
    c["cum_b"] = (same & (p[:, None] >= p[None, :])).astype(f32)
    c["ones_bd"] = same.astype(f32)
    c["even"] = np.repeat((p[:, None] < CHUNK), P, 1).astype(f32)
    c["odd"] = np.repeat((p[:, None] >= CHUNK), P, 1).astype(f32)
    c["ones"] = np.ones((P, P), f32)
    c["neg_f"] = np.where(same & (p[:, None] <= p[None, :]), 0, -1e30).astype(f32)
    c["neg_b"] = np.where(same & (p[:, None] >= p[None, :]), 0, -1e30).astype(f32)
    for b in LEVELS:
        m = (p[:, None] // (2 * b) == p[None, :] // (2 * b)) & (p[:, None] // b != p[None, :] // b)
        c[f"level{b}"] = m.astype(f32)
    tok = np.arange(SEQ).reshape(TT, P).T.astype(f32)
    half = A_HD // 2
    inv = (10000.0 ** (-np.arange(half, dtype=f32) / half)).astype(f32)
    ang = (tok[:, :, None] * inv).astype(f32)
    c["cos_a"] = np.concatenate([np.cos(ang)] * 2, -1).astype(f32).reshape(P, -1)
    c["sin_a"] = np.concatenate([-np.sin(ang), np.sin(ang)], -1).astype(f32).reshape(P, -1)
    inv = (10000.0 ** (-np.arange(0, 64, 2, dtype=f32) / 64)).astype(f32)
    both = []
    for ids in (tok // 64, tok % 64):
        a = (ids.astype(f32)[:, :, None] * inv).astype(f32)
        both.append((np.concatenate([np.cos(a)] * 2, -1), np.concatenate([-np.sin(a), np.sin(a)], -1)))
    c["cos_2"] = np.concatenate([both[0][0], both[1][0]], -1).astype(f32).reshape(P, -1)
    c["sin_2"] = np.concatenate([both[0][1], both[1][1]], -1).astype(f32).reshape(P, -1)
    return c


def attention_masks():
    i, j = np.arange(SEQ)[:, None], np.arange(SEQ)[None, :]
    m = [np.where((abs(i - j) <= w // 2) & ((i - j) % d == 0), 0, -1e30) for w, d in A_GROUPS]
    m = np.stack(m, 1).astype(np.float32)
    return np.ascontiguousarray(m.reshape(TT, P, NG, SEQ).transpose(1, 0, 2, 3)).reshape(P, -1)


class Counter:

    def __init__(self, nc, name):
        self.sem, self.name, self.n = nc.alloc_semaphore(name), name, 0
        self.var, self.per, self.top = None, 0, 0

    def inc(self, ins, by=1):
        ins.then_inc(self.sem, by)
        self.n += by
        return (self, self.n, self.var is not None)

    def now(self):
        return (self, self.n, self.var is not None)

    def back(self, k):
        return (self, max(self.n - k, 0), self.var is not None)


def w(eng, *marks):
    best = {}
    for m in marks:
        if m is not None and (m[0] not in best or best[m[0]][1] <= m[1]):
            best[m[0]] = m
    for c, v, moving in best.values():
        if moving and c.var is not None and c.per:
            eng.wait_ge(c.sem, c.var * c.per + v)
        elif v > 0:
            eng.wait_ge(c.sem, v)


def bc(ap, axis, n):
    ap = ap.unsqueeze(axis)
    shape = list(ap.shape)
    shape[axis] = n
    return ap.to_broadcast(shape)


def build(nc, ins, out, const_at, vec_at, row_at):
    pe, act, dve, pool, sp = nc.tensor, nc.scalar, nc.vector, nc.gpsimd, nc.sync
    T, A, V, G = (Counter(nc, "s_" + n) for n in ("pe", "act", "dve", "pool"))
    raw_in = [Counter(nc, f"s_raw{i}") for i in range(2)]
    hi_ok = [Counter(nc, f"s_hi{i}") for i in range(2)]
    lo_ok = [Counter(nc, f"s_lo{i}") for i in range(2)]
    used = [Counter(nc, f"s_used{i}") for i in range(2)]
    L = Counter(nc, "s_small")
    stored = Counter(nc, "s_stored")
    counters = [T, A, V, G, *raw_in, *hi_ok, *lo_ok, *used]

    def w_apart(eng, *marks):
        w(eng, *marks)
        if eng is dve:
            dve.memset(unused[:, 0:1], 0.0)
        else:
            pool.tensor_tensor(unused[:, 2:3], unused[:, 1:2], unused[:, 1:2], ALU.add)

    @contextmanager
    def loop(n, chunks, **per):
        names = dict(pe=T, act=A, dve=V, pool=G)
        each = {c: 0 for c in counters}
        each.update({names[k]: v for k, v in per.items()})
        each.update({c: chunks for c in (*hi_ok, *lo_ok, *used)})
        each.update({c: 32 * chunks for c in raw_in})
        with nc.Fori(0, n) as i:
            for c in counters:
                c.var, c.per, c.top = i, each[c], c.n
            yield i
            made = {c.name: (c.n - c.top, c.per) for c in counters}
            assert all(a == b for a, b in made.values()), f"increments per iteration: {made}"
            for c in counters:
                c.n, c.var = c.top + n * c.per, None

    at = [nc.sbuf_base + (-nc.sbuf_base) % 64]

    def place(name, shape, dt=F32, offset=None):
        n = int(np.prod(shape[1:]))
        t = nc.alloc_sbuf_tensor_at(name, shape, dt, offset=at[0] if offset is None else offset)
        if offset is None:
            at[0] += 4 * n
        return t

    ps = nc.alloc_psum_tensor("ps", [P, 8, 512], F32)
    raw = place("raw", [P, 2, HK, CW])
    whi = place("whi", [P, 2, HK, CW], F32R)
    wlo = place("wlo", [P, 2, HK, CW], F32R)
    resid = place("resid", [P, TT, D])
    cst = place("cst", [P, ins["consts"].shape[1]])
    vec = place("vec", [P, ins["vecs"].shape[1]])
    modcol = place("modcol", [P, 4, KT, 2])
    grow = place("grow", [P, 2, D])
    ccur = place("ccur", [P, 2, 16])
    unused = place("unused", [P, 8])
    xs = place("xs", [P, 4, KT, SEQ], F32R)
    arena_at = at[0]
    arena_n = (nc.sbuf_usable_end - arena_at) // 4 // 8 * 8
    hid = place("hid", [P, 2, FT, SEQ], F32R, offset=arena_at + 4 * (arena_n - 2 * FT * SEQ))
    XS = 4 * KT * SEQ
    wide = place("wide", [P, arena_n + XS], offset=arena_at - 4 * XS)

    class Carve:

        def __init__(self, start=0, end=arena_n):
            self.at, self.end = start, end

        def __call__(self, *shape):
            n = int(np.prod(shape))
            v = wide[:, XS + self.at:XS + self.at + n]
            self.at += n
            assert self.at <= self.end, (self.at, self.end)
            names = "abcdef"[:len(shape)]
            if len(shape) > 1:
                v = v.rearrange(f"p ({' '.join(names)}) -> p {' '.join(names)}", **dict(zip(names, shape)))
            return v

    def const(name):
        a, b = const_at[name]
        return cst[:, a:b]

    def vcol(name):
        a, b = vec_at[name]
        return vec[:, a:b]

    def load_row(dst, name):
        a, b = row_at[name]
        L.inc(act.dma_start(dst, ins["rows"][a:b].partition_broadcast(P)), 16)

    ident = const("ident")

    def xh(k, t0, t1, seq=0):
        return xs[:, 2 * seq, k, t0:t1]

    def xl(k, t0, t1, seq=0):
        return xs[:, 2 * seq + 1, k, t0:t1]

    def request(source):
        if source is None:
            return
        for s in range(2):
            srcs, nk = source(s)
            w(sp, hi_ok[s].now(), lo_ok[s].now())
            for (k0, k1, c0, c1), src in srcs:
                raw_in[s].inc(sp.dma_start(raw[:, s, k0:k1, c0:c1], src), 16)
            w(act, raw_in[s].now(), used[s].now())
            hi_ok[s].inc(act.activation(whi[:, s, 0:nk, :], raw[:, s, 0:nk, :], ACT.Copy))
            w(dve, raw_in[s].now(), hi_ok[s].now())
            lo_ok[s].inc(dve.tensor_tensor(wlo[:, s, 0:nk, :], raw[:, s, 0:nk, :],
                                           whi[:, s, 0:nk, :].bitcast(F32), ALU.subtract))

    def cols(wmat, c0, k0=0, nks=(HK, HK)):
        def source(s):
            nk, kk = nks[s], k0 + (nks[0] if s else 0)
            h = nk // 2
            return [((j * h, (j + 1) * h, 0, CW),
                     wmat[(kk + j * h) * P:(kk + (j + 1) * h) * P, bass.ds(c0, CW)].rearrange("(k p) n -> p k n", p=P))
                    for j in range(2)], nk
        return source

    def gate_up(wmat, c):
        def source(s):
            return [((0, HK, 256 * j, 256 * (j + 1)),
                     wmat[s * HK * P:(s + 1) * HK * P, bass.ds(c * 256 + j * FF, 256)].rearrange("(k p) n -> p k n", p=P))
                    for j in range(2)], HK
        return source

    def mm3(o, ahi, alo, bhi, blo, start, stop):
        pe.matmul(o, ahi, bhi, start=start, stop=False)
        pe.matmul(o, ahi, blo, start=False, stop=False)
        return pe.matmul(o, alo, bhi, start=False, stop=stop)

    def chunk_tok(banks, tiles=(0, 1), width=CW):
        for s in range(2):
            w(pe, hi_ok[s].now(), lo_ok[s].now())
            for b, t in zip(banks, tiles):
                for k in range(HK):
                    kk, t0 = s * HK + k, (t % 2) * P
                    i_ = mm3(ps[:, b, 0:width], xh(kk, t0, t0 + P, t // 2), xl(kk, t0, t0 + P, t // 2),
                             whi[:, s, k, 0:width], wlo[:, s, k, 0:width],
                             s == 0 and k == 0, s == 1 and k == HK - 1)
            m = used[s].inc(i_)
        return m

    def chunk_feat(banks, both=False):
        n = 2 * SEQ if both else SEQ
        for s in range(2):
            w(pe, hi_ok[s].now(), lo_ok[s].now())
            for mb, b in enumerate(banks):
                for k in range(HK):
                    kk = s * HK + k
                    if both:
                        rh, rl = xs[:, 0:4:2, kk, :], xs[:, 1:4:2, kk, :]
                    else:
                        rh, rl = xs[:, 0, kk, :], xs[:, 1, kk, :]
                    i_ = mm3(ps[:, b, 0:n], whi[:, s, k, mb * P:(mb + 1) * P],
                             wlo[:, s, k, mb * P:(mb + 1) * P], rh, rl,
                             s == 0 and k == 0, s == 1 and k == HK - 1)
            m = used[s].inc(i_)
        return m

    def settle(*engs):
        for e in engs or (pe, act, dve, pool):
            w(e, T.now(), A.now(), V.now(), G.now(), used[0].now(), used[1].now())

    def rstd_of(src, n, width, st, sq):
        for j in range(n):
            w(act, A.now())
            A.inc(act.activation(sq, src[:, j, :], ACT.Square, accum_out=st[:, j:j + 1]))
        w(dve, A.now())
        V.inc(dve.tensor_scalar(st[:, 0:n], st[:, 0:n], 1.0 / width, EPS, ALU.mult, ALU.add))
        w(act, V.now())
        A.inc(act.activation(st[:, 0:n], st[:, 0:n], ACT.Sqrt))
        w(dve, A.now())
        V.inc(dve.reciprocal(st[:, 0:n], st[:, 0:n]))

    def to_split(src, seq, stage, scale=None, shift=None):
        read = [None, None]
        for g in range(KT // 2):
            b = g % 2
            w(pe, read[b])
            for j in range(2):
                for t in range(TT):
                    i_ = pe.transpose(ps[:, b, (j * 2 + t) * P:(j * 2 + t + 1) * P], src(t, 2 * g + j), ident)
            m = T.inc(i_)
            view = ps[:, b, :].rearrange("p (k n) -> p k n", k=2)
            stv = stage[:, b, :].rearrange("p (k n) -> p k n", k=2)
            w(dve, m, V.now())
            if scale is None:
                V.inc(dve.tensor_copy(stv, view))
            else:
                V.inc(dve.tensor_tensor(stv, view, bc(scale[:, 2 * g:2 * g + 2], 2, SEQ), ALU.mult))
            read[b] = V.now()
            if shift is not None:
                w(dve, V.now())
                V.inc(dve.tensor_tensor(stv, stv, bc(shift[:, 2 * g:2 * g + 2], 2, SEQ), ALU.add))
            w(act, V.now())
            hs = xs[:, 2 * seq, 2 * g:2 * g + 2, :]
            A.inc(act.activation(hs, stv, ACT.Copy))
            w(dve, A.now())
            V.inc(dve.tensor_tensor(xs[:, 2 * seq + 1, 2 * g:2 * g + 2, :], stv, hs.bitcast(F32), ALU.subtract))
        w(pe, A.now(), V.now())

    def norm_split(src, seq, c, scale, shift=None):
        st, sq, xn, stage = c(8), c(D), c(TT, D), c(2, 512)
        settle()
        rstd_of(src, TT, D, st, sq)
        w(dve, V.now())
        for t in range(TT):
            V.inc(dve.tensor_scalar(xn[:, t, :], src[:, t, :], st[:, t:t + 1], None, ALU.mult))
        w(pe, V.now())
        to_split(lambda t, k: xn[:, t, k * P:(k + 1) * P], seq, stage, scale, shift)

    def add_product(wmat, nxt, gate=None, tmp=None):
        for n in range(2):
            m = chunk_tok((2 * n, 2 * n + 1))
            request(cols(wmat, CW) if n == 0 else nxt)
            o = resid[:, :, n * CW:(n + 1) * CW]
            w(dve, m, V.now())
            if gate is None:
                V.inc(dve.tensor_tensor(o, o, ps[:, 2 * n:2 * n + 2, :], ALU.add))
            else:
                V.inc(dve.tensor_tensor(tmp, ps[:, 2 * n:2 * n + 2, :], bc(gate[:, n * CW:(n + 1) * CW], 1, TT), ALU.mult))
                w(dve, V.now())
                V.inc(dve.tensor_tensor(o, o, tmp, ALU.add))

    def ffn(w_up, w_down, nxt, conv=None, gate=None):
        settle()
        c = Carve(end=arena_n - 2 * FT * SEQ)
        tmp, val = c(2, 2, SEQ), c(2, 2, SEQ)
        yb, zb = (c(2, 4, SEQ), c(2, 4, SEQ)) if conv is not None else (None, None)
        prod = c(TT, CW)
        nv, na, ng = (4, 3, 1) if conv is not None else (2, 2, 0)

        def one(ci, par, after):
            b0 = 4 * par
            w(pe, V.back(nv), A.back(na))
            m = chunk_feat(range(b0, b0 + 4))
            two_ago = (V.back(nv), A.back(na))
            request(after)
            up = ps[:, b0 + 2:b0 + 4, 0:SEQ]
            if conv is None:
                w(act, m, *two_ago)
                A.inc(act.activation(tmp[:, par, :, :], ps[:, b0:b0 + 2, 0:SEQ], ACT.Silu))
            else:
                y, z = yb[:, par, :, :], zb[:, par, :, :]
                taps = ccur[:, par, :].rearrange("p (a t b) -> p a t b", a=2, t=4)
                w(pool, *two_ago)
                G.inc(pool.tensor_copy(taps, conv[:, :, :, bass.ds(ci * 2, 2)]))
                tap = [[taps[:, q // 2, t, q % 2:q % 2 + 1] for t in range(4)] for q in range(4)]
                w(act, m, G.now(), *two_ago)
                for q in range(4):
                    i_ = act.activation(y[:, q, :], ps[:, b0 + q, 0:SEQ], ACT.Identity, scale=tap[q][1], bias=tap[q][3])
                A.inc(i_)
                w(dve, A.now(), V.now())
                for q in range(4):
                    dve.scalar_tensor_tensor(z[:, q, 1:SEQ], ps[:, b0 + q, 0:SEQ - 1], tap[q][0],
                                             y[:, q, 1:SEQ], ALU.mult, ALU.add)
                V.inc(dve.tensor_copy(z[:, :, 0:1], y[:, :, 0:1]))
                w(dve, V.now())
                for q in range(4):
                    dve.scalar_tensor_tensor(y[:, q, 0:SEQ - 1], ps[:, b0 + q, 1:SEQ], tap[q][2],
                                             z[:, q, 0:SEQ - 1], ALU.mult, ALU.add)
                V.inc(dve.tensor_copy(y[:, :, SEQ - 1:SEQ], z[:, :, SEQ - 1:SEQ]))
                w(act, V.now())
                A.inc(act.activation(tmp[:, par, :, :], y[:, 0:2, :], ACT.Silu))
                up = y[:, 2:4, :]
            w(dve, A.now(), V.now())
            V.inc(dve.tensor_tensor(val[:, par, :, :], tmp[:, par, :, :], up, ALU.mult))
            w(act, V.now())
            hs = hid[:, 0, bass.ds(ci * 2, 2), :]
            A.inc(act.activation(hs, val[:, par, :, :], ACT.Copy))
            w(dve, A.now())
            V.inc(dve.tensor_tensor(hid[:, 1, bass.ds(ci * 2, 2), :], val[:, par, :, :], hs.bitcast(F32), ALU.subtract))

        with loop((N_FFC - 1) // 2, 2, dve=2 * nv, act=2 * na, pool=2 * ng) as i:
            one(i * 2, 0, gate_up(w_up, i * 2 + 1))
            one(i * 2 + 1, 1, gate_up(w_up, i * 2 + 2))
        splits = ((0, (HK, HK)), (8, (HK, HK)), (16, (HK, 2)))
        one(N_FFC - 1, 0, cols(w_down, 0, *splits[0]))
        settle(pe)
        for n in range(2):
            for j, (k0, nks) in enumerate(splits):
                for s in range(2):
                    w(pe, hi_ok[s].now(), lo_ok[s].now())
                    for t in range(TT):
                        for k in range(nks[s]):
                            kk = k0 + s * HK + k
                            i_ = mm3(ps[:, 2 * n + t, :], hid[:, 0, kk, t * P:(t + 1) * P],
                                     hid[:, 1, kk, t * P:(t + 1) * P], whi[:, s, k, :], wlo[:, s, k, :],
                                     kk == 0, kk == FT - 1)
                    m = used[s].inc(i_)
                if j < 2:
                    request(cols(w_down, n * CW, *splits[j + 1]))
                else:
                    request(cols(w_down, CW, *splits[0]) if n == 0 else nxt)
            o = resid[:, :, n * CW:(n + 1) * CW]
            pv = ps[:, 2 * n:2 * n + 2, :]
            w(dve, m, V.now())
            if gate is not None:
                V.inc(dve.tensor_tensor(prod, pv, bc(gate[:, n * CW:(n + 1) * CW], 1, TT), ALU.mult))
                w(dve, V.now())
                pv = prod
            V.inc(dve.tensor_tensor(o, o, pv, ALU.add))

    def head_norm_rope(x, nh, hd, nt, cos, sin, dst, bufs, rope=True):
        sq, r, xn, a, b = bufs
        n = nt * nh
        g = sq[:, 0:n * hd]
        w(act, V.now(), G.now())
        A.inc(act.activation(g.rearrange("p (t m) -> p t m", t=nt), x, ACT.Square))
        w(dve, A.now())
        V.inc(dve.tensor_reduce(r[:, 0:n], g.rearrange("p (n d) -> p n d", d=hd), AX.X, ALU.add))
        w(dve, V.now())
        V.inc(dve.tensor_scalar(r[:, 0:n], r[:, 0:n], 1.0 / hd, EPS, ALU.mult, ALU.add))
        w(act, V.now())
        A.inc(act.activation(r[:, 0:n], r[:, 0:n], ACT.Sqrt))
        w(dve, A.now())
        V.inc(dve.reciprocal(r[:, 0:n], r[:, 0:n]))
        w(dve, V.now(), G.now())
        xv = xn[:, 0:n * hd].rearrange("p (t h d) -> p t h d", t=nt, d=hd)
        for t in range(nt):
            i_ = dve.tensor_tensor(xv[:, t], x[:, t, :].rearrange("p (h d) -> p h d", d=hd),
                                   bc(r[:, t * nh:(t + 1) * nh], 2, hd), ALU.mult)
        V.inc(i_)
        done_psum = V.now()
        av, bv = (q[:, 0:n * hd].rearrange("p (t h d) -> p t h d", t=nt, d=hd) for q in (a, b))
        w_apart(pool, V.now())
        for t in range(nt):
            i_ = pool.tensor_tensor(av[:, t], xv[:, t], bc(cos[:, t, :], 1, nh), ALU.mult)
        G.inc(i_)
        w(dve, V.now())
        hh = 32
        for t in range(nt):
            for q in range(hd // 64):
                for s_ in range(2):
                    o0, i0 = q * 64 + s_ * hh, q * 64 + (1 - s_) * hh
                    i_ = dve.tensor_tensor(bv[:, t, :, o0:o0 + hh], xv[:, t, :, i0:i0 + hh],
                                           bc(sin[:, t, o0:o0 + hh], 1, nh), ALU.mult)
        V.inc(i_)
        w_apart(pool, V.now(), G.now())
        for t in range(nt):
            i_ = pool.tensor_tensor(dst(t), av[:, t], bv[:, t], ALU.add)
        G.inc(i_)
        return done_psum

    def layer_a(nxt):
        w_in, w_out = ins["a_w_in"][0], ins["a_w_out"][0]
        c = Carve()
        q_k = c(2, NG, TT, D)
        vv = c(NG, TT, D)
        keep = c.at
        tabs = c(2, NG, 2, TT, A_HD)
        gains = c(2, NG, A_HD)
        sq = c(1024)
        bufs = (sq, c(16), c(1024), c(1024), sq)
        load_row(gains.rearrange("p a b c -> p (a b c)"), "a_gains")
        w(pool, L.now())
        cosv = const("cos_a").rearrange("p (t d) -> p t d", t=TT)
        sinv = const("sin_a").rearrange("p (t d) -> p t d", t=TT)
        for j in range(2):
            for g in range(NG):
                for t in range(TT):
                    G.inc(pool.tensor_tensor(tabs[:, 0, g, j, t, :], cosv[:, t, :], gains[:, j, g, :], ALU.mult))
                    for s_ in range(2):
                        o, i_ = slice(s_ * 32, s_ * 32 + 32), slice(32 - s_ * 32, 64 - s_ * 32)
                        G.inc(pool.tensor_tensor(tabs[:, 1, g, j, t, o], sinv[:, t, o], gains[:, j, g, i_], ALU.mult))
        w(dve, G.now())

        def chunk(g, j, nxt_, ends):
            kind, half, gi = j // 2, j % 2, bass.ds(g, 1)
            b0 = 2 * (j % 4)
            w(pe, *ends[max(j - 1, 0)])
            m = chunk_tok((b0, b0 + 1))
            request(nxt_)
            w(act, m)
            w(dve, m)
            x = ps[:, b0:b0 + 2, :]
            flat = "p a t d -> p (a t) d"
            if kind < 2:
                head_norm_rope(
                    x, 8, A_HD, TT, tabs[:, 0, gi, kind, :, :].rearrange(flat), tabs[:, 1, gi, kind, :, :].rearrange(flat),
                    lambda t: q_k[:, kind, gi, t, half * CW:(half + 1) * CW].rearrange("p a (h d) -> p (a h) d", d=A_HD),
                    bufs)
            else:
                A.inc(act.activation(vv[:, gi, :, half * CW:(half + 1) * CW].rearrange(flat), x, ACT.Copy))
            ends.append((V.now(), A.now()))

        with loop(NG - 1, 6, act=2 * 4 + 2, dve=5 * 4, pool=2 * 4) as g:
            ends = [(V.now(), A.now())]
            for j in range(6):
                chunk(g, j, cols(w_in, g * (3 * D) + (j + 1) * CW), ends)
        ends = [(V.now(), A.now())]
        for j in range(6):
            chunk(NG - 1, j, cols(w_in, (NG - 1) * 3 * D + (j + 1) * CW) if j < 5 else cols(w_out, 0), ends)

        c = Carve(-XS, -XS // 2)
        stg, kT = c(2, 6, P), c(6, P)
        qz = [c(6, P) for _ in range(2)]
        o = Carve(-XS // 2, 0)(TT, D)
        c = Carve(start=keep)
        S, E, ET = (c(2, NG * SEQ) for _ in range(3))
        mask = c(TT, NG * SEQ)
        mx, ngm, l, rl = (c(4) for _ in range(4))
        settle()
        w(act, V.now())
        L.inc(act.dma_start(mask.rearrange("p a b -> p (a b)"), ins["a_mask"]), 16)
        w(dve, L.now())
        for h in range(2):
            V.inc(dve.memset(qz[h][64 - 64 * h:128 - 64 * h, :, :], 0.0))
        scale = A_HD ** -0.5

        with loop(A_HEADS // 2, 0, pe=1 + 3 * 4, act=2 + 2 * 4, dve=1 + 5 * 4, pool=0) as hp:
            pair = bass.ds(hp * P, P)
            w(act, T.now())
            for kind in range(2):
                for g in range(NG):
                    i_ = act.activation(stg[:, kind, 2 * g:2 * g + 2, :], q_k[:, kind, g, :, pair], ACT.Copy)
            A.inc(i_)
            w(pe, A.now(), V.now())
            for kind in range(2):
                for j in range(6):
                    b = 2 * kind + j // 4
                    i_ = pe.transpose(ps[:, b, (j % 4) * P:(j % 4 + 1) * P], stg[:, kind, j, :], ident)
            tm = T.inc(i_)
            pq = ps[:, 0:2, :].rearrange("p a b -> p (a b)")
            pk = ps[:, 2:4, :].rearrange("p a b -> p (a b)")
            w(act, tm)
            A.inc(act.activation(kT.rearrange("p a b -> p (a b)"), pk[:, 0:768], ACT.Copy))
            w(dve, tm)
            for h in range(2):
                r = slice(64 * h, 64 * h + 64)
                i_ = dve.tensor_copy(qz[h][r].rearrange("p a b -> p (a b)"), pq[r, 0:768])
            V.inc(i_)
            w(pe, A.now(), V.now())
            state = {}

            def scores(u):
                h, t, par = u // 2, u % 2, u % 2
                b = 4 + 2 * par
                if u >= 2:
                    w(pe, state[u - 2]["out"])
                for g in range(NG):
                    i_ = pe.matmul(ps[:, b + g // 2, (g % 2) * SEQ:(g % 2 + 1) * SEQ], qz[h][:, 2 * g + t, :],
                                   kT[:, 2 * g:2 * g + 2, :], start=True, stop=True)
                w_apart(dve, T.inc(i_), A.now())
                sc = ps[:, b:b + 2, :].rearrange("p a b -> p (a b)")[:, 0:NG * SEQ]
                V.inc(dve.tensor_tensor_reduce(out=S[:, par, :], in0=sc, in1=mask[:, t, :], scale=1.0, scalar=-3e38,
                                               op0=ALU.add, op1=ALU.max, accum_out=mx[:, u:u + 1]))
                w(dve, V.now())
                V.inc(dve.tensor_scalar(ngm[:, u:u + 1], mx[:, u:u + 1], -scale, None, ALU.mult))
                w(act, V.now(), T.now())
                A.inc(act.activation(E[:, par, :], S[:, par, :], ACT.Exp, bias=ngm[:, u:u + 1], scale=scale,
                                     accum_out=l[:, u:u + 1]))
                state[u] = {"exp": A.now()}

            def values(u):
                h, t, par = u // 2, u % 2, u % 2
                b = 2 * par
                w(pe, state[u]["exp"])
                for j in range(6):
                    i_ = pe.transpose(ps[:, b + j // 4, (j % 4) * P:(j % 4 + 1) * P], E[:, par, j * P:(j + 1) * P], ident)
                tm = T.inc(i_)
                w(act, tm)
                A.inc(act.activation(ET[:, par, 0:512], ps[:, b, :], ACT.Copy))
                w(dve, tm, state[u]["exp"])
                V.inc(dve.tensor_copy(ET[:, par, 512:768], ps[:, b + 1, 0:256]))
                V.inc(dve.reciprocal(rl[:, u:u + 1], l[:, u:u + 1]))
                w(pe, A.now(), V.now())
                po = ps[:, 5 + 2 * par, 256:384]
                for j in range(6):
                    i_ = pe.matmul(po, ET[:, par, j * P:(j + 1) * P], vv[:, j // 2, j % 2, pair], start=(j == 0), stop=(j == 5))
                w(dve, T.inc(i_), V.now())
                state[u]["out"] = V.inc(dve.tensor_scalar(
                    o[:, t, bass.ds(hp * P + 64 * h, 64)], po[:, 64 * h:64 * h + 64], rl[:, u:u + 1], None, ALU.mult))

            for u in range(4):
                scores(u)
                if u:
                    values(u - 1)
            values(3)

        c = Carve()
        stage = c(2, 512)
        settle()
        to_split(lambda t, k: o[:, t, k * P:(k + 1) * P], 0, stage)
        add_product(w_out, nxt)

    def layer_b(nxt):
        w_in, w_out = ins["b_w_in"][0], ins["b_w_out"][0]
        QK, VW = GLA_HEADS * GLA_DK, GLA_HEADS * GLA_DV
        settle()
        c = Carve()
        qT, kT_ = c(GLA_HEADS, SEQ), c(GLA_HEADS, SEQ)
        v, r = c(TT, VW), c(TT, VW)
        la = c(2, GLA_HEADS * SEQ)
        wz = c(KT, 2 * GLA_RANK)
        z, zT = c(TT, 2 * GLA_RANK), c(2, SEQ)
        wg = c(2, QK)
        gain = c(VW)
        t1, t2 = c(2, GLA_HEADS * SEQ), c(2, GLA_HEADS * SEQ)
        w(act, V.now(), T.now(), G.now())
        L.inc(act.dma_start(wz, w_in[:, 2 * QK + 2 * VW:].rearrange("(k p) n -> p k n", p=P)), 16)
        L.inc(act.dma_start(wg[0:GLA_RANK, 0, :], ins["b_w_gate_f"][0]), 16)
        L.inc(act.dma_start(wg[0:GLA_RANK, 1, :], ins["b_w_gate_b"][0]), 16)
        load_row(gain, "b_out_norm")

        m = chunk_feat(range(0, 4))
        request(cols(w_in, CW))
        w(act, m)
        A.inc(act.activation(qT, ps[:, 0:4, 0:SEQ], ACT.Copy, scale=GLA_DK ** -0.5))
        m = chunk_feat(range(4, 8))
        request(cols(w_in, 2 * CW))
        w(act, m)
        A.inc(act.activation(kT_, ps[:, 4:8, 0:SEQ], ACT.Copy))
        for j in range(4):
            dst = (v, r)[j // 2]
            b0 = 2 * j
            w(pe, A.now())
            m = chunk_tok((b0, b0 + 1))
            request(cols(w_in, (3 + j) * CW) if j < 3 else cols(w_out, 0))
            w(act, m)
            o_ = dst[:, :, (j % 2) * CW:(j % 2 + 1) * CW]
            A.inc(act.activation(o_, ps[:, b0:b0 + 2, :], ACT.Copy if j < 2 else ACT.Silu))
        w(pe, L.now(), A.now(), V.now())
        for t in range(TT):
            for k in range(KT):
                pe.matmul(ps[:, t, 0:32], xs[:, 0, k, t * P:(t + 1) * P].bitcast(F32), wz[:, k, :], start=(k == 0), stop=False)
                i_ = pe.matmul(ps[:, t, 0:32], xs[:, 1, k, t * P:(t + 1) * P].bitcast(F32), wz[:, k, :], start=False, stop=(k == KT - 1))
        w(dve, T.inc(i_))
        V.inc(dve.tensor_copy(z, ps[:, 0:2, 0:32]))
        w(pe, V.now())
        for d in range(2):
            for t in range(TT):
                i_ = pe.transpose(ps[0:GLA_RANK, 2 + d, t * P:(t + 1) * P], z[:, t, 16 * d:16 * d + 16], ident)
        w(dve, T.inc(i_))
        V.inc(dve.tensor_copy(zT[0:GLA_RANK, :, :], ps[0:GLA_RANK, 2:4, 0:SEQ]))
        w(pe, V.now())
        for d in range(2):
            for h in range(GLA_HEADS):
                i_ = pe.matmul(ps[:, 4 + 2 * d + h // 2, (h % 2) * SEQ:(h % 2 + 1) * SEQ],
                               wg[0:GLA_RANK, d, h * P:(h + 1) * P], zT[0:GLA_RANK, d, :], start=True, stop=True)
        w(dve, T.inc(i_))
        bias = vcol("gla_bias").rearrange("p (d h) -> p d h", d=2)
        for d in range(2):
            i_ = dve.tensor_tensor(t1[:, d].rearrange("p (h n) -> p h n", h=4),
                                   ps[:, 4 + 2 * d:6 + 2 * d, :].rearrange("p b (h n) -> p (b h) n", h=2),
                                   bc(bias[:, d, :], 2, SEQ), ALU.add)
        w(act, V.inc(i_))
        A.inc(act.activation(t2, t1, ACT.Abs))
        w(act, A.now())
        A.inc(act.activation(t2, t2, ACT.Exp, scale=-1.0))
        w(act, A.now())
        A.inc(act.activation(t2, t2, ACT.Ln, bias=1.0))
        w(dve, A.now(), V.now())
        V.inc(dve.tensor_scalar(t1, t1, 0.0, 1.0 / GLA_TAU, ALU.min, ALU.mult))
        w(dve, V.now())
        V.inc(dve.scalar_tensor_tensor(la, t2, -1.0 / GLA_TAU, t1, ALU.mult, ALU.add))
        keepm = t1[:, 0, :]
        w(dve, V.now())
        V.inc(dve.memset(keepm, 1.0))
        w(dve, V.now())
        V.inc(dve.memset(keepm.rearrange("p (n c) -> p n c", c=CHUNK)[:, :, 0:1], 0.0))
        w(dve, V.now())
        V.inc(dve.tensor_tensor_scan(t2[:, 0, :], keepm, la[:, 0, :], 0.0, ALU.mult, ALU.add))
        V.inc(dve.tensor_tensor_scan(t2[:, 1, ::-1], keepm, la[:, 1, ::-1], 0.0, ALU.mult, ALU.add))
        w(dve, V.now())
        NB = GLA_HEADS * NCH
        e1, e2 = la, c(2, GLA_HEADS * SEQ)
        e3 = t1
        dec = c(2, NB)
        b4 = t2.rearrange("p d (n c) -> p d n c", c=CHUNK)
        e34 = e3.rearrange("p d (n c) -> p d n c", c=CHUNK)
        last = [b4[:, 0, :, CHUNK - 1], b4[:, 1, :, 0]]
        for d in range(2):
            i_ = dve.tensor_tensor(e34[:, d], bc(last[d], 2, CHUNK), b4[:, d], ALU.subtract)
        V.inc(i_)
        w(act, V.now())
        for d in range(2):
            act.activation(dec[:, d, :], last[d], ACT.Exp)
        act.activation(e1, t2, ACT.Exp)
        act.activation(e2, t2, ACT.Exp, scale=-1.0)
        A.inc(act.activation(e3, e3, ACT.Exp))

        o = c(TT, VW)
        qd, kd, ke = c(2, SEQ), c(2, SEQ), c(2, SEQ)
        kt = [c(2, TT, P) for _ in range(2)]
        AT = c(TT, P)
        S = c(2, NCH, GLA_DV)
        settle(dve, act, pe)
        V.inc(dve.memset(AT, 0.0))
        for q in range(2):
            V.inc(dve.memset(kt[q][64 - 64 * q:128 - 64 * q], 0.0))
        w(dve, V.now())
        mf, mb = const("gla_f").bitcast(I32), const("gla_b").bitcast(I32)
        with loop(GLA_HEADS, 0, pe=4 + TT, act=1, dve=2 + 2 + 2 * (NCH - 1) + TT) as h:
            hs = bass.ds(h * SEQ, SEQ)
            hv = bass.ds(h * GLA_DV, GLA_DV)
            w(dve, T.now(), A.now(), V.now())
            for d in range(2):
                e = [x[:, d, hs] for x in (e1, e2, e3)]
                qh, kh = (x[:, bass.ds(h, 1), :].rearrange("p a n -> p (a n)") for x in (qT, kT_))
                dve.tensor_tensor(qd[:, d, :], qh, e[0], ALU.mult)
                dve.tensor_tensor(kd[:, d, :], kh, e[1], ALU.mult)
                i_ = dve.tensor_tensor(ke[:, d, :], kh, e[2], ALU.mult)
                V.inc(i_)
            w(pe, V.now(), A.now())
            for d in range(2):
                for t in range(TT):
                    i_ = pe.transpose(ps[:, 0, (2 * d + t) * P:(2 * d + t + 1) * P], ke[:, d, t * P:(t + 1) * P], ident)
            w(act, T.inc(i_))
            for q in range(2):
                rr = slice(64 * q, 64 * q + 64)
                i_ = act.activation(kt[q][rr].rearrange("p a b c -> p (a b c)"), ps[rr, 0, :], ACT.Copy)
            A.inc(i_)
            for d in range(2):
                for t in range(TT):
                    i_ = pe.matmul(ps[:, 1, (2 * d + t) * P:(2 * d + t + 1) * P], kd[:, d, t * P:(t + 1) * P],
                                   qd[:, d, t * P:(t + 1) * P], start=True, stop=True)
            m = T.inc(i_)
            for d, mk in ((0, mf), (1, mb)):
                w_apart(dve, m, V.now())
                for t in range(TT):
                    i_ = dve.copy_predicated(AT[:, t, :], mk, ps[:, 1, (2 * d + t) * P:(2 * d + t + 1) * P])
                V.inc(i_)
            w(pe, A.now())
            kv = {}
            for d in range(2):
                for j in range(NCH - 1):
                    n = j if d == 0 else NCH - 1 - j
                    slot = ps[:, 2 + d * 2 + j // 2, (j % 2) * SEQ:(j % 2 + 1) * SEQ]
                    kv[d, j] = slot
                    i_ = pe.matmul(slot, kt[n % 2][:, d, n // 2, :], v[:, n // 2, hv], start=True, stop=True)
                w(dve, T.inc(i_))
                for j in range(NCH - 1):
                    n = j if d == 0 else NCH - 1 - j
                    to = n + 1 if d == 0 else n - 1
                    if j == 0:
                        i_ = dve.tensor_copy(S[:, d, to, :], kv[d, j])
                    else:
                        w(dve, V.now())
                        i_ = dve.scalar_tensor_tensor(S[:, d, to, :], S[:, d, n, :], dec[:, d, bass.ds(h * NCH + n, 1)],
                                                      kv[d, j], ALU.mult, ALU.add)
                    V.inc(i_)
            w(pe, V.now())
            for t in range(TT):
                po = ps[:, 6 + t, 0:GLA_DV]
                pe.matmul(po, AT[:, t, :], v[:, t, hv], start=True, stop=False)
                for q in range(2):
                    n = 2 * t + q
                    rows, cs = slice(64 * q, 64 * q + 64), slice(n * CHUNK, (n + 1) * CHUNK)
                    dirs = [d for d in range(2) if not (d == 0 and n == 0) and not (d == 1 and n == NCH - 1)]
                    for d in dirs:
                        i_ = pe.matmul(ps[rows, 6 + t, 0:GLA_DV], qd[:, d, cs], S[:, d, n, :], start=False,
                                       stop=(d == dirs[-1]))
                w(dve, T.inc(i_))
                V.inc(dve.tensor_copy(o[:, t, hv], po))
        settle(act, dve, pe)
        sq, st = e1.rearrange("p a b -> p (a b)"), dec.rearrange("p a b -> p (a b)")
        A.inc(act.activation(sq, o.rearrange("p a b -> p (a b)"), ACT.Square))
        w(dve, A.now())
        nh = TT * GLA_HEADS
        V.inc(dve.tensor_reduce(st[:, 0:nh], sq.rearrange("p (n d) -> p n d", d=GLA_DV), AX.X, ALU.add))
        w(dve, V.now())
        V.inc(dve.tensor_scalar(st[:, 0:nh], st[:, 0:nh], 1.0 / GLA_DV, EPS, ALU.mult, ALU.add))
        w(act, V.now())
        A.inc(act.activation(st[:, 0:nh], st[:, 0:nh], ACT.Sqrt))
        w(dve, A.now())
        V.inc(dve.reciprocal(st[:, 0:nh], st[:, 0:nh]))
        w(dve, V.now(), L.now())
        o3 = o.rearrange("p a (n d) -> p (a n) d", d=GLA_DV)
        V.inc(dve.tensor_tensor(o3, o3, bc(st[:, 0:nh], 2, GLA_DV), ALU.mult))
        w(dve, V.now())
        V.inc(dve.tensor_tensor(o, o, bc(gain, 1, TT), ALU.mult))
        w(dve, V.now())
        V.inc(dve.tensor_tensor(o, o, r, ALU.mult))
        settle()
        to_split(lambda t, k: o[:, t, k * P:(k + 1) * P], 0, e2.rearrange("p a (b n) -> p (a b) n", n=512)[:, 0:2, :])
        add_product(w_out, nxt)

    def modulation(nxt):
        w_mod = ins["w_mod_2"][0]
        settle()
        c = Carve()
        bias, sil, wide_c, rows = c(6, D), c(2, KT), c(KT, SEQ), c(2, CW)
        load_row(bias.rearrange("p a b -> p (a b)"), "b_mod")
        w(act, V.now())
        act.activation(sil[:, 0, :], vcol("c"), ACT.Silu)
        A.inc(act.activation(sil[:, 1, :], vcol("c_ctx"), ACT.Silu))
        w(dve, A.now())
        dve.tensor_copy(wide_c[:, :, 0:192], bc(sil[:, 0, :], 2, 192))
        V.inc(dve.tensor_copy(wide_c[:, :, 192:256], bc(sil[:, 1, :], 2, 64)))
        w(act, V.now())
        A.inc(act.activation(xs[:, 0, :, :], wide_c, ACT.Copy))
        w(dve, A.now(), L.now())
        V.inc(dve.tensor_tensor(xs[:, 1, :, :], wide_c, xs[:, 0, :, :].bitcast(F32), ALU.subtract))
        w(pe, V.now())
        ends = [None, None]
        for j in range(12):
            which, n = j // 2, j % 2
            b = j % 2
            w(pe, ends[b])
            m = chunk_tok((b,), (1,) if which < 2 else (0,))
            request(cols(w_mod, (j + 1) * CW) if j < 11 else nxt)
            brow = bias[:, which, n * CW:(n + 1) * CW]
            w(dve, m, V.now(), T.now())
            if which % 3 == 2:
                V.inc(dve.tensor_tensor(grow[:, which // 3, n * CW:(n + 1) * CW], ps[:, b, :], brow, ALU.add))
                ends[b] = V.now()
                continue
            V.inc(dve.tensor_tensor(rows[:, b, :], ps[:, b, :], brow, ALU.add))
            ends[b] = V.now()
            w(pe, V.now())
            for q in range(4):
                i_ = pe.transpose(ps[:, 2 + b, q * P:(q + 1) * P], rows[:, b, q * P:(q + 1) * P], ident)
            w(dve, T.inc(i_))
            v_ = (0, 1, None, 2, 3)[which]
            colv = ps[:, 2 + b, :].rearrange("p (q n) -> p q n", q=4)[:, :, 0:P:64]
            V.inc(dve.tensor_scalar(modcol[:, v_, 4 * n:4 * n + 4, :], colv, 1.0 if v_ % 2 else 0.0, None, ALU.add))
            ends[b] = V.now()

    def attention_2(akv_next, o):
        w_in = ins["w_in_2"][0]
        QW = 3616
        c = Carve(end=arena_n - 2048)
        k, v, q = c(NT2, KV2 * HD2), c(NT2, KV2 * HD2), c(TT, NH2 * HD2)
        tk, tq = c(2, NT2, HD2), c(2, TT, HD2)
        gk, gq = c(HD2), c(HD2)
        sq = c(1024)
        bufs = (sq, c(16), c(1024), c(1024), sq)
        kT = c(KV2, NT2 * P)
        settle(act)
        load_row(gk, "k_norm")
        load_row(gq, "q_norm")
        cosv = const("cos_2").rearrange("p (t d) -> p t d", t=TT)
        sinv = const("sin_2").rearrange("p (t d) -> p t d", t=TT)
        settle(pool)
        w(pool, L.now())
        for tab, gain in ((tk, gk), (tq, gq)):
            for t in range(TT):
                pool.tensor_tensor(tab[:, 0, t, :], cosv[:, t, :], gain, ALU.mult)
                for s_ in range(4):
                    o_, i_ = slice(s_ * 32, s_ * 32 + 32), slice((s_ ^ 1) * 32, (s_ ^ 1) * 32 + 32)
                    pool.tensor_tensor(tab[:, 1, t, o_], sinv[:, t, o_], gain[:, i_], ALU.mult)
        for t in range(TT, NT2):
            pool.tensor_copy(tk[:, 0, t, :], gk)
        G.inc(pool.memset(tk[:, 1, TT:NT2, :], 0.0))
        m = chunk_tok((0, 1, 2, 3), (0, 1, 2, 3))
        request(cols(w_in, QW))
        w(act, m)
        w(dve, m, G.now())
        head_norm_rope(ps[:, 0:4, 0:256], KV2, HD2, NT2, tk[:, 0], tk[:, 1],
                       lambda t: k[:, t, :].rearrange("p (h d) -> p h d", d=HD2), bufs)
        w(act, V.now())
        A.inc(act.activation(v, ps[:, 0:4, 256:512], ACT.Copy))
        for n in range(2):
            b0 = 4 + 2 * n
            m = chunk_tok((b0, b0 + 1))
            request(cols(w_in, QW + CW) if n == 0 else akv_next)
            w(act, m)
            w(dve, m)
            head_norm_rope(ps[:, b0:b0 + 2, :], 4, HD2, TT, tq[:, 0], tq[:, 1],
                           lambda t: q[:, t, n * CW:(n + 1) * CW].rearrange("p (h d) -> p h d", d=HD2), bufs)
        settle(pe)
        for g in range(KV2):
            for t in range(NT2):
                i_ = pe.transpose(ps[:, g, t * P:(t + 1) * P], k[:, t, g * HD2:(g + 1) * HD2], ident)
        w(dve, T.inc(i_))
        V.inc(dve.tensor_copy(kT, ps[:, 0:2, :]))
        c.at = 0 + NT2 * 512 + 2048
        stg, qT = c(TT, CW), c(TT, CW)
        E, ET = c(2, CW), c(2, CW)
        mx, ngm, l, rl = (c(8) for _ in range(4))
        assert c.at <= NT2 * 512 + 2048 + 1536 + 256 + 1024 * 3 + 16
        settle(act, dve)
        scale = HD2 ** -0.5
        with loop(KV2, 0, pe=1 + 8 * 3, act=1 + 8 * 1, dve=1 + 8 * 5) as g:
            gcols = bass.ds(g * CW, CW)
            w(act, T.now())
            A.inc(act.activation(stg, q[:, :, gcols], ACT.Copy))
            w(pe, A.now(), V.now())
            for t in range(TT):
                for h in range(GROUP2):
                    i_ = pe.transpose(ps[:, t, h * P:(h + 1) * P], stg[:, t, h * P:(h + 1) * P], ident)
            w(dve, T.inc(i_))
            V.inc(dve.tensor_copy(qT, ps[:, 0:2, :]))
            state = {}

            def scores(u):
                h, t, par = u // 2, u % 2, u % 2
                w(pe, V.now() if u < 2 else state[u - 2]["exp"])
                i_ = pe.matmul(ps[:, 2 + par, :], qT[:, t, h * P:(h + 1) * P],
                               kT[:, bass.ds(g, 1), :].rearrange("p a n -> p (a n)"), start=True, stop=True)
                w(dve, T.inc(i_), A.now())
                V.inc(dve.tensor_reduce(mx[:, u:u + 1], ps[:, 2 + par, :], AX.X, ALU.max))
                w(dve, V.now())
                V.inc(dve.tensor_scalar(ngm[:, u:u + 1], mx[:, u:u + 1], -scale, None, ALU.mult))
                w(act, V.now(), T.now())
                state[u] = {"exp": A.inc(act.activation(E[:, par, :], ps[:, 2 + par, :], ACT.Exp, bias=ngm[:, u:u + 1],
                                                        scale=scale, accum_out=l[:, u:u + 1]))}

            def values(u):
                h, t, par = u // 2, u % 2, u % 2
                w(pe, state[u]["exp"], V.now() if u < 2 else state[u - 2]["out"])
                for j in range(NT2):
                    i_ = pe.transpose(ps[:, 4 + par, j * P:(j + 1) * P], E[:, par, j * P:(j + 1) * P], ident)
                w(dve, T.inc(i_), state[u]["exp"], V.now())
                V.inc(dve.tensor_copy(ET[:, par, :], ps[:, 4 + par, :]))
                m_ = V.now()
                V.inc(dve.reciprocal(rl[:, u:u + 1], l[:, u:u + 1]))
                w(pe, m_)
                for j in range(NT2):
                    i_ = pe.matmul(ps[:, 6 + par, 0:P], ET[:, par, j * P:(j + 1) * P], v[:, j, bass.ds(g * HD2, HD2)],
                                   start=(j == 0), stop=(j == NT2 - 1))
                w(dve, T.inc(i_), V.now())
                state[u]["out"] = V.inc(dve.tensor_scalar(o[:, t, bass.ds(g * CW + h * P, P)], ps[:, 6 + par, 0:P],
                                                          rl[:, u:u + 1], None, ALU.mult))

            for u in range(8):
                scores(u)
                if u:
                    values(u - 1)
            values(7)

    def gdn_inputs(qkv, nxt):
        w_in, c0 = ins["w_in_2"][0], 512
        settle()
        c = Carve(start=24 * 512, end=arena_n - 2048)
        y, z = c(4, 2, SEQ), c(4, 2, SEQ)
        taps_all = vcol("gdn_conv").rearrange("p (b t) -> p b t", t=3)

        def one(ci, par, after, ends):
            b0 = 4 * par
            w(pe, *ends)
            m = chunk_feat(range(b0, b0 + 4), both=True)
            request(after)
            taps = ccur[:, par, 0:12].rearrange("p (b t) -> p b t", t=3)
            w(pool, V.now(), A.now())
            G.inc(pool.tensor_copy(taps, taps_all[:, bass.ds(ci * 4, 4), :]))
            xq = ps[:, b0:b0 + 4, :].rearrange("p b (s n) -> p b s n", s=2)
            w(act, m, G.now(), V.now(), A.now())
            for q in range(4):
                i_ = act.activation(y[:, q], xq[:, q], ACT.Copy, scale=taps[:, q, 1:2])
            w(dve, A.inc(i_), V.now())
            for q in range(4):
                dve.scalar_tensor_tensor(z[:, q, :, 1:SEQ], xq[:, q, :, 0:SEQ - 1], taps[:, q, 0:1], y[:, q, :, 1:SEQ],
                                         ALU.mult, ALU.add)
            V.inc(dve.tensor_copy(z[:, :, :, 0:1], y[:, :, :, 0:1]))
            w(dve, V.now())
            for q in range(4):
                dve.scalar_tensor_tensor(y[:, q, :, 0:SEQ - 1], xq[:, q, :, 1:SEQ], taps[:, q, 2:3],
                                         z[:, q, :, 0:SEQ - 1], ALU.mult, ALU.add)
            V.inc(dve.tensor_copy(y[:, :, :, SEQ - 1:SEQ], z[:, :, :, SEQ - 1:SEQ]))
            w(act, V.now())
            A.inc(act.activation(qkv[:, bass.ds(ci * 4, 4), :], y.rearrange("p b s n -> p b (s n)"), ACT.Silu))

        with loop(2, 2, act=4, dve=4, pool=2) as i:
            for par in range(2):
                ends = (V.back(2), A.back(2))
                one(i * 2 + par, par, cols(w_in, c0 + (i * 2 + par + 1) * CW), ends)
        for ci in (4, 5):
            one(ci, ci % 2, cols(w_in, c0 + (ci + 1) * CW) if ci == 4 else nxt, (V.back(2), A.back(2)))

    def gdn_scalars(sc, c):
        wz, zf = c(KT, 32), c(512)
        a_log, dt = c(16), c(16)
        la, t1, t2 = c(NT2, 16), c(NT2, 16), c(NT2, 16)
        settle(act)
        L.inc(act.dma_start(wz, ins["w_in_2"][0][:, 3584:3616].rearrange("(k p) n -> p k n", p=P)), 16)
        load_row(a_log, "a_log")
        load_row(dt, "dt_bias")
        settle(pe, dve)
        w(pe, L.now())
        w(dve, L.now())
        for k in range(KT):
            pe.matmul(ps[0:32, 0, :], wz[:, k, :], xs[:, 0:4:2, k, :].bitcast(F32), start=(k == 0), stop=False)
            i_ = pe.matmul(ps[0:32, 0, :], wz[:, k, :], xs[:, 1:4:2, k, :].bitcast(F32), start=False, stop=(k == KT - 1))
        w(dve, T.inc(i_))
        V.inc(dve.tensor_copy(zf[0:32, :], ps[0:32, 0, :]))
        w(pe, V.now())
        for t in range(NT2):
            i_ = pe.transpose(ps[:, 1, 32 * t:32 * t + 32], zf[0:32, t * P:(t + 1) * P], ident[0:32, 0:32])
        m = T.inc(i_)
        z = ps[:, 1, 0:128].rearrange("p (t n) -> p t n", t=NT2)
        kinds = sc.rearrange("p k t d h -> p k t (d h)")
        w(act, m)
        A.inc(act.activation(kinds[:, 1], z[:, :, 0:16], ACT.Sigmoid))
        w(dve, A.now())
        V.inc(dve.tensor_tensor(t1, z[:, :, 16:32], bc(dt, 1, NT2), ALU.add))
        w(act, V.now())
        A.inc(act.activation(t2, t1, ACT.Abs))
        w(act, A.now())
        A.inc(act.activation(t2, t2, ACT.Exp, scale=-1.0))
        act.activation(a_log, a_log, ACT.Exp)
        w(act, A.now())
        A.inc(act.activation(t2, t2, ACT.Ln, bias=1.0))
        w(dve, A.now())
        V.inc(dve.scalar_tensor_tensor(t1, t1, 0.0, t2, ALU.max, ALU.add))
        w(dve, V.now())
        V.inc(dve.scalar_tensor_tensor(la, t1, -1.0, bc(a_log, 1, NT2), ALU.mult, ALU.mult))
        w(pe, V.now())
        flat = la.rearrange("p t n -> p (t n)")
        for j, name in enumerate(("cum_f", "cum_b", "ones_bd", "even", "odd")):
            i_ = pe.matmul(ps[:, 2 + j, 0:64], const(name), flat, start=True, stop=True)
        m = T.inc(i_)
        w(dve, m)
        res = [ps[:, 2 + j, 0:64].rearrange("p (t d h) -> p t d h", t=NT2, d=2) for j in range(5)]
        for d in range(2):
            i_ = dve.tensor_copy(sc[:, 0, :, d, :], res[d][:, :, d, :])
        V.inc(i_)
        w(dve, V.now())
        V.inc(dve.tensor_tensor(t1, ps[:, 4, 0:64].rearrange("p (t n) -> p t n", t=NT2), kinds[:, 0], ALU.subtract))
        w(act, V.now())
        act.activation(kinds[:, 2], kinds[:, 0], ACT.Exp)
        act.activation(kinds[:, 3], t1, ACT.Exp)
        for q in range(2):
            i_ = act.activation(kinds[:, 5 + q], ps[:, 5 + q, 0:64].rearrange("p (t n) -> p t n", t=NT2), ACT.Exp)
        w(dve, A.inc(i_))
        V.inc(dve.scalar_tensor_tensor(kinds[:, 4], kinds[:, 1], -1.0, kinds[:, 2], ALU.mult, ALU.mult))

    def gdn_heads(qkv, sc, o, lo, hi):
        c = lo
        NM = NT2 * 2
        hc = c(7, NT2 * 2)
        kn, qn, vs = c(CW), c(SEQ), c(CW)
        PT = c(2, TT, P)
        NTm, XT = c(2, NT2, P), c(2, NT2, P)
        X, Y = c(2, NT2, P), c(2, NT2, P)
        big = c(2 * NM * P)
        c = hi
        S = c(2, 6, P)
        PD = c(TT, P)
        decT = Y
        Ig, Ib = (big[:, j * NM * P:(j + 1) * NM * P].rearrange("p (d t n) -> p d t n", d=2, t=NT2) for j in range(2))
        BT = (Ig, Ib)
        flatx = X.rearrange("p d t n -> p (d t n)")
        sqq = flatx[:, 0:768]
        rr = S.rearrange("p d t n -> p (d t n)")[:, 0:768]
        R, dl = X, Y
        kd = (Ig, Ib)
        h4 = hc.rearrange("p k (t d) -> p k d t", d=2)
        chunks = {0: [(1, 0, 0), (1, 0, 1), (1, 1, 0), (1, 1, 1), (0, 0, 0), (0, 0, 1), (0, 1, 0), (0, 1, 1)]}
        chunks[1] = chunks[0][3::-1] + chunks[0][:3:-1]
        settle()
        negs = (const("neg_f"), const("neg_b"))
        nlev = len(LEVELS) - 1
        with loop(GDN_HEADS, 0, **GDN_PER) as h:
            blk = lambda j: qkv[:, bass.ds(h + 8 * j, 1), :].rearrange("p a n -> p (a n)")
            settle(act, dve, pe, pool)
            V.inc(dve.tensor_copy(hc, sc.rearrange("p k t d h -> p k (t d) h")[:, :, :, bass.ds(h, 1)].rearrange("p k n a -> p k (n a)")))
            act.activation(sqq[:, 0:512], blk(1), ACT.Square)
            A.inc(act.activation(sqq[:, 512:768], blk(0)[:, 0:SEQ], ACT.Square))
            ma = A.now()
            A.inc(act.activation(vs, blk(2), ACT.Copy))
            w_apart(pool, V.now())
            for d in range(2):
                for t in range(NT2):
                    pool.tensor_scalar(Ig[:, d, t, :], ident, h4[:, 0, d, t:t + 1], None, ALU.mult)
                    i_ = pool.tensor_scalar(Ib[:, d, t, :], ident, h4[:, 1, d, t:t + 1], None, ALU.mult)
            mg = G.inc(i_)
            w(pe, ma)
            pe.matmul(ps[:, 0, :], const("ones"), sqq[:, 0:512], start=True, stop=True)
            mt = T.inc(pe.matmul(ps[:, 1, 0:SEQ], const("ones"), sqq[:, 512:768], start=True, stop=True))
            w(dve, mt)
            dve.tensor_scalar(rr[:, 0:512], ps[:, 0, :], EPS, None, ALU.add)
            V.inc(dve.tensor_scalar(rr[:, 512:768], ps[:, 1, 0:SEQ], EPS, None, ALU.add))
            w(act, V.now())
            A.inc(act.activation(rr, rr, ACT.Sqrt))
            w(dve, A.now())
            V.inc(dve.reciprocal(rr, rr))
            w(dve, V.now())
            dve.tensor_tensor(kn, blk(1), rr[:, 0:512], ALU.mult)
            V.inc(dve.scalar_tensor_tensor(qn, blk(0)[:, 0:SEQ], GDN_D ** -0.5, rr[:, 512:768], ALU.mult, ALU.mult))
            w(pe, mg)
            for d in range(2):
                pe.matmul(ps[:, 2 + d, :], const("ones_bd"), Ig[:, d].rearrange("p t n -> p (t n)"), start=True, stop=True)
                i_ = pe.matmul(ps[:, 4 + d, :], const("ones_bd"), Ib[:, d].rearrange("p t n -> p (t n)"), start=True, stop=True)
            mt = T.inc(i_)
            w(pe, V.now())
            for t in range(NT2):
                pe.matmul(ps[:, 6, t * P:(t + 1) * P], kn[:, t * P:(t + 1) * P], kn[:, t * P:(t + 1) * P], start=True, stop=True)
            for t in range(TT):
                i_ = pe.matmul(ps[:, 7, t * P:(t + 1) * P], kn[:, t * P:(t + 1) * P], qn[:, t * P:(t + 1) * P], start=True, stop=True)
            mk = T.inc(i_)
            w(dve, mt)
            for d in range(2):
                for t in range(NT2):
                    i_ = dve.scalar_tensor_tensor(decT[:, d, t, :], ps[:, 2 + d, t * P:(t + 1) * P], h4[:, 0, d, t:t + 1],
                                                  negs[d], ALU.subtract, ALU.add)
            w(act, V.inc(i_))
            A.inc(act.activation(decT, decT, ACT.Exp))
            w(dve, A.now(), mk)
            for d in range(2):
                dve.tensor_tensor(PT[:, d], decT[:, d, 0:TT, :], ps[:, 7, 0:SEQ].rearrange("p (t n) -> p t n", t=TT), ALU.mult)
                i_ = dve.tensor_tensor(NTm[:, d], decT[:, d], ps[:, 6, :].rearrange("p (t n) -> p t n", t=NT2), ALU.mult)
            V.inc(i_)
            w(dve, V.now())
            for d in range(2):
                i_ = dve.tensor_tensor(NTm[:, d], NTm[:, d], ps[:, 4 + d, :].rearrange("p (t n) -> p t n", t=NT2), ALU.mult)
            V.inc(i_)
            lev = [const(f"level{b}") for b in LEVELS]
            w(dve, V.now(), T.now())
            V.inc(dve.tensor_tensor(BT[1], NTm, lev0_bc(lev[0]), ALU.mult))
            w(dve, V.now())
            V.inc(dve.tensor_tensor(XT, id_bc(ident), BT[1], ALU.subtract))
            bt_ok = {}

            def level_part(j):
                w(pool, V.now(), T.now(), G.now())
                bt_ok[j] = G.inc(pool.tensor_tensor(BT[(j - 1) % 2], NTm, lev0_bc(lev[j]), ALU.mult))

            level_part(1)
            xt_ok = [V.now(), V.now()]
            for j in range(1, nlev + 1):
                bt = BT[(j - 1) % 2]
                x_ok = [None, None]
                for d in range(2):
                    w(pe, xt_ok[d])
                    for t in range(NT2):
                        i_ = pe.transpose(ps[:, d, t * P:(t + 1) * P], XT[:, d, t, :], ident)
                    w(act, T.inc(i_))
                    x_ok[d] = A.inc(act.activation(X[:, d].rearrange("p t n -> p (t n)"), ps[:, d, :], ACT.Copy))
                y_ok = [None, None]
                for d in range(2):
                    w(pe, x_ok[d], bt_ok[j])
                    for t in range(NT2):
                        i_ = pe.matmul(ps[:, 2 + d, t * P:(t + 1) * P], bt[:, d, t, :], X[:, d, t, :], start=True, stop=True)
                    w(act, T.inc(i_))
                    y_ok[d] = A.inc(act.activation(Y[:, d].rearrange("p t n -> p (t n)"), ps[:, 2 + d, :], ACT.Copy))
                if j < nlev:
                    level_part(j + 1)
                for d in range(2):
                    w(pe, y_ok[d])
                    for t in range(NT2):
                        i_ = pe.matmul(ps[:, 4 + d, t * P:(t + 1) * P], Y[:, d, t, :], XT[:, d, t, :], start=True, stop=True)
                    w(dve, T.inc(i_))
                    xt_ok[d] = V.inc(dve.tensor_tensor(XT[:, d].rearrange("p t n -> p (t n)"), XT[:, d].rearrange("p t n -> p (t n)"),
                                                       ps[:, 4 + d, :], ALU.subtract))
            w(pe, A.now(), V.now())
            for t in range(NT2):
                pe.transpose(ps[:, 6, t * P:(t + 1) * P], kn[:, t * P:(t + 1) * P], ident)
                i_ = pe.transpose(ps[:, 7, t * P:(t + 1) * P], vs[:, t * P:(t + 1) * P], ident)
            mt = T.inc(i_)
            w(dve, V.now(), mt)
            for q in range(2):
                i_ = dve.memset(kd[q][64 - 64 * q:128 - 64 * q], 0.0)
            V.inc(i_)
            for d in range(2):
                for q in range(2):
                    rw = slice(64 * q, 64 * q + 64)
                    dve.tensor_tensor(kd[q][rw, d], ps[rw, 6, :].rearrange("p (t n) -> p t n", t=NT2), bc(h4[rw, 3, d, :], 2, P), ALU.mult)
                i_ = dve.tensor_tensor(R[:, d], ps[:, 7, :].rearrange("p (t n) -> p t n", t=NT2), bc(h4[:, 1, d, :], 2, P), ALU.mult)
            V.inc(i_)
            s_ok = [V.now(), V.now()]
            slot = [None, None]
            for st in range(8):
                for d in range(2):
                    seq, tl, q = chunks[d][st]
                    t = 2 * seq + tl
                    rw = slice(64 * q, 64 * q + 64)
                    nx = (5, 4, 5, None, None, None, None, None)[st]
                    xi = lambda s_: 2 * chunks[d][s_][1] + chunks[d][s_][2]
                    if st >= 3:
                        nx = xi(st + 1) if st < 7 else None
                    b = 2 * d
                    if st:
                        w(pe, s_ok[d])
                        i_ = pe.matmul(ps[:, b, 0:P], kn[:, t * P:(t + 1) * P], S[:, d, slot[d], :], start=True, stop=True)
                        w(dve, T.inc(i_), V.now())
                        V.inc(dve.scalar_tensor_tensor(R[rw, d, t, :], ps[rw, b, 0:P], h4[rw, 4, d, t:t + 1], R[rw, d, t, :],
                                                       ALU.mult, ALU.add))
                    w(pe, V.now())
                    i_ = pe.matmul(ps[:, b + 1, 0:P], XT[:, d, t, :], R[:, d, t, :], start=True, stop=True)
                    w(act, T.inc(i_))
                    A.inc(act.activation(dl[:, d, t, :], ps[:, b + 1, 0:P], ACT.Copy))
                    if nx is not None:
                        w(pe, A.now())
                        i_ = pe.matmul(ps[:, 4 + d, 0:P], kd[q][:, d, t, :], dl[:, d, t, :], start=True, stop=True)
                        w(dve, T.inc(i_), V.now())
                        if st == 0:
                            V.inc(dve.tensor_copy(S[:, d, nx, :], ps[:, 4 + d, 0:P]))
                        else:
                            V.inc(dve.scalar_tensor_tensor(S[:, d, nx, :], S[:, d, slot[d], :], h4[:, 5 + q, d, t:t + 1],
                                                           ps[:, 4 + d, 0:P], ALU.mult, ALU.add))
                        slot[d] = nx
                        s_ok[d] = V.now()
            w(pe, V.now(), A.now())
            for t in range(TT):
                for d in range(2):
                    i_ = pe.matmul(ps[:, 6, t * P:(t + 1) * P], PT[:, d, t, :], dl[:, d, t, :], start=(d == 0), stop=(d == 1))
            mt = T.inc(i_)
            w(act, mt)
            A.inc(act.activation(PD.rearrange("p t n -> p (t n)"), ps[:, 6, 0:SEQ], ACT.Copy))
            for d in range(2):
                for t in range(TT):
                    for q in range(2):
                        i_ = pe.matmul(ps[64 * q:64 * q + 64, 7, (2 * d + t) * P:(2 * d + t + 1) * P],
                                       qn[:, (2 * t + q) * CHUNK:(2 * t + q + 1) * CHUNK], S[:, d, 2 * t + q, :], start=True, stop=True)
            w(dve, T.inc(i_), A.now())
            for d in range(2):
                if d:
                    w(dve, V.now())
                for t in range(TT):
                    dst = PD[:, t, :] if d == 0 else o[:, t, bass.ds(h * P, P)]
                    i_ = dve.scalar_tensor_tensor(dst, ps[:, 7, (2 * d + t) * P:(2 * d + t + 1) * P], h4[:, 2, d, t:t + 1],
                                                  PD[:, t, :], ALU.mult, ALU.add)
                V.inc(i_)

    def lev0_bc(m):
        return bc(bc(m, 1, NT2), 1, 2)

    id_bc = lev0_bc

    def layer_c(nxt):
        w_in = ins["w_in_2"][0]
        settle()
        ctx = Carve(start=8192)(TT, D)
        w(act, V.now())
        L.inc(act.dma_start(ctx, ins["ctx_2"][0].rearrange("(t p) d -> p t d", p=P)), 16)
        w(act, L.now())
        w(dve, L.now())
        norm_split(ctx, 1, Carve(), modcol[:, 1, :, 1], modcol[:, 0, :, 1])
        norm_split(resid, 0, Carve(), modcol[:, 1, :, 0], modcol[:, 0, :, 0])
        attn = Carve(start=arena_n - 2048)(TT, D)
        attention_2(cols(w_in, 512), attn)
        Z0 = 4640
        c = Carve()
        qkv = c(24, CW)
        gdn_inputs(qkv, cols(w_in, Z0))
        gdn = c(TT, D)
        sc = c(7, NT2, 2, GDN_HEADS)
        gdn_scalars(sc, Carve(start=c.at, end=arena_n - 2048))
        gdn_heads(qkv, sc, gdn, Carve(c.at, arena_n - 2048), Carve(-XS // 2, 0))
        settle()
        c = Carve()
        z, gt = c(TT, D), c(TT, 2 * D)
        y = c(TT, D)
        sq = c(TT * D)
        st = c(16)
        gain = c(GDN_D)
        stage = c(2, 512)
        assert c.at <= 24 * CW
        load_row(gain, "gdn_norm")
        reads = [A.now()] * 4
        for j in range(6):
            b0 = 2 * (j % 4)
            w(pe, reads[j - 4] if j >= 4 else None)
            m = chunk_tok((b0, b0 + 1))
            request(cols(w_in, Z0 + (j + 1) * CW) if j < 5 else cols(ins["w_pa_2"][0], 0))
            w(act, m)
            dst = z[:, :, j * CW:(j + 1) * CW] if j < 2 else gt[:, :, (j - 2) * CW:(j - 1) * CW]
            A.inc(act.activation(dst, ps[:, b0:b0 + 2, :], ACT.Silu if j < 2 else ACT.Sigmoid))
            reads.append(A.now())
        nh = TT * GDN_HEADS
        A.inc(act.activation(sq, gdn.rearrange("p t n -> p (t n)"), ACT.Square))
        w(dve, A.now())
        V.inc(dve.tensor_reduce(st[:, 0:nh], sq.rearrange("p (n d) -> p n d", d=GDN_D), AX.X, ALU.add))
        w(dve, V.now())
        V.inc(dve.tensor_scalar(st[:, 0:nh], st[:, 0:nh], 1.0 / GDN_D, EPS, ALU.mult, ALU.add))
        w(act, V.now())
        A.inc(act.activation(st[:, 0:nh], st[:, 0:nh], ACT.Sqrt))
        w(dve, A.now())
        V.inc(dve.reciprocal(st[:, 0:nh], st[:, 0:nh]))
        w(dve, V.now(), L.now())
        o3 = gdn.rearrange("p t (h d) -> p (t h) d", d=GDN_D)
        V.inc(dve.tensor_tensor(o3, o3, bc(st[:, 0:nh], 2, GDN_D), ALU.mult))
        w(dve, V.now())
        V.inc(dve.tensor_tensor(o3, o3, bc(gain, 1, nh), ALU.mult))
        w(dve, V.now())
        V.inc(dve.tensor_tensor(gdn, gdn, z, ALU.mult))
        settle()
        to_split(lambda t, k: attn[:, t, k * P:(k + 1) * P], 0, stage)
        settle()
        to_split(lambda t, k: gdn[:, t, k * P:(k + 1) * P], 1, stage)
        after = [cols(ins["w_pa_2"][0], CW), cols(ins["w_pd_2"][0], 0), cols(ins["w_pd_2"][0], CW), cols(ins["w_out_2"][0], 0)]
        prod = sq.rearrange("p (t n) -> p t n", t=TT)
        for j in range(4):
            n, br = j % 2, j // 2
            b0 = 2 * j
            m = chunk_tok((b0, b0 + 1), (0, 1) if br == 0 else (2, 3))
            request(after[j])
            yo, g_ = y[:, :, n * CW:(n + 1) * CW], gt[:, :, j * CW:(j + 1) * CW]
            w(dve, m, V.now(), A.now())
            if br == 0:
                V.inc(dve.tensor_tensor(yo, ps[:, b0:b0 + 2, :], g_, ALU.mult))
            else:
                pr = prod[:, :, 0:CW]
                V.inc(dve.tensor_tensor(pr, ps[:, b0:b0 + 2, :], g_, ALU.mult))
                w(dve, V.now())
                V.inc(dve.tensor_tensor(yo, yo, pr, ALU.add))
        settle()
        to_split(lambda t, k: y[:, t, k * P:(k + 1) * P], 0, stage)
        add_product(ins["w_out_2"][0], nxt, gate=grow[:, 0, :], tmp=z[:, :, 0:CW])



    L.inc(act.dma_start(cst[:, :], ins["consts"]), 16)
    L.inc(act.dma_start(vec[:, :], ins["vecs"]), 16)
    L.inc(act.dma_start(resid[:, :, :], ins["x"][0].rearrange("(t p) d -> p t d", p=P)), 16)
    request(cols(ins["a_w_in"][0], 0))
    V.inc(dve.memset(unused[:, :], 0.0))
    w(pool, V.now())
    for e in (pe, act, dve, pool):
        w(e, L.now())
    a_norm = vcol("attn_norm").rearrange("p (l k) -> p l k", k=KT)
    f_norm = vcol("ffn_norm").rearrange("p (l k) -> p l k", k=KT)

    def finish(src):
        settle(sp)
        stored.inc(sp.dma_start(out[0].rearrange("(t p) d -> p t d", p=P), src), 16)
        w(sp, stored.now())

    first_gu = [gate_up(ins["ffn_w_gate_up"][i], 0) for i in range(2)]
    norm_split(resid, 0, Carve(), a_norm[:, 0, :])
    layer_a(first_gu[0])
    norm_split(resid, 0, Carve(), f_norm[:, 0, :])
    ffn(ins["ffn_w_gate_up"][0], ins["ffn_w_down"][0], cols(ins["b_w_in"][0], 0))
    norm_split(resid, 0, Carve(), a_norm[:, 1, :])
    layer_b(first_gu[1])
    norm_split(resid, 0, Carve(), f_norm[:, 1, :])
    ffn(ins["ffn_w_gate_up"][1], ins["ffn_w_down"][1], cols(ins["w_mod_2"][0], 0))
    modulation(cols(ins["w_in_2"][0], 0))
    layer_c(gate_up(ins["w_up_2"][0], 0))
    norm_split(resid, 0, Carve(), modcol[:, 3, :, 0], modcol[:, 2, :, 0])
    conv = vcol("ffn_conv").rearrange("p (a t n) -> p a t n", a=2, t=4)
    ffn(ins["w_up_2"][0], ins["w_down_2"][0], None, conv, grow[:, 1, :])
    settle()
    c = Carve()
    st, sq, o, gain = c(8), c(D), c(TT, D), c(D)
    load_row(gain, "final_norm")
    rstd_of(resid, TT, D, st, sq)
    w(dve, V.now(), L.now())
    for t in range(TT):
        V.inc(dve.scalar_tensor_tensor(o[:, t, :], resid[:, t, :], st[:, t:t + 1], gain, ALU.mult, ALU.mult))
    finish(o)




def pack(parts):
    at, n = {}, 0
    for name, a in parts:
        at[name] = (n, n + a.shape[-1])
        n += a.shape[-1]
    return np.ascontiguousarray(np.concatenate([a for _, a in parts], -1)), at


def by_partition(v):
    a = np.asarray(v)
    a = a.reshape(-1, a.shape[-1] // P, P)
    return np.ascontiguousarray(a.reshape(-1, P).T)


_WEIGHTS = ["x", "a_w_in", "a_w_out", "b_w_in", "b_w_gate_f", "b_w_gate_b", "b_w_out", "ffn_w_gate_up",
            "ffn_w_down", "ctx_2", "w_mod_2", "w_in_2", "w_pa_2", "w_pd_2", "w_out_2", "w_up_2", "w_down_2"]


def kernel(**inputs):
    import concourse.bacc as bacc
    from concourse.bass_utils import run_bass_kernel_spmd

    g = {k: np.asarray(v) for k, v in inputs.items()}
    consts, const_at = pack(list(constants().items()))
    conv = np.concatenate([g["ffn_conv_w_2"][0], g["ffn_conv_b_2"]], 0)
    conv = conv.reshape(4, 2, FT, P).transpose(3, 1, 0, 2).reshape(P, -1)
    gdn_conv = g["conv_qkv_w_2"][0].reshape(3, 24, P).transpose(2, 1, 0).reshape(P, -1)
    vecs, vec_at = pack([
        ("attn_norm", by_partition(g["attn_norm"])), ("ffn_norm", by_partition(g["ffn_norm"])),
        ("gla_bias", by_partition(np.concatenate([g["b_gate_bias_f"], g["b_gate_bias_b"]], 0))),
        ("c", by_partition(g["c_2"])), ("c_ctx", by_partition(g["c_ctx_2"][None])),
        ("ffn_conv", conv), ("gdn_conv", gdn_conv)])
    rows, row_at = pack([(n, g[s].reshape(-1)) for n, s in (
        ("b_out_norm", "b_out_norm"), ("q_norm", "q_norm_w_2"), ("k_norm", "k_norm_w_2"), ("a_log", "a_log_2"),
        ("dt_bias", "dt_bias_2"), ("gdn_norm", "gdn_norm_w_2"), ("final_norm", "final_norm_w_2"), ("b_mod", "b_mod_2"))]
        + [("a_gains", np.concatenate([g["a_q_norm"], g["a_k_norm"]], 0).reshape(-1))])
    arrays = {n: np.ascontiguousarray(g[n]) for n in _WEIGHTS}
    arrays.update(consts=consts, vecs=vecs, rows=rows, a_mask=attention_masks())

    nc = bacc.Bacc("TRN2", target_bir_lowering=False, num_devices=1)
    ins = {n: nc.dram_tensor(f"in_{n}", a.shape, F32, kind="ExternalInput").ap() for n, a in arrays.items()}
    out = nc.dram_tensor("out", (1, SEQ, D), F32, kind="ExternalOutput").ap()
    build(nc, ins, out, const_at, vec_at, row_at)
    r = run_bass_kernel_spmd(nc, [{f"in_{n}": a for n, a in arrays.items()}], core_ids=[0])
    return r.results[0]["out"]
```

```python
from contextlib import contextmanager

import concourse.bass as bass
from concourse import mybir
import numpy as np

F32 = mybir.dt.float32
F32R = mybir.dt.float32r
I32 = mybir.dt.int32
ALU = mybir.AluOpType
ACT = mybir.ActivationFunctionType
AX = mybir.AxisListType

P = 128
D = 1024
KT = D // P
SEQ = 256
TT = SEQ // P
EPS = 1e-6
CW = 512
HK = 4

A_GROUPS = ((128, 1), (512, 4), (2048, 16))
NG = len(A_GROUPS)
A_HEADS, A_HD = 16, 64
GLA_HEADS, GLA_DK, GLA_DV, GLA_RANK, GLA_TAU = 4, 128, 256, 16, 16.0
CHUNK = 64
NCH = SEQ // CHUNK
FF = 2816
FT = FF // P
N_FFC = FF // 256
NH2, KV2, HD2 = 8, 2, 128
GROUP2 = NH2 // KV2
GDN_HEADS, GDN_D = 8, 128
NT2 = 4
NK = 10
LEVELS = (1, 2, 4, 8, 16, 32)
GDN_PER = dict(pe=80, act=43, dve=50, pool=7)


def constants():
    p = np.arange(P)
    f32 = np.float32
    c = {}
    c["ident"] = np.eye(P, dtype=f32)
    same = p[:, None] // CHUNK == p[None, :] // CHUNK
    c["gla_f"] = (same & (p[:, None] <= p[None, :])).astype(np.int32).view(f32)
    c["gla_b"] = (same & (p[:, None] > p[None, :])).astype(np.int32).view(f32)
    c["cum_f"] = (same & (p[:, None] <= p[None, :])).astype(f32)
    c["cum_b"] = (same & (p[:, None] >= p[None, :])).astype(f32)
    c["ones_bd"] = same.astype(f32)
    c["even"] = np.repeat((p[:, None] < CHUNK), P, 1).astype(f32)
    c["odd"] = np.repeat((p[:, None] >= CHUNK), P, 1).astype(f32)
    c["ones"] = np.ones((P, P), f32)
    c["neg_f"] = np.where(same & (p[:, None] <= p[None, :]), 0, -1e30).astype(f32)
    c["neg_b"] = np.where(same & (p[:, None] >= p[None, :]), 0, -1e30).astype(f32)
    for b in LEVELS:
        m = (p[:, None] // (2 * b) == p[None, :] // (2 * b)) & (p[:, None] // b != p[None, :] // b)
        c[f"level{b}"] = m.astype(f32)
    tok = np.arange(SEQ).reshape(TT, P).T.astype(f32)
    half = A_HD // 2
    inv = (10000.0 ** (-np.arange(half, dtype=f32) / half)).astype(f32)
    ang = (tok[:, :, None] * inv).astype(f32)
    c["cos_a"] = np.concatenate([np.cos(ang)] * 2, -1).astype(f32).reshape(P, -1)
    c["sin_a"] = np.concatenate([-np.sin(ang), np.sin(ang)], -1).astype(f32).reshape(P, -1)
    inv = (10000.0 ** (-np.arange(0, 64, 2, dtype=f32) / 64)).astype(f32)
    both = []
    for ids in (tok // 64, tok % 64):
        a = (ids.astype(f32)[:, :, None] * inv).astype(f32)
        both.append((np.concatenate([np.cos(a)] * 2, -1), np.concatenate([-np.sin(a), np.sin(a)], -1)))
    c["cos_2"] = np.concatenate([both[0][0], both[1][0]], -1).astype(f32).reshape(P, -1)
    c["sin_2"] = np.concatenate([both[0][1], both[1][1]], -1).astype(f32).reshape(P, -1)
    return c


def attention_masks():
    i, j = np.arange(SEQ)[:, None], np.arange(SEQ)[None, :]
    m = [np.where((abs(i - j) <= w // 2) & ((i - j) % d == 0), 0, -1e30) for w, d in A_GROUPS]
    m = np.stack(m, 1).astype(np.float32)
    return np.ascontiguousarray(m.reshape(TT, P, NG, SEQ).transpose(1, 0, 2, 3)).reshape(P, -1)


class Counter:

    def __init__(self, nc, name):
        self.sem, self.name, self.n = nc.alloc_semaphore(name), name, 0
        self.var, self.per, self.top = None, 0, 0

    def inc(self, ins, by=1):
        ins.then_inc(self.sem, by)
        self.n += by
        return (self, self.n, self.var is not None)

    def now(self):
        return (self, self.n, self.var is not None)

    def back(self, k):
        return (self, max(self.n - k, 0), self.var is not None)


def w(eng, *marks):
    best = {}
    for m in marks:
        if m is not None and (m[0] not in best or best[m[0]][1] <= m[1]):
            best[m[0]] = m
    for c, v, moving in best.values():
        if moving and c.var is not None and c.per:
            eng.wait_ge(c.sem, c.var * c.per + v)
        elif v > 0:
            eng.wait_ge(c.sem, v)


def bc(ap, axis, n):
    ap = ap.unsqueeze(axis)
    shape = list(ap.shape)
    shape[axis] = n
    return ap.to_broadcast(shape)


def build(nc, ins, out, const_at, vec_at, row_at):
    pe, act, dve, pool, sp = nc.tensor, nc.scalar, nc.vector, nc.gpsimd, nc.sync
    T, A, V, G = (Counter(nc, "s_" + n) for n in ("pe", "act", "dve", "pool"))
    raw_in = [Counter(nc, f"s_raw{i}") for i in range(2)]
    hi_ok = [Counter(nc, f"s_hi{i}") for i in range(2)]
    lo_ok = [Counter(nc, f"s_lo{i}") for i in range(2)]
    used = [Counter(nc, f"s_used{i}") for i in range(2)]
    L = Counter(nc, "s_small")
    stored = Counter(nc, "s_stored")
    counters = [T, A, V, G, *raw_in, *hi_ok, *lo_ok, *used]

    def w_apart(eng, *marks):
        w(eng, *marks)
        if eng is dve:
            dve.memset(unused[:, 0:1], 0.0)
        elif eng is act:
            act.activation(unused[:, 3:4], unused[:, 1:2], ACT.Copy)
        else:
            pool.tensor_tensor(unused[:, 2:3], unused[:, 1:2], unused[:, 1:2], ALU.add)

    @contextmanager
    def loop(n, chunks, **per):
        names = dict(pe=T, act=A, dve=V, pool=G)
        each = {c: 0 for c in counters}
        each.update({names[k]: v for k, v in per.items()})
        each.update({c: chunks for c in (*hi_ok, *lo_ok, *used)})
        each.update({c: 32 * chunks for c in raw_in})
        with nc.Fori(0, n) as i:
            for c in counters:
                c.var, c.per, c.top = i, each[c], c.n
            yield i
            made = {c.name: (c.n - c.top, c.per) for c in counters}
            assert all(a == b for a, b in made.values()), f"increments per iteration: {made}"
            for c in counters:
                c.n, c.var = c.top + n * c.per, None

    at = [nc.sbuf_base + (-nc.sbuf_base) % 64]

    def place(name, shape, dt=F32, offset=None):
        n = int(np.prod(shape[1:]))
        t = nc.alloc_sbuf_tensor_at(name, shape, dt, offset=at[0] if offset is None else offset)
        if offset is None:
            at[0] += 4 * n
        return t

    ps = nc.alloc_psum_tensor("ps", [P, 8, 512], F32)
    raw = place("raw", [P, 2, HK, CW])
    whi = place("whi", [P, 2, HK, CW], F32R)
    wlo = place("wlo", [P, 2, HK, CW], F32R)
    resid = place("resid", [P, TT, D])
    cst = place("cst", [P, ins["consts"].shape[1]])
    vec = place("vec", [P, ins["vecs"].shape[1]])
    modcol = place("modcol", [P, 4, KT, 2])
    grow = place("grow", [P, 2, D])
    ccur = place("ccur", [P, 2, 16])
    small = place("small", [P, 8])
    unused, eps_col = small[:, 0:4], small[:, 4:5]
    xs = place("xs", [P, 4, KT, SEQ], F32R)
    arena_at = at[0]
    arena_n = (nc.sbuf_usable_end - arena_at) // 4 // 8 * 8
    hid = place("hid", [P, 2, FT, SEQ], F32R, offset=arena_at + 4 * (arena_n - 2 * FT * SEQ))
    XS = 4 * KT * SEQ
    wide = place("wide", [P, arena_n + XS], offset=arena_at - 4 * XS)

    class Carve:

        def __init__(self, start=0, end=arena_n):
            self.at, self.end = start, end

        def __call__(self, *shape):
            n = int(np.prod(shape))
            v = wide[:, XS + self.at:XS + self.at + n]
            self.at += n
            assert self.at <= self.end, (self.at, self.end)
            names = "abcdef"[:len(shape)]
            if len(shape) > 1:
                v = v.rearrange(f"p ({' '.join(names)}) -> p {' '.join(names)}", **dict(zip(names, shape)))
            return v

    def const(name):
        a, b = const_at[name]
        return cst[:, a:b]

    def vcol(name):
        a, b = vec_at[name]
        return vec[:, a:b]

    def load_row(dst, name):
        a, b = row_at[name]
        L.inc(act.dma_start(dst, ins["rows"][a:b].partition_broadcast(P)), 16)

    ident = const("ident")

    def xh(k, t0, t1, seq=0):
        return xs[:, 2 * seq, k, t0:t1]

    def xl(k, t0, t1, seq=0):
        return xs[:, 2 * seq + 1, k, t0:t1]

    def request(source):
        if source is None:
            return
        for s in range(2):
            srcs, nk = source(s)
            w(sp, hi_ok[s].now(), lo_ok[s].now())
            for (k0, k1, c0, c1), src in srcs:
                raw_in[s].inc(sp.dma_start(raw[:, s, k0:k1, c0:c1], src), 16)
            w(act, raw_in[s].now(), used[s].now())
            hi_ok[s].inc(act.activation(whi[:, s, 0:nk, :], raw[:, s, 0:nk, :], ACT.Copy))
            w(dve, raw_in[s].now(), hi_ok[s].now())
            lo_ok[s].inc(dve.tensor_tensor(wlo[:, s, 0:nk, :], raw[:, s, 0:nk, :],
                                           whi[:, s, 0:nk, :].bitcast(F32), ALU.subtract))

    def cols(wmat, c0, k0=0, nks=(HK, HK)):
        def source(s):
            nk, kk = nks[s], k0 + (nks[0] if s else 0)
            h = nk // 2
            return [((j * h, (j + 1) * h, 0, CW),
                     wmat[(kk + j * h) * P:(kk + (j + 1) * h) * P, bass.ds(c0, CW)].rearrange("(k p) n -> p k n", p=P))
                    for j in range(2)], nk
        return source

    def gate_up(wmat, c):
        def source(s):
            return [((0, HK, 256 * j, 256 * (j + 1)),
                     wmat[s * HK * P:(s + 1) * HK * P, bass.ds(c * 256 + j * FF, 256)].rearrange("(k p) n -> p k n", p=P))
                    for j in range(2)], HK
        return source

    def mm3(o, ahi, alo, bhi, blo, start, stop):
        pe.matmul(o, ahi, bhi, start=start, stop=False)
        pe.matmul(o, ahi, blo, start=False, stop=False)
        return pe.matmul(o, alo, bhi, start=False, stop=stop)

    def chunk_tok(banks, tiles=(0, 1), width=CW):
        for s in range(2):
            w(pe, hi_ok[s].now(), lo_ok[s].now())
            for b, t in zip(banks, tiles):
                for k in range(HK):
                    kk, t0 = s * HK + k, (t % 2) * P
                    i_ = mm3(ps[:, b, 0:width], xh(kk, t0, t0 + P, t // 2), xl(kk, t0, t0 + P, t // 2),
                             whi[:, s, k, 0:width], wlo[:, s, k, 0:width],
                             s == 0 and k == 0, s == 1 and k == HK - 1)
            m = used[s].inc(i_)
        return m

    def chunk_feat(banks, both=False):
        n = 2 * SEQ if both else SEQ
        for s in range(2):
            w(pe, hi_ok[s].now(), lo_ok[s].now())
            for mb, b in enumerate(banks):
                for k in range(HK):
                    kk = s * HK + k
                    if both:
                        rh, rl = xs[:, 0:4:2, kk, :], xs[:, 1:4:2, kk, :]
                    else:
                        rh, rl = xs[:, 0, kk, :], xs[:, 1, kk, :]
                    i_ = mm3(ps[:, b, 0:n], whi[:, s, k, mb * P:(mb + 1) * P],
                             wlo[:, s, k, mb * P:(mb + 1) * P], rh, rl,
                             s == 0 and k == 0, s == 1 and k == HK - 1)
            m = used[s].inc(i_)
        return m

    def settle(*engs):
        for e in engs or (pe, act, dve, pool):
            w(e, T.now(), A.now(), V.now(), G.now(), used[0].now(), used[1].now())

    def rsqrt(dst, src):
        w(dve, A.inc(act.activation(dst, src, ACT.Sqrt, bias=eps_col)))
        return V.inc(dve.reciprocal(dst, dst))

    def rstd_of(src, n, width, st, sq):
        for j in range(n):
            w(act, A.now())
            A.inc(act.activation(sq, src[:, j, :], ACT.Square, scale=width ** -0.5, accum_out=st[:, j:j + 1]))
        w(act, A.now())
        rsqrt(st[:, 0:n], st[:, 0:n])

    def to_split(src, seq, stage, scale=None, shift=None):
        read = [None, None]
        for g in range(KT // 2):
            b = g % 2
            w(pe, read[b])
            for j in range(2):
                for t in range(TT):
                    i_ = pe.transpose(ps[:, b, (j * 2 + t) * P:(j * 2 + t + 1) * P], src(t, 2 * g + j), ident)
            m = T.inc(i_)
            view = ps[:, b, :].rearrange("p (k n) -> p k n", k=2)
            stv = stage[:, b, :].rearrange("p (k n) -> p k n", k=2)
            w(dve, m, V.now())
            if scale is None:
                V.inc(dve.tensor_copy(stv, view))
            else:
                V.inc(dve.tensor_tensor(stv, view, bc(scale[:, 2 * g:2 * g + 2], 2, SEQ), ALU.mult))
            read[b] = V.now()
            if shift is not None:
                w(dve, V.now())
                V.inc(dve.tensor_tensor(stv, stv, bc(shift[:, 2 * g:2 * g + 2], 2, SEQ), ALU.add))
            w(act, V.now())
            hs = xs[:, 2 * seq, 2 * g:2 * g + 2, :]
            A.inc(act.activation(hs, stv, ACT.Copy))
            w(dve, A.now())
            V.inc(dve.tensor_tensor(xs[:, 2 * seq + 1, 2 * g:2 * g + 2, :], stv, hs.bitcast(F32), ALU.subtract))
        w(pe, A.now(), V.now())

    def norm_split(src, seq, c, scale, shift=None):
        st, sq, xn, stage = c(8), c(D), c(TT, D), c(2, 512)
        settle()
        rstd_of(src, TT, D, st, sq)
        w(dve, V.now())
        for t in range(TT):
            V.inc(dve.tensor_scalar(xn[:, t, :], src[:, t, :], st[:, t:t + 1], None, ALU.mult))
        w(pe, V.now())
        to_split(lambda t, k: xn[:, t, k * P:(k + 1) * P], seq, stage, scale, shift)

    def add_product(wmat, nxt, gate=None, tmp=None):
        for n in range(2):
            m = chunk_tok((2 * n, 2 * n + 1))
            request(cols(wmat, CW) if n == 0 else nxt)
            o = resid[:, :, n * CW:(n + 1) * CW]
            w(dve, m, V.now())
            if gate is None:
                V.inc(dve.tensor_tensor(o, o, ps[:, 2 * n:2 * n + 2, :], ALU.add))
            else:
                V.inc(dve.tensor_tensor(tmp, ps[:, 2 * n:2 * n + 2, :], bc(gate[:, n * CW:(n + 1) * CW], 1, TT), ALU.mult))
                w(dve, V.now())
                V.inc(dve.tensor_tensor(o, o, tmp, ALU.add))

    def ffn(w_up, w_down, nxt, conv=None, gate=None):
        settle()
        c = Carve(end=arena_n - 2 * FT * SEQ)
        tmp, val = c(2, 2, SEQ), c(2, 2, SEQ)
        yb, zb = (c(2, 4, SEQ), c(2, 4, SEQ)) if conv is not None else (None, None)
        prod = c(TT, CW)
        nv, na, ng = (4, 3, 1) if conv is not None else (2, 2, 0)

        def one(ci, par, after):
            b0 = 4 * par
            w(pe, V.back(nv), A.back(na))
            m = chunk_feat(range(b0, b0 + 4))
            two_ago = (V.back(nv), A.back(na))
            request(after)
            up = ps[:, b0 + 2:b0 + 4, 0:SEQ]
            if conv is None:
                w(act, m, *two_ago)
                A.inc(act.activation(tmp[:, par, :, :], ps[:, b0:b0 + 2, 0:SEQ], ACT.Silu))
            else:
                y, z = yb[:, par, :, :], zb[:, par, :, :]
                taps = ccur[:, par, :].rearrange("p (a t b) -> p a t b", a=2, t=4)
                w(pool, *two_ago)
                G.inc(pool.tensor_copy(taps, conv[:, :, :, bass.ds(ci * 2, 2)]))
                tap = [[taps[:, q // 2, t, q % 2:q % 2 + 1] for t in range(4)] for q in range(4)]
                w(act, m, G.now(), *two_ago)
                for q in range(4):
                    i_ = act.activation(y[:, q, :], ps[:, b0 + q, 0:SEQ], ACT.Identity, scale=tap[q][1], bias=tap[q][3])
                A.inc(i_)
                w(dve, A.now(), V.now())
                for q in range(4):
                    dve.scalar_tensor_tensor(z[:, q, 1:SEQ], ps[:, b0 + q, 0:SEQ - 1], tap[q][0],
                                             y[:, q, 1:SEQ], ALU.mult, ALU.add)
                V.inc(dve.tensor_copy(z[:, :, 0:1], y[:, :, 0:1]))
                w(dve, V.now())
                for q in range(4):
                    dve.scalar_tensor_tensor(y[:, q, 0:SEQ - 1], ps[:, b0 + q, 1:SEQ], tap[q][2],
                                             z[:, q, 0:SEQ - 1], ALU.mult, ALU.add)
                V.inc(dve.tensor_copy(y[:, :, SEQ - 1:SEQ], z[:, :, SEQ - 1:SEQ]))
                w(act, V.now())
                A.inc(act.activation(tmp[:, par, :, :], y[:, 0:2, :], ACT.Silu))
                up = y[:, 2:4, :]
            w(dve, A.now(), V.now())
            V.inc(dve.tensor_tensor(val[:, par, :, :], tmp[:, par, :, :], up, ALU.mult))
            w(act, V.now())
            hs = hid[:, 0, bass.ds(ci * 2, 2), :]
            A.inc(act.activation(hs, val[:, par, :, :], ACT.Copy))
            w(dve, A.now())
            V.inc(dve.tensor_tensor(hid[:, 1, bass.ds(ci * 2, 2), :], val[:, par, :, :], hs.bitcast(F32), ALU.subtract))

        with loop((N_FFC - 1) // 2, 2, dve=2 * nv, act=2 * na, pool=2 * ng) as i:
            one(i * 2, 0, gate_up(w_up, i * 2 + 1))
            one(i * 2 + 1, 1, gate_up(w_up, i * 2 + 2))
        splits = ((0, (HK, HK)), (8, (HK, HK)), (16, (HK, 2)))
        one(N_FFC - 1, 0, cols(w_down, 0, *splits[0]))
        settle(pe)
        for n in range(2):
            for j, (k0, nks) in enumerate(splits):
                for s in range(2):
                    w(pe, hi_ok[s].now(), lo_ok[s].now())
                    for t in range(TT):
                        for k in range(nks[s]):
                            kk = k0 + s * HK + k
                            i_ = mm3(ps[:, 2 * n + t, :], hid[:, 0, kk, t * P:(t + 1) * P],
                                     hid[:, 1, kk, t * P:(t + 1) * P], whi[:, s, k, :], wlo[:, s, k, :],
                                     kk == 0, kk == FT - 1)
                    m = used[s].inc(i_)
                if j < 2:
                    request(cols(w_down, n * CW, *splits[j + 1]))
                else:
                    request(cols(w_down, CW, *splits[0]) if n == 0 else nxt)
            o = resid[:, :, n * CW:(n + 1) * CW]
            pv = ps[:, 2 * n:2 * n + 2, :]
            w(dve, m, V.now())
            if gate is not None:
                V.inc(dve.tensor_tensor(prod, pv, bc(gate[:, n * CW:(n + 1) * CW], 1, TT), ALU.mult))
                w(dve, V.now())
                pv = prod
            V.inc(dve.tensor_tensor(o, o, pv, ALU.add))

    def head_norm_rope(x, nh, hd, nt, cos, sin, dst, bufs, rope=True):
        sq, r, xn, a, b = bufs
        n = nt * nh
        g = sq[:, 0:n * hd]
        w(act, V.now(), G.now())
        A.inc(act.activation(g.rearrange("p (t m) -> p t m", t=nt), x, ACT.Square, scale=hd ** -0.5))
        w(dve, A.now())
        V.inc(dve.tensor_reduce(r[:, 0:n], g.rearrange("p (n d) -> p n d", d=hd), AX.X, ALU.add))
        w(act, V.now())
        rsqrt(r[:, 0:n], r[:, 0:n])
        w(dve, V.now(), G.now())
        xv = xn[:, 0:n * hd].rearrange("p (t h d) -> p t h d", t=nt, d=hd)
        for t in range(nt):
            i_ = dve.tensor_tensor(xv[:, t], x[:, t, :].rearrange("p (h d) -> p h d", d=hd),
                                   bc(r[:, t * nh:(t + 1) * nh], 2, hd), ALU.mult)
        V.inc(i_)
        done_psum = V.now()
        av, bv = (q[:, 0:n * hd].rearrange("p (t h d) -> p t h d", t=nt, d=hd) for q in (a, b))
        w_apart(pool, V.now())
        for t in range(nt):
            i_ = pool.tensor_tensor(av[:, t], xv[:, t], bc(cos[:, t, :], 1, nh), ALU.mult)
        G.inc(i_)
        w(dve, V.now())
        hh = 32
        for t in range(nt):
            for q in range(hd // 64):
                for s_ in range(2):
                    o0, i0 = q * 64 + s_ * hh, q * 64 + (1 - s_) * hh
                    i_ = dve.tensor_tensor(bv[:, t, :, o0:o0 + hh], xv[:, t, :, i0:i0 + hh],
                                           bc(sin[:, t, o0:o0 + hh], 1, nh), ALU.mult)
        V.inc(i_)
        w_apart(pool, V.now(), G.now())
        for t in range(nt):
            i_ = pool.tensor_tensor(dst(t), av[:, t], bv[:, t], ALU.add)
        G.inc(i_)
        return done_psum

    def layer_a(nxt):
        w_in, w_out = ins["a_w_in"][0], ins["a_w_out"][0]
        c = Carve()
        q_k = c(2, NG, TT, D)
        vv = c(NG, TT, D)
        keep = c.at
        tabs = c(2, NG, 2, TT, A_HD)
        gains = c(2, NG, A_HD)
        sq = c(1024)
        bufs = (sq, c(16), c(1024), c(1024), sq)
        load_row(gains.rearrange("p a b c -> p (a b c)"), "a_gains")
        w(pool, L.now())
        cosv = const("cos_a").rearrange("p (t d) -> p t d", t=TT)
        sinv = const("sin_a").rearrange("p (t d) -> p t d", t=TT)
        for j in range(2):
            for g in range(NG):
                for t in range(TT):
                    G.inc(pool.tensor_tensor(tabs[:, 0, g, j, t, :], cosv[:, t, :], gains[:, j, g, :], ALU.mult))
                    for s_ in range(2):
                        o, i_ = slice(s_ * 32, s_ * 32 + 32), slice(32 - s_ * 32, 64 - s_ * 32)
                        G.inc(pool.tensor_tensor(tabs[:, 1, g, j, t, o], sinv[:, t, o], gains[:, j, g, i_], ALU.mult))
        w(dve, G.now())

        def chunk(g, j, nxt_, ends):
            kind, half, gi = j // 2, j % 2, bass.ds(g, 1)
            b0 = 2 * (j % 4)
            w(pe, *ends[max(j - 1, 0)])
            m = chunk_tok((b0, b0 + 1))
            request(nxt_)
            w(act, m)
            w(dve, m)
            x = ps[:, b0:b0 + 2, :]
            flat = "p a t d -> p (a t) d"
            if kind < 2:
                head_norm_rope(
                    x, 8, A_HD, TT, tabs[:, 0, gi, kind, :, :].rearrange(flat), tabs[:, 1, gi, kind, :, :].rearrange(flat),
                    lambda t: q_k[:, kind, gi, t, half * CW:(half + 1) * CW].rearrange("p a (h d) -> p (a h) d", d=A_HD),
                    bufs)
            else:
                A.inc(act.activation(vv[:, gi, :, half * CW:(half + 1) * CW].rearrange(flat), x, ACT.Copy))
            ends.append((V.now(), A.now()))

        with loop(NG - 1, 6, act=2 * 4 + 2, dve=4 * 4, pool=2 * 4) as g:
            ends = [(V.now(), A.now())]
            for j in range(6):
                chunk(g, j, cols(w_in, g * (3 * D) + (j + 1) * CW), ends)
        ends = [(V.now(), A.now())]
        for j in range(6):
            chunk(NG - 1, j, cols(w_in, (NG - 1) * 3 * D + (j + 1) * CW) if j < 5 else cols(w_out, 0), ends)

        o = Carve(-TT * D, 0)(TT, D)
        c = Carve(-XS, -TT * D)
        stg = c(2, 6, P)
        kT = [c(6, P) for _ in range(2)]
        qz = [[c(6, P) for _ in range(2)] for _ in range(2)]
        c = Carve(start=keep)
        S, E, ET = (c(2, NG * SEQ) for _ in range(3))
        mask = c(TT, NG * SEQ)
        U = 8
        mx, ngm, l, rl = (c(U) for _ in range(4))
        settle()
        w(act, V.now())
        L.inc(act.dma_start(mask.rearrange("p a b -> p (a b)"), ins["a_mask"]), 16)
        w(dve, L.now())
        for z_ in qz:
            for h in range(2):
                V.inc(dve.memset(z_[h][64 - 64 * h:128 - 64 * h, :, :], 0.0))
        scale = A_HD ** -0.5

        def columns(hp, off, n):
            return bass.ds(hp * P + off, n) if not isinstance(hp, int) else slice(hp * P + off, hp * P + off + n)

        def stage_pair(hp, *free):
            w_apart(pool, *free)
            for kind in range(2):
                for g in range(NG):
                    i_ = pool.tensor_copy(stg[:, kind, 2 * g:2 * g + 2, :], q_k[:, kind, g, :, columns(hp, 0, P)])
            return G.inc(i_)

        def transposed(kind, par, b, staged, *free):
            w(pe, staged, *free)
            for j in range(6):
                i_ = pe.transpose(ps[:, b + j // 4, (j % 4) * P:(j % 4 + 1) * P], stg[:, kind, j, :], ident)
            src = ps[:, b:b + 2, :].rearrange("p a b -> p (a b)")
            m = T.inc(i_)
            if kind:
                w(act, m)
                return A.inc(act.activation(kT[par].rearrange("p a b -> p (a b)"), src[:, 0:768], ACT.Copy))
            w(dve, m)
            for h in range(2):
                r = slice(64 * h, 64 * h + 64)
                i_ = dve.tensor_copy(qz[par][h][r].rearrange("p a b -> p (a b)"), src[r, 0:768])
            return V.inc(i_)

        def two_pairs(i, ready, last):
            ex, read, out, et = {0: ready["exp"]}, {0: ready["read"]}, {-2: ready["out"], -1: ready["out"]}, {}
            pair_ok, staged = {0: None, 1: None}, ready["staged"]
            bank_ok = {0: None, 1: None}

            def scores(u, after_pair=()):
                pr, h, t, par = u // 4 % 2, u // 2 % 2, u % 2, u % 2
                b = 4 + 2 * par
                w(pe, read.get(u - 2), ready["out"] if u < 2 else None, *after_pair)
                for g in range(NG):
                    i_ = pe.matmul(ps[:, b + g // 2, (g % 2) * SEQ:(g % 2 + 1) * SEQ], qz[pr][h][:, 2 * g + t, :],
                                   kT[pr][:, 2 * g:2 * g + 2, :], start=True, stop=True)
                w_apart(dve, T.inc(i_), ex.get(u - 2, ready["exp"]))
                n = u % U
                sc = ps[:, b:b + 2, :].rearrange("p a b -> p (a b)")[:, 0:NG * SEQ]
                read[u] = V.inc(dve.tensor_tensor_reduce(out=S[:, par, :], in0=sc, in1=mask[:, t, :], scale=1.0, scalar=-3e38,
                                                         op0=ALU.add, op1=ALU.max, accum_out=mx[:, n:n + 1]))
                w(dve, read[u])
                return V.inc(dve.tensor_scalar(ngm[:, n:n + 1], mx[:, n:n + 1], -scale, None, ALU.mult))

            def exponentials(u, m):
                par, n = u % 2, u % U
                w(act, m, T.now())
                ex[u] = A.inc(act.activation(E[:, par, :], S[:, par, :], ACT.Exp, bias=ngm[:, n:n + 1], scale=scale,
                                             accum_out=l[:, n:n + 1]))

            def transposes(u):
                par, n = u % 2, u % U
                b = 2 * par
                w(pe, ex[u], out[u - 2], bank_ok[par])
                for j in range(6):
                    i_ = pe.transpose(ps[:, b + j // 4, (j % 4) * P:(j % 4 + 1) * P], E[:, par, j * P:(j + 1) * P], ident)
                tm = T.inc(i_)
                w(act, tm)
                ma = A.inc(act.activation(ET[:, par, 0:512], ps[:, b, :], ACT.Copy))
                w(dve, tm, ex[u])
                mv = V.inc(dve.tensor_copy(ET[:, par, 512:768], ps[:, b + 1, 0:256]))
                et[u] = (ma, mv, V.inc(dve.reciprocal(rl[:, n:n + 1], l[:, n:n + 1])))

            def values(u):
                pr, h, t, par = u // 4, u // 2 % 2, u % 2, u % 2
                w(pe, *et[u][:2])
                po = ps[:, 2 * par + 1, 256:384]
                for j in range(6):
                    i_ = pe.matmul(po, ET[:, par, j * P:(j + 1) * P], vv[:, j // 2, j % 2, columns(i * 2 + pr, 0, P)],
                                   start=(j == 0), stop=(j == 5))
                w(dve, T.inc(i_), et[u][2])
                out[u] = V.inc(dve.tensor_scalar(o[:, t, columns(i * 2 + pr, 64 * h, 64)], po[:, 64 * h:64 * h + 64],
                                                 rl[:, u:u + 1], None, ALU.mult))

            for u in range(U):
                m = None
                if u + 1 < U or not last:
                    after_pair = (pair_ok[1], ready.get("k1")) if u + 1 == 4 else (pair_ok[0], ready.get("k0")) if u + 1 == U else ()
                    m = scores(u + 1, after_pair)
                transposes(u)
                if m is not None:
                    exponentials(u + 1, m)
                if u:
                    values(u - 1)
                if u in (1, 2) or (u in (5, 6) and not last):
                    kind, par_ = 0 if u in (1, 5) else 1, 1 if u < 4 else 0
                    b = 2 * ((u - 1) % 2)
                    ok = transposed(kind, par_, b, staged, out[u - 1])
                    bank_ok[(u - 1) % 2] = ok
                    if kind == 0:
                        pair_ok[par_] = ok
                    else:
                        ready[f"k{par_}"] = ok
                        if par_ == 1 and not last:
                            staged = stage_pair(i * 2 + 2, T.now())
                        elif par_ == 0:
                            staged = stage_pair(i * 2 + 3, T.now())
            values(U - 1)

        m = stage_pair(0, V.now())
        mq = transposed(0, 0, 0, m, V.now())
        mk = transposed(1, 0, 2, m)
        m = stage_pair(1, T.now())
        for g in range(NG):
            w(pe, mq, mk)
            i_ = pe.matmul(ps[:, 4 + g // 2, (g % 2) * SEQ:(g % 2 + 1) * SEQ], qz[0][0][:, 2 * g, :],
                           kT[0][:, 2 * g:2 * g + 2, :], start=True, stop=True)
        w_apart(dve, T.inc(i_))
        V.inc(dve.tensor_tensor_reduce(out=S[:, 0, :], in0=ps[:, 4:6, :].rearrange("p a b -> p (a b)")[:, 0:NG * SEQ],
                                       in1=mask[:, 0, :], scale=1.0, scalar=-3e38, op0=ALU.add, op1=ALU.max,
                                       accum_out=mx[:, 0:1]))
        w(dve, V.now())
        V.inc(dve.tensor_scalar(ngm[:, 0:1], mx[:, 0:1], -scale, None, ALU.mult))
        w(act, V.now())
        A.inc(act.activation(E[:, 0, :], S[:, 0, :], ACT.Exp, bias=ngm[:, 0:1], scale=scale, accum_out=l[:, 0:1]))

        def before():
            return {"exp": A.now(), "read": V.now(), "out": V.now(), "staged": G.now()}

        with loop(A_HEADS // 4 - 1, 0, pe=3 * U + 4, act=2 * U + 2, dve=5 * U + 2, pool=2) as i:
            two_pairs(i, before(), False)
        two_pairs(A_HEADS // 4 - 1, before(), True)

        c = Carve()
        stage = c(2, 512)
        settle()
        to_split(lambda t, k: o[:, t, k * P:(k + 1) * P], 0, stage)
        add_product(w_out, nxt)

    def layer_b(nxt):
        w_in, w_out = ins["b_w_in"][0], ins["b_w_out"][0]
        QK, VW = GLA_HEADS * GLA_DK, GLA_HEADS * GLA_DV
        settle()
        c = Carve()
        qT, kT_ = c(GLA_HEADS, SEQ), c(GLA_HEADS, SEQ)
        v, r = c(TT, VW), c(TT, VW)
        la = c(2, GLA_HEADS * SEQ)
        wz = c(KT, 2 * GLA_RANK)
        z, zT = c(TT, 2 * GLA_RANK), c(2, SEQ)
        wg = c(2, QK)
        gain = c(VW)
        t1, t2 = c(2, GLA_HEADS * SEQ), c(2, GLA_HEADS * SEQ)
        w(act, V.now(), T.now(), G.now())
        L.inc(act.dma_start(wz, w_in[:, 2 * QK + 2 * VW:].rearrange("(k p) n -> p k n", p=P)), 16)
        L.inc(act.dma_start(wg[0:GLA_RANK, 0, :], ins["b_w_gate_f"][0]), 16)
        L.inc(act.dma_start(wg[0:GLA_RANK, 1, :], ins["b_w_gate_b"][0]), 16)
        load_row(gain, "b_out_norm")

        m = chunk_feat(range(0, 4))
        request(cols(w_in, CW))
        w(act, m)
        A.inc(act.activation(qT, ps[:, 0:4, 0:SEQ], ACT.Copy, scale=GLA_DK ** -0.5))
        m = chunk_feat(range(4, 8))
        request(cols(w_in, 2 * CW))
        w(act, m)
        A.inc(act.activation(kT_, ps[:, 4:8, 0:SEQ], ACT.Copy))
        for j in range(4):
            dst = (v, r)[j // 2]
            b0 = 2 * j
            w(pe, A.now())
            m = chunk_tok((b0, b0 + 1))
            request(cols(w_in, (3 + j) * CW) if j < 3 else cols(w_out, 0))
            w(act, m)
            o_ = dst[:, :, (j % 2) * CW:(j % 2 + 1) * CW]
            A.inc(act.activation(o_, ps[:, b0:b0 + 2, :], ACT.Copy if j < 2 else ACT.Silu))
        w(pe, L.now(), A.now(), V.now())
        for t in range(TT):
            for k in range(KT):
                pe.matmul(ps[:, t, 0:32], xs[:, 0, k, t * P:(t + 1) * P].bitcast(F32), wz[:, k, :], start=(k == 0), stop=False)
                i_ = pe.matmul(ps[:, t, 0:32], xs[:, 1, k, t * P:(t + 1) * P].bitcast(F32), wz[:, k, :], start=False, stop=(k == KT - 1))
        w(dve, T.inc(i_))
        V.inc(dve.tensor_copy(z, ps[:, 0:2, 0:32]))
        w(pe, V.now())
        for d in range(2):
            for t in range(TT):
                i_ = pe.transpose(ps[0:GLA_RANK, 2 + d, t * P:(t + 1) * P], z[:, t, 16 * d:16 * d + 16], ident)
        w(dve, T.inc(i_))
        V.inc(dve.tensor_copy(zT[0:GLA_RANK, :, :], ps[0:GLA_RANK, 2:4, 0:SEQ]))
        w(pe, V.now())
        for d in range(2):
            for h in range(GLA_HEADS):
                i_ = pe.matmul(ps[:, 4 + 2 * d + h // 2, (h % 2) * SEQ:(h % 2 + 1) * SEQ],
                               wg[0:GLA_RANK, d, h * P:(h + 1) * P], zT[0:GLA_RANK, d, :], start=True, stop=True)
        w(dve, T.inc(i_))
        bias = vcol("gla_bias").rearrange("p (d h) -> p d h", d=2)
        for d in range(2):
            i_ = dve.tensor_tensor(t1[:, d].rearrange("p (h n) -> p h n", h=4),
                                   ps[:, 4 + 2 * d:6 + 2 * d, :].rearrange("p b (h n) -> p (b h) n", h=2),
                                   bc(bias[:, d, :], 2, SEQ), ALU.add)
        w(act, V.inc(i_))
        A.inc(act.activation(t2, t1, ACT.Abs))
        w(act, A.now())
        A.inc(act.activation(t2, t2, ACT.Exp, scale=-1.0))
        w(act, A.now())
        A.inc(act.activation(t2, t2, ACT.Ln, bias=1.0))
        w(dve, A.now(), V.now())
        V.inc(dve.tensor_scalar(t1, t1, 0.0, 1.0 / GLA_TAU, ALU.min, ALU.mult))
        w(dve, V.now())
        V.inc(dve.scalar_tensor_tensor(la, t2, -1.0 / GLA_TAU, t1, ALU.mult, ALU.add))
        keepm = t1[:, 0, :]
        w(dve, V.now())
        V.inc(dve.memset(keepm, 1.0))
        w(dve, V.now())
        V.inc(dve.memset(keepm.rearrange("p (n c) -> p n c", c=CHUNK)[:, :, 0:1], 0.0))
        w(dve, V.now())
        V.inc(dve.tensor_tensor_scan(t2[:, 0, :], keepm, la[:, 0, :], 0.0, ALU.mult, ALU.add))
        V.inc(dve.tensor_tensor_scan(t2[:, 1, ::-1], keepm, la[:, 1, ::-1], 0.0, ALU.mult, ALU.add))
        w(dve, V.now())
        NB = GLA_HEADS * NCH
        e1, e2 = la, c(2, GLA_HEADS * SEQ)
        e3 = t1
        dec = c(2, NB)
        b4 = t2.rearrange("p d (n c) -> p d n c", c=CHUNK)
        e34 = e3.rearrange("p d (n c) -> p d n c", c=CHUNK)
        last = [b4[:, 0, :, CHUNK - 1], b4[:, 1, :, 0]]
        for d in range(2):
            i_ = dve.tensor_tensor(e34[:, d], bc(last[d], 2, CHUNK), b4[:, d], ALU.subtract)
        V.inc(i_)
        w(act, V.now())
        for d in range(2):
            act.activation(dec[:, d, :], last[d], ACT.Exp)
        act.activation(e1, t2, ACT.Exp)
        act.activation(e2, t2, ACT.Exp, scale=-1.0)
        A.inc(act.activation(e3, e3, ACT.Exp))

        o = c(TT, VW)
        qd, kd, ke = c(2, SEQ), c(2, SEQ), c(2, SEQ)
        kt = [c(2, TT, P) for _ in range(2)]
        AT = c(TT, P)
        S = c(2, NCH, GLA_DV)
        settle(dve, act, pe)
        V.inc(dve.memset(AT, 0.0))
        for q in range(2):
            V.inc(dve.memset(kt[q][64 - 64 * q:128 - 64 * q], 0.0))
        w(dve, V.now())
        mf, mb = const("gla_f").bitcast(I32), const("gla_b").bitcast(I32)
        with loop(GLA_HEADS, 0, pe=4 + TT, act=1, dve=2 + 2 + 2 * (NCH - 1) + TT) as h:
            hs = bass.ds(h * SEQ, SEQ)
            hv = bass.ds(h * GLA_DV, GLA_DV)
            w(dve, T.now(), A.now(), V.now())
            for d in range(2):
                e = [x[:, d, hs] for x in (e1, e2, e3)]
                qh, kh = (x[:, bass.ds(h, 1), :].rearrange("p a n -> p (a n)") for x in (qT, kT_))
                dve.tensor_tensor(qd[:, d, :], qh, e[0], ALU.mult)
                dve.tensor_tensor(kd[:, d, :], kh, e[1], ALU.mult)
                i_ = dve.tensor_tensor(ke[:, d, :], kh, e[2], ALU.mult)
                V.inc(i_)
            w(pe, V.now(), A.now())
            for d in range(2):
                for t in range(TT):
                    i_ = pe.transpose(ps[:, 0, (2 * d + t) * P:(2 * d + t + 1) * P], ke[:, d, t * P:(t + 1) * P], ident)
            w(act, T.inc(i_))
            for q in range(2):
                rr = slice(64 * q, 64 * q + 64)
                i_ = act.activation(kt[q][rr].rearrange("p a b c -> p (a b c)"), ps[rr, 0, :], ACT.Copy)
            A.inc(i_)
            for d in range(2):
                for t in range(TT):
                    i_ = pe.matmul(ps[:, 1, (2 * d + t) * P:(2 * d + t + 1) * P], kd[:, d, t * P:(t + 1) * P],
                                   qd[:, d, t * P:(t + 1) * P], start=True, stop=True)
            m = T.inc(i_)
            for d, mk in ((0, mf), (1, mb)):
                w_apart(dve, m, V.now())
                for t in range(TT):
                    i_ = dve.copy_predicated(AT[:, t, :], mk, ps[:, 1, (2 * d + t) * P:(2 * d + t + 1) * P])
                V.inc(i_)
            w(pe, A.now())
            kv = {}
            for d in range(2):
                for j in range(NCH - 1):
                    n = j if d == 0 else NCH - 1 - j
                    slot = ps[:, 2 + d * 2 + j // 2, (j % 2) * SEQ:(j % 2 + 1) * SEQ]
                    kv[d, j] = slot
                    i_ = pe.matmul(slot, kt[n % 2][:, d, n // 2, :], v[:, n // 2, hv], start=True, stop=True)
                w(dve, T.inc(i_))
                for j in range(NCH - 1):
                    n = j if d == 0 else NCH - 1 - j
                    to = n + 1 if d == 0 else n - 1
                    if j == 0:
                        i_ = dve.tensor_copy(S[:, d, to, :], kv[d, j])
                    else:
                        w(dve, V.now())
                        i_ = dve.scalar_tensor_tensor(S[:, d, to, :], S[:, d, n, :], dec[:, d, bass.ds(h * NCH + n, 1)],
                                                      kv[d, j], ALU.mult, ALU.add)
                    V.inc(i_)
            w(pe, V.now())
            for t in range(TT):
                po = ps[:, 6 + t, 0:GLA_DV]
                pe.matmul(po, AT[:, t, :], v[:, t, hv], start=True, stop=False)
                for q in range(2):
                    n = 2 * t + q
                    rows, cs = slice(64 * q, 64 * q + 64), slice(n * CHUNK, (n + 1) * CHUNK)
                    dirs = [d for d in range(2) if not (d == 0 and n == 0) and not (d == 1 and n == NCH - 1)]
                    for d in dirs:
                        i_ = pe.matmul(ps[rows, 6 + t, 0:GLA_DV], qd[:, d, cs], S[:, d, n, :], start=False,
                                       stop=(d == dirs[-1]))
                w(dve, T.inc(i_))
                V.inc(dve.tensor_copy(o[:, t, hv], po))
        settle(act, dve, pe)
        sq, st = e1.rearrange("p a b -> p (a b)"), dec.rearrange("p a b -> p (a b)")
        A.inc(act.activation(sq, o.rearrange("p a b -> p (a b)"), ACT.Square, scale=GLA_DV ** -0.5))
        w(dve, A.now())
        nh = TT * GLA_HEADS
        V.inc(dve.tensor_reduce(st[:, 0:nh], sq.rearrange("p (n d) -> p n d", d=GLA_DV), AX.X, ALU.add))
        w(act, V.now())
        w(dve, rsqrt(st[:, 0:nh], st[:, 0:nh]), L.now())
        o3 = o.rearrange("p a (n d) -> p (a n) d", d=GLA_DV)
        V.inc(dve.tensor_tensor(o3, o3, bc(st[:, 0:nh], 2, GLA_DV), ALU.mult))
        w(dve, V.now())
        V.inc(dve.tensor_tensor(o, o, bc(gain, 1, TT), ALU.mult))
        w(dve, V.now())
        V.inc(dve.tensor_tensor(o, o, r, ALU.mult))
        settle()
        to_split(lambda t, k: o[:, t, k * P:(k + 1) * P], 0, e2.rearrange("p a (b n) -> p (a b) n", n=512)[:, 0:2, :])
        add_product(w_out, nxt)

    def modulation(nxt):
        w_mod = ins["w_mod_2"][0]
        settle()
        c = Carve()
        bias, sil, wide_c, rows = c(6, D), c(2, KT), c(KT, SEQ), c(2, CW)
        load_row(bias.rearrange("p a b -> p (a b)"), "b_mod")
        w(act, V.now())
        act.activation(sil[:, 0, :], vcol("c"), ACT.Silu)
        A.inc(act.activation(sil[:, 1, :], vcol("c_ctx"), ACT.Silu))
        w(dve, A.now())
        dve.tensor_copy(wide_c[:, :, 0:192], bc(sil[:, 0, :], 2, 192))
        V.inc(dve.tensor_copy(wide_c[:, :, 192:256], bc(sil[:, 1, :], 2, 64)))
        w(act, V.now())
        A.inc(act.activation(xs[:, 0, :, :], wide_c, ACT.Copy))
        w(dve, A.now(), L.now())
        V.inc(dve.tensor_tensor(xs[:, 1, :, :], wide_c, xs[:, 0, :, :].bitcast(F32), ALU.subtract))
        w(pe, V.now())
        ends = [None, None]
        for j in range(12):
            which, n = j // 2, j % 2
            b = j % 2
            w(pe, ends[b])
            m = chunk_tok((b,), (1,) if which < 2 else (0,))
            request(cols(w_mod, (j + 1) * CW) if j < 11 else nxt)
            brow = bias[:, which, n * CW:(n + 1) * CW]
            w(dve, m, V.now(), T.now())
            if which % 3 == 2:
                V.inc(dve.tensor_tensor(grow[:, which // 3, n * CW:(n + 1) * CW], ps[:, b, :], brow, ALU.add))
                ends[b] = V.now()
                continue
            V.inc(dve.tensor_tensor(rows[:, b, :], ps[:, b, :], brow, ALU.add))
            ends[b] = V.now()
            w(pe, V.now())
            for q in range(4):
                i_ = pe.transpose(ps[:, 2 + b, q * P:(q + 1) * P], rows[:, b, q * P:(q + 1) * P], ident)
            w(dve, T.inc(i_))
            v_ = (0, 1, None, 2, 3)[which]
            colv = ps[:, 2 + b, :].rearrange("p (q n) -> p q n", q=4)[:, :, 0:P:64]
            V.inc(dve.tensor_scalar(modcol[:, v_, 4 * n:4 * n + 4, :], colv, 1.0 if v_ % 2 else 0.0, None, ALU.add))
            ends[b] = V.now()

    def attention_2(akv_next, o):
        w_in = ins["w_in_2"][0]
        QW = 3616
        c = Carve(end=arena_n - 2048)
        k, v, q = c(NT2, KV2 * HD2), c(NT2, KV2 * HD2), c(TT, NH2 * HD2)
        tk, tq = c(2, NT2, HD2), c(2, TT, HD2)
        gk, gq = c(HD2), c(HD2)
        sq = c(1024)
        bufs = (sq, c(16), c(1024), c(1024), sq)
        kT = c(KV2, NT2 * P)
        settle(act)
        load_row(gk, "k_norm")
        load_row(gq, "q_norm")
        cosv = const("cos_2").rearrange("p (t d) -> p t d", t=TT)
        sinv = const("sin_2").rearrange("p (t d) -> p t d", t=TT)
        settle(pool)
        w(pool, L.now())
        for tab, gain in ((tk, gk), (tq, gq)):
            for t in range(TT):
                pool.tensor_tensor(tab[:, 0, t, :], cosv[:, t, :], gain, ALU.mult)
                for s_ in range(4):
                    o_, i_ = slice(s_ * 32, s_ * 32 + 32), slice((s_ ^ 1) * 32, (s_ ^ 1) * 32 + 32)
                    pool.tensor_tensor(tab[:, 1, t, o_], sinv[:, t, o_], gain[:, i_], ALU.mult)
        for t in range(TT, NT2):
            pool.tensor_copy(tk[:, 0, t, :], gk)
        G.inc(pool.memset(tk[:, 1, TT:NT2, :], 0.0))
        m = chunk_tok((0, 1, 2, 3), (0, 1, 2, 3))
        request(cols(w_in, QW))
        w(act, m)
        w(dve, m, G.now())
        head_norm_rope(ps[:, 0:4, 0:256], KV2, HD2, NT2, tk[:, 0], tk[:, 1],
                       lambda t: k[:, t, :].rearrange("p (h d) -> p h d", d=HD2), bufs)
        w(act, V.now())
        A.inc(act.activation(v, ps[:, 0:4, 256:512], ACT.Copy))
        for n in range(2):
            b0 = 4 + 2 * n
            m = chunk_tok((b0, b0 + 1))
            request(cols(w_in, QW + CW) if n == 0 else akv_next)
            w(act, m)
            w(dve, m)
            head_norm_rope(ps[:, b0:b0 + 2, :], 4, HD2, TT, tq[:, 0], tq[:, 1],
                           lambda t: q[:, t, n * CW:(n + 1) * CW].rearrange("p (h d) -> p h d", d=HD2), bufs)
        settle(pe)
        for g in range(KV2):
            for t in range(NT2):
                i_ = pe.transpose(ps[:, g, t * P:(t + 1) * P], k[:, t, g * HD2:(g + 1) * HD2], ident)
        w(dve, T.inc(i_))
        V.inc(dve.tensor_copy(kT, ps[:, 0:2, :]))
        c.at = 0 + NT2 * 512 + 2048
        stg, qT = c(TT, CW), c(TT, CW)
        E, ET = c(2, CW), c(2, CW)
        mx, ngm, l, rl = (c(8) for _ in range(4))
        assert c.at <= NT2 * 512 + 2048 + 1536 + 256 + 1024 * 3 + 16
        settle(act, dve)
        scale = HD2 ** -0.5
        with loop(KV2, 0, pe=1 + 8 * 3, act=1 + 8 * 1, dve=1 + 8 * 5) as g:
            gcols = bass.ds(g * CW, CW)
            w(act, T.now())
            A.inc(act.activation(stg, q[:, :, gcols], ACT.Copy))
            w(pe, A.now(), V.now())
            for t in range(TT):
                for h in range(GROUP2):
                    i_ = pe.transpose(ps[:, t, h * P:(h + 1) * P], stg[:, t, h * P:(h + 1) * P], ident)
            w(dve, T.inc(i_))
            V.inc(dve.tensor_copy(qT, ps[:, 0:2, :]))
            state = {}

            def scores(u):
                h, t, par = u // 2, u % 2, u % 2
                w(pe, V.now() if u < 2 else state[u - 2]["exp"])
                i_ = pe.matmul(ps[:, 2 + par, :], qT[:, t, h * P:(h + 1) * P],
                               kT[:, bass.ds(g, 1), :].rearrange("p a n -> p (a n)"), start=True, stop=True)
                w(dve, T.inc(i_), A.now())
                V.inc(dve.tensor_reduce(mx[:, u:u + 1], ps[:, 2 + par, :], AX.X, ALU.max))
                w(dve, V.now())
                V.inc(dve.tensor_scalar(ngm[:, u:u + 1], mx[:, u:u + 1], -scale, None, ALU.mult))
                w(act, V.now(), T.now())
                state[u] = {"exp": A.inc(act.activation(E[:, par, :], ps[:, 2 + par, :], ACT.Exp, bias=ngm[:, u:u + 1],
                                                        scale=scale, accum_out=l[:, u:u + 1]))}

            def values(u):
                h, t, par = u // 2, u % 2, u % 2
                w(pe, state[u]["exp"], V.now() if u < 2 else state[u - 2]["out"])
                for j in range(NT2):
                    i_ = pe.transpose(ps[:, 4 + par, j * P:(j + 1) * P], E[:, par, j * P:(j + 1) * P], ident)
                w(dve, T.inc(i_), state[u]["exp"], V.now())
                V.inc(dve.tensor_copy(ET[:, par, :], ps[:, 4 + par, :]))
                m_ = V.now()
                V.inc(dve.reciprocal(rl[:, u:u + 1], l[:, u:u + 1]))
                w(pe, m_)
                for j in range(NT2):
                    i_ = pe.matmul(ps[:, 6 + par, 0:P], ET[:, par, j * P:(j + 1) * P], v[:, j, bass.ds(g * HD2, HD2)],
                                   start=(j == 0), stop=(j == NT2 - 1))
                w(dve, T.inc(i_), V.now())
                state[u]["out"] = V.inc(dve.tensor_scalar(o[:, t, bass.ds(g * CW + h * P, P)], ps[:, 6 + par, 0:P],
                                                          rl[:, u:u + 1], None, ALU.mult))

            for u in range(8):
                scores(u)
                if u:
                    values(u - 1)
            values(7)

    def gdn_inputs(qkv, nxt):
        w_in, c0 = ins["w_in_2"][0], 512
        settle()
        c = Carve(start=24 * 512, end=arena_n - 2048)
        y, z = c(4, 2, SEQ), c(4, 2, SEQ)
        taps_all = vcol("gdn_conv").rearrange("p (b t) -> p b t", t=3)

        def one(ci, par, after, ends):
            b0 = 4 * par
            w(pe, *ends)
            m = chunk_feat(range(b0, b0 + 4), both=True)
            request(after)
            taps = ccur[:, par, 0:12].rearrange("p (b t) -> p b t", t=3)
            w(pool, V.now(), A.now())
            G.inc(pool.tensor_copy(taps, taps_all[:, bass.ds(ci * 4, 4), :]))
            xq = ps[:, b0:b0 + 4, :].rearrange("p b (s n) -> p b s n", s=2)
            w(act, m, G.now(), V.now(), A.now())
            for q in range(4):
                i_ = act.activation(y[:, q], xq[:, q], ACT.Copy, scale=taps[:, q, 1:2])
            w(dve, A.inc(i_), V.now())
            for q in range(4):
                dve.scalar_tensor_tensor(z[:, q, :, 1:SEQ], xq[:, q, :, 0:SEQ - 1], taps[:, q, 0:1], y[:, q, :, 1:SEQ],
                                         ALU.mult, ALU.add)
            V.inc(dve.tensor_copy(z[:, :, :, 0:1], y[:, :, :, 0:1]))
            w(dve, V.now())
            for q in range(4):
                dve.scalar_tensor_tensor(y[:, q, :, 0:SEQ - 1], xq[:, q, :, 1:SEQ], taps[:, q, 2:3],
                                         z[:, q, :, 0:SEQ - 1], ALU.mult, ALU.add)
            V.inc(dve.tensor_copy(y[:, :, :, SEQ - 1:SEQ], z[:, :, :, SEQ - 1:SEQ]))
            w(act, V.now())
            A.inc(act.activation(qkv[:, bass.ds(ci * 4, 4), :], y.rearrange("p b s n -> p b (s n)"), ACT.Silu))

        with loop(2, 2, act=4, dve=4, pool=2) as i:
            for par in range(2):
                ends = (V.back(2), A.back(2))
                one(i * 2 + par, par, cols(w_in, c0 + (i * 2 + par + 1) * CW), ends)
        for ci in (4, 5):
            one(ci, ci % 2, cols(w_in, c0 + (ci + 1) * CW) if ci == 4 else nxt, (V.back(2), A.back(2)))

    def gdn_scalars(qkv, sc, c):
        wz, zf = c(KT, 32), c(512)
        a_log, dt = c(16), c(16)
        la, t1, t2 = c(NT2, 16), c(NT2, 16), c(NT2, 16)
        sq, rn = c(4, CW), c(NT2, 2, GDN_HEADS)
        settle(act)
        L.inc(act.dma_start(wz, ins["w_in_2"][0][:, 3584:3616].rearrange("(k p) n -> p k n", p=P)), 16)
        load_row(a_log, "a_log")
        load_row(dt, "dt_bias")
        settle(pe, dve)
        w(pe, L.now())
        w(dve, L.now())
        for k in range(KT):
            pe.matmul(ps[0:32, 0, :], wz[:, k, :], xs[:, 0:4:2, k, :].bitcast(F32), start=(k == 0), stop=False)
            i_ = pe.matmul(ps[0:32, 0, :], wz[:, k, :], xs[:, 1:4:2, k, :].bitcast(F32), start=False, stop=(k == KT - 1))
        w(dve, T.inc(i_))
        V.inc(dve.tensor_copy(zf[0:32, :], ps[0:32, 0, :]))
        lens = ps[:, 7, 0:64].rearrange("p (t a h) -> p t a h", t=NT2, a=2)
        read = T.now()
        for g in range(4):
            w(act, read)
            sq_ok = A.inc(act.activation(sq, qkv[:, 4 * g:4 * g + 4, :], ACT.Square))
            w(pe, sq_ok)
            for j in range(4):
                for t in range(NT2):
                    i_ = pe.matmul(lens[:, t, g // 2, 4 * (g % 2) + j:4 * (g % 2) + j + 1], sq[:, j, t * P:(t + 1) * P],
                                   const("ones")[:, 0:1], start=True, stop=True)
            read = T.inc(i_)
        w(act, read)
        A.inc(act.activation(rn, lens, ACT.Sqrt, bias=eps_col))
        w(dve, A.now())
        rn_ok = V.inc(dve.reciprocal(rn, rn))
        w(pe, rn_ok)
        for t in range(NT2):
            i_ = pe.transpose(ps[:, 1, 32 * t:32 * t + 32], zf[0:32, t * P:(t + 1) * P], ident[0:32, 0:32])
        m = T.inc(i_)
        z = ps[:, 1, 0:128].rearrange("p (t n) -> p t n", t=NT2)
        kinds = sc.rearrange("p k t d h -> p k t (d h)")
        w(act, m)
        A.inc(act.activation(kinds[:, 9], z[:, :, 0:16], ACT.Sigmoid))
        w(dve, A.now())
        V.inc(dve.tensor_tensor(t1, z[:, :, 16:32], bc(dt, 1, NT2), ALU.add))
        w(act, V.now())
        A.inc(act.activation(t2, t1, ACT.Abs))
        w(act, A.now())
        A.inc(act.activation(t2, t2, ACT.Exp, scale=-1.0))
        act.activation(a_log, a_log, ACT.Exp)
        w(act, A.now())
        A.inc(act.activation(t2, t2, ACT.Ln, bias=1.0))
        w(dve, A.now())
        V.inc(dve.scalar_tensor_tensor(t1, t1, 0.0, t2, ALU.max, ALU.add))
        w(dve, V.now())
        V.inc(dve.scalar_tensor_tensor(la, t1, -1.0, bc(a_log, 1, NT2), ALU.mult, ALU.mult))
        w(pe, V.now())
        flat = la.rearrange("p t n -> p (t n)")
        for j, name in enumerate(("cum_f", "cum_b", "ones_bd", "even", "odd")):
            i_ = pe.matmul(ps[:, 2 + j, 0:64], const(name), flat, start=True, stop=True)
        m = T.inc(i_)
        w(dve, m)
        res = [ps[:, 2 + j, 0:64].rearrange("p (t d h) -> p t d h", t=NT2, d=2) for j in range(5)]
        for d in range(2):
            dve.tensor_copy(sc[:, 0, :, d, :], res[d][:, :, d, :])
            dve.tensor_copy(sc[:, 7, :, d, :], rn[:, :, 1, :])
            i_ = dve.tensor_scalar(sc[:, 8, :, d, :], rn[:, :, 0, :], GDN_D ** -0.5, None, ALU.mult)
        V.inc(i_)
        w(dve, V.now())
        V.inc(dve.tensor_tensor(t1, ps[:, 4, 0:64].rearrange("p (t n) -> p t n", t=NT2), kinds[:, 0], ALU.subtract))
        w(act, V.now())
        act.activation(kinds[:, 2], kinds[:, 0], ACT.Exp)
        act.activation(kinds[:, 3], t1, ACT.Exp)
        for q in range(2):
            i_ = act.activation(kinds[:, 5 + q], ps[:, 5 + q, 0:64].rearrange("p (t n) -> p t n", t=NT2), ACT.Exp)
        w(dve, A.inc(i_))
        V.inc(dve.tensor_tensor(kinds[:, 1], kinds[:, 9], kinds[:, 7], ALU.mult))
        w(dve, V.now())
        dve.tensor_tensor(kinds[:, 3], kinds[:, 3], kinds[:, 7], ALU.mult)
        V.inc(dve.scalar_tensor_tensor(kinds[:, 4], kinds[:, 1], -1.0, kinds[:, 2], ALU.mult, ALU.mult))
        w(dve, V.now())
        V.inc(dve.tensor_tensor(kinds[:, 2], kinds[:, 2], kinds[:, 8], ALU.mult))

    def gdn_heads(qkv, sc, o, lo, hi):
        NM = NT2 * 2
        hn = lo(NK, NT2 * 2)
        PTn, NTm, XT, X, Y = lo(2, TT, P), lo(2, NT2, P), lo(2, NT2, P), lo(2, NT2, P), lo(2, NT2, P)
        BT = [lo(2, NT2, P) for _ in range(2)]
        Ig, Ib = BT
        decT = Y
        hc = lo(NK, NT2 * 2)
        R, PT, PD, S, qst, dl = hi(2, NT2, P), hi(2, TT, P), hi(TT, P), hi(2, 4, P), hi(SEQ), lo(2, NT2, P)
        kn = hi(CW)
        Sc = hi(2, 2, P)
        half = [raw[:, q].rearrange("p a b -> p (a b)") for q in range(2)]
        four = "p (d t n) -> p d t n"
        kd = [half[q][:, 0:NM * P].rearrange(four, d=2, t=NT2) for q in range(2)]
        XTr = half[0][:, NM * P:].rearrange(four, d=2, t=NT2)
        kst, vst = half[1][:, NM * P:NM * P + CW], half[1][:, NM * P + CW:]
        rowed = lambda a: a.rearrange("p k (t d) -> p k d t", d=2)
        chunks = {0: [(1, 0, 0), (1, 0, 1), (1, 1, 0), (1, 1, 1), (0, 0, 0), (0, 0, 1), (0, 1, 0), (0, 1, 1)]}
        chunks[1] = chunks[0][3::-1] + chunks[0][:3:-1]
        settle()
        for e in (act, dve):
            w(e, hi_ok[0].now(), hi_ok[1].now(), lo_ok[0].now(), lo_ok[1].now())
        negs = (const("neg_f"), const("neg_b"))
        lev = [const(f"level{b}") for b in LEVELS]
        for q in range(2):
            i_ = dve.memset(kd[q][64 - 64 * q:128 - 64 * q], 0.0)
        V.inc(i_)
        hd = rowed(hn)
        hr = rowed(hc)

        def block(h, j):
            return qkv[:, bass.ds(h + 8 * j, 1) if not isinstance(h, int) else slice(h + 8 * j, h + 8 * j + 1), :].rearrange("p a n -> p (a n)")

        def column(h):
            c_ = bass.ds(h, 1) if not isinstance(h, int) else slice(h, h + 1)
            return sc.rearrange("p k t d h -> p k (t d) h")[:, :, :, c_].rearrange("p k n a -> p k (n a)")

        def prepare(h, ready):
            w(dve, *ready["hn free"])
            v0 = V.inc(dve.tensor_copy(hn, column(h)))
            w_apart(pool, v0, ready["BT free"])
            w_apart(act, v0, ready["BT free"])
            mk = A.inc(act.activation(kn, block(h, 1), ACT.Copy))
            for d in range(2):
                for t in range(NT2):
                    if t < 2:
                        ig = pool.tensor_scalar(Ig[:, d, t, :], ident, hd[:, 0, d, t:t + 1], None, ALU.mult)
                    else:
                        ia = act.activation(Ig[:, d, t, :], ident, ACT.Copy, scale=hd[:, 0, d, t:t + 1])
            mg = (G.inc(ig), A.inc(ia))
            for d in range(2):
                for t in range(NT2):
                    if t < 1:
                        ig = pool.tensor_scalar(Ib[:, d, t, :], ident, hd[:, 1, d, t:t + 1], None, ALU.mult)
                    else:
                        ia = act.activation(Ib[:, d, t, :], ident, ACT.Copy, scale=hd[:, 1, d, t:t + 1])
            mi = (G.inc(ig), A.inc(ia))
            kh, qh = kn, block(h, 0)
            w(pe, ready["banks free"], mk)
            for t in range(NT2):
                pe.matmul(ps[:, 4, t * P:(t + 1) * P], kh[:, t * P:(t + 1) * P], kh[:, t * P:(t + 1) * P], start=True, stop=True)
            for t in range(TT):
                i_ = pe.matmul(ps[:, 5, t * P:(t + 1) * P], kh[:, t * P:(t + 1) * P], qh[:, t * P:(t + 1) * P], start=True, stop=True)
            mk = T.inc(i_)
            yield
            yield
            w(pe, *mg)
            for d in range(2):
                i_ = pe.matmul(ps[:, d, :], const("ones_bd"), Ig[:, d].rearrange("p t n -> p (t n)"), start=True, stop=True)
            mr = T.inc(i_)
            yield
            w(pe, *mi)
            for d in range(2):
                i_ = pe.matmul(ps[:, 2 + d, :], const("ones_bd"), Ib[:, d].rearrange("p t n -> p (t n)"), start=True, stop=True)
            mb = T.inc(i_)
            yield
            w(dve, mr)
            for d in range(2):
                for t in range(NT2):
                    i_ = dve.scalar_tensor_tensor(decT[:, d, t, :], ps[:, d, t * P:(t + 1) * P], hd[:, 0, d, t:t + 1],
                                                  negs[d], ALU.subtract, ALU.add)
                md = V.inc(i_)
                w(act, md)
                me = A.inc(act.activation(decT[:, d], decT[:, d], ACT.Exp))
                yield
            for d in range(2):
                w(dve, me, mk)
                for t in range(NT2):
                    kq = ps[:, 5, t * P:(t + 1) * P]
                    if t < TT:
                        dve.scalar_tensor_tensor(PTn[:, d, t], kq, hd[:, 7, d, t:t + 1], decT[:, d, t], ALU.mult, ALU.mult)
                    i_ = dve.scalar_tensor_tensor(NTm[:, d, t], ps[:, 4, t * P:(t + 1) * P], hd[:, 7, d, t:t + 1],
                                                  decT[:, d, t], ALU.mult, ALU.mult)
                mn = ready["mn"] = V.inc(i_)
                yield
            w(dve, mn, mb)
            for d in range(2):
                i_ = dve.tensor_tensor(NTm[:, d], NTm[:, d], ps[:, 2 + d, :].rearrange("p (t n) -> p t n", t=NT2), ALU.mult)
            mn = V.inc(i_)
            yield
            bt_ok = {}

            def level_part(j, free):
                w(pool, mn, free)
                bt_ok[j] = G.inc(pool.tensor_tensor(BT[(j - 1) % 2], NTm, lev0_bc(lev[j]), ALU.mult))

            w(dve, mn, mb)
            v1 = V.inc(dve.tensor_tensor(XT, NTm, lev0_bc(lev[0]), ALU.mult))
            level_part(1, mb)
            w(dve, v1)
            v1 = V.inc(dve.tensor_tensor(XT, lev0_bc(ident), XT, ALU.subtract))
            level_part(2, mb)
            yield
            xt_ok = [v1, v1]
            for j in range(1, len(LEVELS)):
                bt = BT[(j - 1) % 2]
                x_ok, y_ok = [None, None], [None, None]
                for d in range(2):
                    w(pe, xt_ok[d])
                    for t in range(NT2):
                        i_ = pe.transpose(ps[:, d, t * P:(t + 1) * P], XT[:, d, t, :], ident)
                    w(act, T.inc(i_))
                    x_ok[d] = A.inc(act.activation(X[:, d].rearrange("p t n -> p (t n)"), ps[:, d, :], ACT.Copy))
                    yield
                for d in range(2):
                    w(pe, x_ok[d], bt_ok[j])
                    for t in range(NT2):
                        i_ = pe.matmul(ps[:, 2 + d, t * P:(t + 1) * P], bt[:, d, t, :], X[:, d, t, :], start=True, stop=True)
                    mt = T.inc(i_)
                    w(act, mt)
                    y_ok[d] = A.inc(act.activation(Y[:, d].rearrange("p t n -> p (t n)"), ps[:, 2 + d, :], ACT.Copy))
                    yield
                if j + 2 < len(LEVELS):
                    level_part(j + 2, mt)
                if j + 1 == len(LEVELS):
                    w(dve, ready["rec"])
                for d in range(2):
                    w(pe, y_ok[d])
                    for t in range(NT2):
                        i_ = pe.matmul(ps[:, 4 + d, t * P:(t + 1) * P], Y[:, d, t, :], XT[:, d, t, :], start=True, stop=True)
                    w(dve, T.inc(i_))
                    to = XT if j + 1 < len(LEVELS) else XTr
                    xt_ok[d] = V.inc(dve.tensor_tensor(to[:, d].rearrange("p t n -> p (t n)"), XT[:, d].rearrange("p t n -> p (t n)"),
                                                       ps[:, 4 + d, :], ALU.subtract))
                    yield
            ready["XTr"] = xt_ok[1]
            ready["BT free"] = mt
            ready["banks free"] = xt_ok[1]

        def operands(h, ready):
            w_apart(act, ready["out"])
            act.activation(kst, block(h, 1), ACT.Copy)
            act.activation(qst, block(h, 0)[:, 0:SEQ], ACT.Copy)
            ma = A.inc(act.activation(vst, block(h, 2), ACT.Copy))
            w(dve, ready["out"], ready["mn"])
            dve.tensor_copy(PT, PTn)
            mc = V.inc(dve.tensor_copy(hc, hn))
            ready["hn free"] = (mc,)
            w(pe, ma, mc)
            for t in range(NT2):
                pe.transpose(ps[:, 6, t * P:(t + 1) * P], kst[:, t * P:(t + 1) * P], ident)
                i_ = pe.transpose(ps[:, 7, t * P:(t + 1) * P], vst[:, t * P:(t + 1) * P], ident)
            mt = T.inc(i_)
            yield
            w(dve, mt, mc)
            for d in range(2):
                for q in range(2):
                    rw = slice(64 * q, 64 * q + 64)
                    dve.tensor_tensor(kd[q][rw, d], ps[rw, 6, :].rearrange("p (t n) -> p t n", t=NT2), bc(hr[rw, 3, d, :], 2, P), ALU.mult)
                i_ = dve.tensor_tensor(R[:, d], ps[:, 7, :].rearrange("p (t n) -> p t n", t=NT2), bc(hr[:, 9, d, :], 2, P), ALU.mult)
            ready["R"] = V.inc(i_)
            yield

        def state_at(d, n):
            return S[:, d, n, :] if n < 4 else Sc[:, d, n - 4, :]

        def recur(h, ready):
            s_ok = [ready["R"]] * 2
            r_ok = [ready["R"]] * 2
            slot = [None, None]
            d_ok = [None, None]
            for st in range(8):
                where = []
                for d in range(2):
                    seq, tl, q = chunks[d][st]
                    t = 2 * seq + tl
                    nx = (5, 4, 5, None, None, None, None, None)[st]
                    if 3 <= st < 7:
                        nx = 2 * chunks[d][st + 1][1] + chunks[d][st + 1][2]
                    where.append((t, q, slice(64 * q, 64 * q + 64), nx))
                if st:
                    for d in range(2):
                        t, q, rw, nx = where[d]
                        w(pe, s_ok[d])
                        i_ = pe.matmul(ps[:, 6 + d, 0:P], kst[:, t * P:(t + 1) * P], state_at(d, slot[d]), start=True, stop=True)
                        w(dve, T.inc(i_), r_ok[d])
                        r_ok[d] = V.inc(dve.scalar_tensor_tensor(R[rw, d, t, :], ps[rw, 6 + d, 0:P], hr[rw, 4, d, t:t + 1],
                                                                 R[rw, d, t, :], ALU.mult, ALU.add))
                    yield
                for d in range(2):
                    t, q, rw, nx = where[d]
                    w(pe, r_ok[d], ready["XTr"])
                    i_ = pe.matmul(ps[:, 6 + d, P:2 * P], XTr[:, d, t, :], R[:, d, t, :], start=True, stop=True)
                    w(act, T.inc(i_))
                    d_ok[d] = A.inc(act.activation(dl[:, d, t, :], ps[:, 6 + d, P:2 * P], ACT.Copy))
                yield
                if st < 7:
                    for d in range(2):
                        t, q, rw, nx = where[d]
                        w(pe, d_ok[d])
                        i_ = pe.matmul(ps[:, 6 + d, 2 * P:3 * P], kd[q][:, d, t, :], dl[:, d, t, :], start=True, stop=True)
                        w(dve, T.inc(i_), s_ok[d])
                        if st == 0:
                            s_ok[d] = V.inc(dve.tensor_copy(state_at(d, nx), ps[:, 6 + d, 2 * P:3 * P]))
                        else:
                            s_ok[d] = V.inc(dve.scalar_tensor_tensor(state_at(d, nx), state_at(d, slot[d]), hr[:, 5 + q, d, t:t + 1],
                                                                     ps[:, 6 + d, 2 * P:3 * P], ALU.mult, ALU.add))
                        slot[d] = nx
                    yield
            w(pe, d_ok[0], d_ok[1], s_ok[0], s_ok[1])
            for t in range(TT):
                for d in range(2):
                    i_ = pe.matmul(ps[:, 6, t * P:(t + 1) * P], PT[:, d, t, :], dl[:, d, t, :], start=(d == 0), stop=(d == 1))
            w(act, T.inc(i_))
            for t in range(TT):
                i_ = act.activation(PD[:, t], ps[:, 6, t * P:(t + 1) * P], ACT.Copy, scale=hr[:, 8, 0, t:t + 1])
            ma = A.inc(i_)
            yield
            for d in range(2):
                for t in range(TT):
                    for q in range(2):
                        i_ = pe.matmul(ps[64 * q:64 * q + 64, 7, (2 * d + t) * P:(2 * d + t + 1) * P],
                                       qst[:, (2 * t + q) * CHUNK:(2 * t + q + 1) * CHUNK], S[:, d, 2 * t + q, :], start=True, stop=True)
            mt = T.inc(i_)
            yield
            w(dve, mt, ma)
            for d in range(2):
                if d:
                    w(dve, md)
                for t in range(TT):
                    c_ = bass.ds(h * P, P) if not isinstance(h, int) else slice(h * P, h * P + P)
                    dst = PD[:, t, :] if d == 0 else o[:, t, c_]
                    i_ = dve.scalar_tensor_tensor(dst, ps[:, 7, (2 * d + t) * P:(2 * d + t + 1) * P], hr[:, 2, d, t:t + 1],
                                                  PD[:, t, :], ALU.mult, ALU.add)
                md = V.inc(i_)
            ready["out"] = md
            ready["rec"] = md
            yield

        def braid(a, b):
            a, b = iter(a), iter(b)
            while any([next(x, "end") is None for x in (a, b)]):
                pass

        def after(first, second):
            yield from first
            yield from second

        def done():
            return {"hn free": (V.now(), A.now(), G.now()), "BT free": T.now(), "banks free": V.now(), "rec": V.now(),
                    "out": V.now(), "mn": V.now(), "R": V.now(), "XTr": V.now()}

        ready = done()
        for _ in after(prepare(0, ready), operands(0, ready)):
            pass
        with loop(GDN_HEADS - 1, 0, **GDN_PER) as h:
            ready = done()
            braid(prepare(h + 1, ready), after(recur(h, ready), operands(h + 1, ready)))
        for _ in recur(GDN_HEADS - 1, done()):
            pass
        settle(sp)

    def lev0_bc(m):
        return bc(bc(m, 1, NT2), 1, 2)

    def layer_c(nxt):
        w_in = ins["w_in_2"][0]
        settle()
        ctx = Carve(start=8192)(TT, D)
        w(act, V.now())
        L.inc(act.dma_start(ctx, ins["ctx_2"][0].rearrange("(t p) d -> p t d", p=P)), 16)
        w(act, L.now())
        w(dve, L.now())
        norm_split(ctx, 1, Carve(), modcol[:, 1, :, 1], modcol[:, 0, :, 1])
        norm_split(resid, 0, Carve(), modcol[:, 1, :, 0], modcol[:, 0, :, 0])
        attn = Carve(start=arena_n - 2048)(TT, D)
        attention_2(cols(w_in, 512), attn)
        Z0 = 4640
        c = Carve()
        qkv = c(24, CW)
        gdn_inputs(qkv, cols(w_in, Z0))
        gdn = c(TT, D)
        sc = c(NK, NT2, 2, GDN_HEADS)
        gdn_scalars(qkv, sc, Carve(start=c.at, end=arena_n - 2048))
        gdn_heads(qkv, sc, gdn, Carve(c.at, arena_n - 2048), Carve(-XS // 2, 0))
        settle()
        c = Carve()
        z, gt = c(TT, D), c(TT, 2 * D)
        y = c(TT, D)
        sq = c(TT * D)
        st = c(16)
        gain = c(GDN_D)
        stage = c(2, 512)
        assert c.at <= 24 * CW
        load_row(gain, "gdn_norm")
        reads = [A.now()] * 4
        for j in range(6):
            b0 = 2 * (j % 4)
            w(pe, reads[j - 4] if j >= 4 else None)
            m = chunk_tok((b0, b0 + 1))
            request(cols(w_in, Z0 + (j + 1) * CW) if j < 5 else cols(ins["w_pa_2"][0], 0))
            w(act, m)
            dst = z[:, :, j * CW:(j + 1) * CW] if j < 2 else gt[:, :, (j - 2) * CW:(j - 1) * CW]
            A.inc(act.activation(dst, ps[:, b0:b0 + 2, :], ACT.Silu if j < 2 else ACT.Sigmoid))
            reads.append(A.now())
        nh = TT * GDN_HEADS
        A.inc(act.activation(sq, gdn.rearrange("p t n -> p (t n)"), ACT.Square, scale=GDN_D ** -0.5))
        w(dve, A.now())
        V.inc(dve.tensor_reduce(st[:, 0:nh], sq.rearrange("p (n d) -> p n d", d=GDN_D), AX.X, ALU.add))
        w(act, V.now())
        w(dve, rsqrt(st[:, 0:nh], st[:, 0:nh]), L.now())
        o3 = gdn.rearrange("p t (h d) -> p (t h) d", d=GDN_D)
        V.inc(dve.tensor_tensor(o3, o3, bc(st[:, 0:nh], 2, GDN_D), ALU.mult))
        w(dve, V.now())
        V.inc(dve.tensor_tensor(o3, o3, bc(gain, 1, nh), ALU.mult))
        w(dve, V.now())
        V.inc(dve.tensor_tensor(gdn, gdn, z, ALU.mult))
        settle()
        to_split(lambda t, k: attn[:, t, k * P:(k + 1) * P], 0, stage)
        settle()
        to_split(lambda t, k: gdn[:, t, k * P:(k + 1) * P], 1, stage)
        after = [cols(ins["w_pa_2"][0], CW), cols(ins["w_pd_2"][0], 0), cols(ins["w_pd_2"][0], CW), cols(ins["w_out_2"][0], 0)]
        prod = sq.rearrange("p (t n) -> p t n", t=TT)
        for j in range(4):
            n, br = j % 2, j // 2
            b0 = 2 * j
            m = chunk_tok((b0, b0 + 1), (0, 1) if br == 0 else (2, 3))
            request(after[j])
            yo, g_ = y[:, :, n * CW:(n + 1) * CW], gt[:, :, j * CW:(j + 1) * CW]
            w(dve, m, V.now(), A.now())
            if br == 0:
                V.inc(dve.tensor_tensor(yo, ps[:, b0:b0 + 2, :], g_, ALU.mult))
            else:
                pr = prod[:, :, 0:CW]
                V.inc(dve.tensor_tensor(pr, ps[:, b0:b0 + 2, :], g_, ALU.mult))
                w(dve, V.now())
                V.inc(dve.tensor_tensor(yo, yo, pr, ALU.add))
        settle()
        to_split(lambda t, k: y[:, t, k * P:(k + 1) * P], 0, stage)
        add_product(ins["w_out_2"][0], nxt, gate=grow[:, 0, :], tmp=z[:, :, 0:CW])



    L.inc(act.dma_start(cst[:, :], ins["consts"]), 16)
    L.inc(act.dma_start(vec[:, :], ins["vecs"]), 16)
    L.inc(act.dma_start(resid[:, :, :], ins["x"][0].rearrange("(t p) d -> p t d", p=P)), 16)
    request(cols(ins["a_w_in"][0], 0))
    V.inc(dve.memset(unused[:, :], 0.0))
    V.inc(dve.memset(eps_col, EPS))
    w(pool, V.now())
    for e in (pe, act, dve, pool):
        w(e, L.now(), V.now())
    a_norm = vcol("attn_norm").rearrange("p (l k) -> p l k", k=KT)
    f_norm = vcol("ffn_norm").rearrange("p (l k) -> p l k", k=KT)

    def finish(src):
        settle(sp)
        stored.inc(sp.dma_start(out[0].rearrange("(t p) d -> p t d", p=P), src), 16)
        w(sp, stored.now())

    first_gu = [gate_up(ins["ffn_w_gate_up"][i], 0) for i in range(2)]
    norm_split(resid, 0, Carve(), a_norm[:, 0, :])
    layer_a(first_gu[0])
    norm_split(resid, 0, Carve(), f_norm[:, 0, :])
    ffn(ins["ffn_w_gate_up"][0], ins["ffn_w_down"][0], cols(ins["b_w_in"][0], 0))
    norm_split(resid, 0, Carve(), a_norm[:, 1, :])
    layer_b(first_gu[1])
    norm_split(resid, 0, Carve(), f_norm[:, 1, :])
    ffn(ins["ffn_w_gate_up"][1], ins["ffn_w_down"][1], cols(ins["w_mod_2"][0], 0))
    modulation(cols(ins["w_in_2"][0], 0))
    layer_c(gate_up(ins["w_up_2"][0], 0))
    norm_split(resid, 0, Carve(), modcol[:, 3, :, 0], modcol[:, 2, :, 0])
    conv = vcol("ffn_conv").rearrange("p (a t n) -> p a t n", a=2, t=4)
    ffn(ins["w_up_2"][0], ins["w_down_2"][0], None, conv, grow[:, 1, :])
    settle()
    c = Carve()
    st, sq, o, gain = c(8), c(D), c(TT, D), c(D)
    load_row(gain, "final_norm")
    rstd_of(resid, TT, D, st, sq)
    w(dve, V.now(), L.now())
    for t in range(TT):
        V.inc(dve.scalar_tensor_tensor(o[:, t, :], resid[:, t, :], st[:, t:t + 1], gain, ALU.mult, ALU.mult))
    finish(o)




def pack(parts):
    at, n = {}, 0
    for name, a in parts:
        at[name] = (n, n + a.shape[-1])
        n += a.shape[-1]
    return np.ascontiguousarray(np.concatenate([a for _, a in parts], -1)), at


def by_partition(v):
    a = np.asarray(v)
    a = a.reshape(-1, a.shape[-1] // P, P)
    return np.ascontiguousarray(a.reshape(-1, P).T)


_WEIGHTS = ["x", "a_w_in", "a_w_out", "b_w_in", "b_w_gate_f", "b_w_gate_b", "b_w_out", "ffn_w_gate_up",
            "ffn_w_down", "ctx_2", "w_mod_2", "w_in_2", "w_pa_2", "w_pd_2", "w_out_2", "w_up_2", "w_down_2"]


def kernel(**inputs):
    import concourse.bacc as bacc
    from concourse.bass_utils import run_bass_kernel_spmd

    g = {k: np.asarray(v) for k, v in inputs.items()}
    consts, const_at = pack(list(constants().items()))
    conv = np.concatenate([g["ffn_conv_w_2"][0], g["ffn_conv_b_2"]], 0)
    conv = conv.reshape(4, 2, FT, P).transpose(3, 1, 0, 2).reshape(P, -1)
    gdn_conv = g["conv_qkv_w_2"][0].reshape(3, 24, P).transpose(2, 1, 0).reshape(P, -1)
    vecs, vec_at = pack([
        ("attn_norm", by_partition(g["attn_norm"])), ("ffn_norm", by_partition(g["ffn_norm"])),
        ("gla_bias", by_partition(np.concatenate([g["b_gate_bias_f"], g["b_gate_bias_b"]], 0))),
        ("c", by_partition(g["c_2"])), ("c_ctx", by_partition(g["c_ctx_2"][None])),
        ("ffn_conv", conv), ("gdn_conv", gdn_conv)])
    rows, row_at = pack([(n, g[s].reshape(-1)) for n, s in (
        ("b_out_norm", "b_out_norm"), ("q_norm", "q_norm_w_2"), ("k_norm", "k_norm_w_2"), ("a_log", "a_log_2"),
        ("dt_bias", "dt_bias_2"), ("gdn_norm", "gdn_norm_w_2"), ("final_norm", "final_norm_w_2"), ("b_mod", "b_mod_2"))]
        + [("a_gains", np.concatenate([g["a_q_norm"], g["a_k_norm"]], 0).reshape(-1))])
    arrays = {n: np.ascontiguousarray(g[n]) for n in _WEIGHTS}
    arrays.update(consts=consts, vecs=vecs, rows=rows, a_mask=attention_masks())

    nc = bacc.Bacc("TRN2", target_bir_lowering=False, num_devices=1)
    ins = {n: nc.dram_tensor(f"in_{n}", a.shape, F32, kind="ExternalInput").ap() for n, a in arrays.items()}
    out = nc.dram_tensor("out", (1, SEQ, D), F32, kind="ExternalOutput").ap()
    build(nc, ins, out, const_at, vec_at, row_at)
    r = run_bass_kernel_spmd(nc, [{f"in_{n}": a for n, a in arrays.items()}], core_ids=[0])
    return r.results[0]["out"]
```

```python
from contextlib import contextmanager

import concourse.bass as bass
from concourse import mybir
import numpy as np

F32 = mybir.dt.float32
F32R = mybir.dt.float32r
I32 = mybir.dt.int32
ALU = mybir.AluOpType
ACT = mybir.ActivationFunctionType
AX = mybir.AxisListType

P = 128
D = 1024
KT = D // P
SEQ = 256
TT = SEQ // P
EPS = 1e-6
CW = 512
HK = 4

A_GROUPS = ((128, 1), (512, 4), (2048, 16))
NG = len(A_GROUPS)
A_HEADS, A_HD = 16, 64
GLA_HEADS, GLA_DK, GLA_DV, GLA_RANK, GLA_TAU = 4, 128, 256, 16, 16.0
CHUNK = 64
NCH = SEQ // CHUNK
FF = 2816
FT = FF // P
N_FFC = FF // 256
NH2, KV2, HD2 = 8, 2, 128
GROUP2 = NH2 // KV2
GDN_HEADS, GDN_D = 8, 128
NT2 = 4
NK = 10
LEVELS = (1, 2, 4, 8, 16, 32)
GDN_PER = dict(pe=80, act=44, dve=51, pool=7)


def constants():
    p = np.arange(P)
    f32 = np.float32
    c = {}
    c["ident"] = np.eye(P, dtype=f32)
    same = p[:, None] // CHUNK == p[None, :] // CHUNK
    c["gla_f"] = (same & (p[:, None] <= p[None, :])).astype(np.int32).view(f32)
    c["gla_b"] = (same & (p[:, None] > p[None, :])).astype(np.int32).view(f32)
    c["cum_f"] = (same & (p[:, None] <= p[None, :])).astype(f32)
    c["cum_b"] = (same & (p[:, None] >= p[None, :])).astype(f32)
    c["ones_bd"] = same.astype(f32)
    c["even"] = np.repeat((p[:, None] < CHUNK), P, 1).astype(f32)
    c["odd"] = np.repeat((p[:, None] >= CHUNK), P, 1).astype(f32)
    c["pick"] = np.zeros((P, 31), f32)
    c["pick"][:, 15] = 1
    c["neg_f"] = np.where(same & (p[:, None] <= p[None, :]), 0, -1e30).astype(f32)
    c["neg_b"] = np.where(same & (p[:, None] >= p[None, :]), 0, -1e30).astype(f32)
    for b in LEVELS:
        m = (p[:, None] // (2 * b) == p[None, :] // (2 * b)) & (p[:, None] // b != p[None, :] // b)
        c[f"level{b}"] = m.astype(f32)
    tok = np.arange(SEQ).reshape(TT, P).T.astype(f32)
    half = A_HD // 2
    inv = (10000.0 ** (-np.arange(half, dtype=f32) / half)).astype(f32)
    ang = (tok[:, :, None] * inv).astype(f32)
    c["cos_a"] = np.concatenate([np.cos(ang)] * 2, -1).astype(f32).reshape(P, -1)
    c["sin_a"] = np.concatenate([-np.sin(ang), np.sin(ang)], -1).astype(f32).reshape(P, -1)
    inv = (10000.0 ** (-np.arange(0, 64, 2, dtype=f32) / 64)).astype(f32)
    both = []
    for ids in (tok // 64, tok % 64):
        a = (ids.astype(f32)[:, :, None] * inv).astype(f32)
        both.append((np.concatenate([np.cos(a)] * 2, -1), np.concatenate([-np.sin(a), np.sin(a)], -1)))
    c["cos_2"] = np.concatenate([both[0][0], both[1][0]], -1).astype(f32).reshape(P, -1)
    c["sin_2"] = np.concatenate([both[0][1], both[1][1]], -1).astype(f32).reshape(P, -1)
    return c


def attention_masks():
    i, j = np.arange(SEQ)[:, None], np.arange(SEQ)[None, :]
    m = [np.where((abs(i - j) <= w // 2) & ((i - j) % d == 0), 0, -1e30) for w, d in A_GROUPS]
    m = np.stack(m, 1).astype(np.float32)
    return np.ascontiguousarray(m.reshape(TT, P, NG, SEQ).transpose(1, 0, 2, 3)).reshape(P, -1)


class Counter:

    def __init__(self, nc, name):
        self.sem, self.name, self.n = nc.alloc_semaphore(name), name, 0
        self.var, self.per, self.top = None, 0, 0

    def inc(self, ins, by=1):
        ins.then_inc(self.sem, by)
        self.n += by
        return (self, self.n, self.var is not None)

    def now(self):
        return (self, self.n, self.var is not None)

    def back(self, k):
        return (self, max(self.n - k, 0), self.var is not None)


def w(eng, *marks):
    best = {}
    for m in marks:
        if m is not None and (m[0] not in best or best[m[0]][1] <= m[1]):
            best[m[0]] = m
    for c, v, moving in best.values():
        if moving and c.var is not None and c.per:
            eng.wait_ge(c.sem, c.var * c.per + v)
        elif v > 0:
            eng.wait_ge(c.sem, v)


def bc(ap, axis, n):
    ap = ap.unsqueeze(axis)
    shape = list(ap.shape)
    shape[axis] = n
    return ap.to_broadcast(shape)


def build(nc, ins, out, const_at, vec_at, row_at):
    pe, act, dve, pool, sp = nc.tensor, nc.scalar, nc.vector, nc.gpsimd, nc.sync
    T, A, V, G = (Counter(nc, "s_" + n) for n in ("pe", "act", "dve", "pool"))
    raw_in = [Counter(nc, f"s_raw{i}") for i in range(2)]
    hi_ok = [Counter(nc, f"s_hi{i}") for i in range(2)]
    lo_ok = [Counter(nc, f"s_lo{i}") for i in range(2)]
    used = [Counter(nc, f"s_used{i}") for i in range(2)]
    L = Counter(nc, "s_small")
    F = Counter(nc, "s_first")
    stored = Counter(nc, "s_stored")
    counters = [T, A, V, G, *raw_in, *hi_ok, *lo_ok, *used]

    def w_apart(eng, *marks):
        w(eng, *marks)
        if eng is dve:
            dve.memset(unused[:, 0:1], 0.0)
        elif eng is act:
            act.activation(unused[:, 3:4], unused[:, 1:2], ACT.Copy)
        else:
            pool.tensor_tensor(unused[:, 2:3], unused[:, 1:2], unused[:, 1:2], ALU.add)

    @contextmanager
    def loop(n, chunks, **per):
        names = dict(pe=T, act=A, dve=V, pool=G)
        each = {c: 0 for c in counters}
        each.update({names[k]: v for k, v in per.items()})
        each.update({c: chunks for c in (*hi_ok, *lo_ok, *used)})
        each.update({c: 32 * chunks for c in raw_in})
        with nc.Fori(0, n) as i:
            for c in counters:
                c.var, c.per, c.top = i, each[c], c.n
            yield i
            made = {c.name: (c.n - c.top, c.per) for c in counters}
            assert all(a == b for a, b in made.values()), f"increments per iteration: {made}"
            for c in counters:
                c.n, c.var = c.top + n * c.per, None

    at = [nc.sbuf_base + (-nc.sbuf_base) % 64]

    def place(name, shape, dt=F32, offset=None):
        n = int(np.prod(shape[1:]))
        t = nc.alloc_sbuf_tensor_at(name, shape, dt, offset=at[0] if offset is None else offset)
        if offset is None:
            at[0] += 4 * (n + -n % 8)
        return t

    ps = nc.alloc_psum_tensor("ps", [P, 8, 512], F32)
    raw = place("raw", [P, 2, HK, CW])
    whi = place("whi", [P, 2, HK, CW], F32R)
    wlo = place("wlo", [P, 2, HK, CW], F32R)
    resid = place("resid", [P, TT, D])
    cst = place("cst", [P, ins["consts"].shape[1]])
    vec = place("vec", [P, ins["vecs"].shape[1]])
    modcol = place("modcol", [P, 4, KT, 2])
    grow = place("grow", [P, 2, D])
    ccur = place("ccur", [P, 2, 16])
    small = place("small", [P, 8])
    unused, eps_col = small[:, 0:4], small[:, 4:5]
    xs = place("xs", [P, 4, KT, SEQ], F32R)
    arena_at = at[0]
    arena_n = (nc.sbuf_usable_end - arena_at) // 4 // 8 * 8
    hid = place("hid", [P, 2, FT, SEQ], F32R, offset=arena_at + 4 * (arena_n - 2 * FT * SEQ))
    wzs = [nc.alloc_sbuf_tensor_at(f"wzs{j}", [P, 2, KT, 32], F32R, offset=arena_at + 4 * (arena_n - 512 - j * TT * D))
           for j in range(2)]
    XS = 4 * KT * SEQ
    wide = place("wide", [P, arena_n + XS], offset=arena_at - 4 * XS)

    class Carve:

        def __init__(self, start=0, end=arena_n):
            self.at, self.end = start, end

        def __call__(self, *shape):
            n = int(np.prod(shape))
            v = wide[:, XS + self.at:XS + self.at + n]
            self.at += n
            assert self.at <= self.end, (self.at, self.end)
            names = "abcdef"[:len(shape)]
            if len(shape) > 1:
                v = v.rearrange(f"p ({' '.join(names)}) -> p {' '.join(names)}", **dict(zip(names, shape)))
            return v

    def const(name):
        a, b = const_at[name]
        return cst[:, a:b]

    def vcol(name):
        a, b = vec_at[name]
        return vec[:, a:b]

    def load_row(dst, name):
        a, b = row_at[name]
        L.inc(act.dma_start(dst, ins["rows"][a:b].partition_broadcast(P)), 16)

    ident = const("ident")

    def xh(k, t0, t1, seq=0):
        return xs[:, 2 * seq, k, t0:t1]

    def xl(k, t0, t1, seq=0):
        return xs[:, 2 * seq + 1, k, t0:t1]

    x_rest = []
    put_off = []

    def request_put_off():
        if put_off:
            request(put_off.pop(), lo_by=pool)

    def request(source, lo_by=dve):
        if source is None:
            return
        for s in range(2):
            srcs, nk = source(s)
            w(sp, hi_ok[s].now(), lo_ok[s].now())
            for (k0, k1, c0, c1), src in srcs:
                raw_in[s].inc(sp.dma_start(raw[:, s, k0:k1, c0:c1], src), 16)
            w(act, raw_in[s].now(), used[s].now())
            hi_ok[s].inc(act.activation(whi[:, s, 0:nk, :], raw[:, s, 0:nk, :], ACT.Copy))
            w(lo_by, raw_in[s].now(), hi_ok[s].now())
            lo_ok[s].inc(lo_by.tensor_tensor(wlo[:, s, 0:nk, :], raw[:, s, 0:nk, :],
                                           whi[:, s, 0:nk, :].bitcast(F32), ALU.subtract))

    def cols(wmat, c0, k0=0, nks=(HK, HK)):
        def source(s):
            nk, kk = nks[s], k0 + (nks[0] if s else 0)
            h = nk // 2
            return [((j * h, (j + 1) * h, 0, CW),
                     wmat[(kk + j * h) * P:(kk + (j + 1) * h) * P, bass.ds(c0, CW)].rearrange("(k p) n -> p k n", p=P))
                    for j in range(2)], nk
        return source

    def gate_up(wmat, c):
        def source(s):
            return [((0, HK, 256 * j, 256 * (j + 1)),
                     wmat[s * HK * P:(s + 1) * HK * P, bass.ds(c * 256 + j * FF, 256)].rearrange("(k p) n -> p k n", p=P))
                    for j in range(2)], HK
        return source

    def mm3(o, ahi, alo, bhi, blo, start, stop):
        pe.matmul(o, ahi, bhi, start=start, stop=False)
        pe.matmul(o, ahi, blo, start=False, stop=False)
        return pe.matmul(o, alo, bhi, start=False, stop=stop)

    def chunk_tok(banks, tiles=(0, 1), width=CW):
        for s in range(2):
            w(pe, hi_ok[s].now(), lo_ok[s].now(), *(x_rest.pop() if s and x_rest else ()))
            for b, t in zip(banks, tiles):
                for k in range(HK):
                    kk, t0 = s * HK + k, (t % 2) * P
                    i_ = mm3(ps[:, b, 0:width], xh(kk, t0, t0 + P, t // 2), xl(kk, t0, t0 + P, t // 2),
                             whi[:, s, k, 0:width], wlo[:, s, k, 0:width],
                             s == 0 and k == 0, s == 1 and k == HK - 1)
            m = used[s].inc(i_)
        return m

    def chunk_feat(banks, both=False):
        n = 2 * SEQ if both else SEQ
        for s in range(2):
            w(pe, hi_ok[s].now(), lo_ok[s].now(), *(x_rest.pop() if s and x_rest else ()))
            for mb, b in enumerate(banks):
                for k in range(HK):
                    kk = s * HK + k
                    if both:
                        rh, rl = xs[:, 0:4:2, kk, :], xs[:, 1:4:2, kk, :]
                    else:
                        rh, rl = xs[:, 0, kk, :], xs[:, 1, kk, :]
                    i_ = mm3(ps[:, b, 0:n], whi[:, s, k, mb * P:(mb + 1) * P],
                             wlo[:, s, k, mb * P:(mb + 1) * P], rh, rl,
                             s == 0 and k == 0, s == 1 and k == HK - 1)
            m = used[s].inc(i_)
        return m

    def settle(*engs):
        for e in engs or (pe, act, dve, pool):
            w(e, T.now(), A.now(), V.now(), G.now(), used[0].now(), used[1].now())

    def rsqrt(dst, src):
        w(dve, A.inc(act.activation(dst, src, ACT.Sqrt, bias=eps_col)))
        return V.inc(dve.reciprocal(dst, dst))

    def rstd_of(src, n, width, st, sq):
        for j in range(n):
            w(act, A.now())
            A.inc(act.activation(sq, src[:, j, :], ACT.Square, scale=width ** -0.5, accum_out=st[:, j:j + 1]))
        w(act, A.now())
        rsqrt(st[:, 0:n], st[:, 0:n])

    def to_split(src, seq, stage, scale=None, shift=None):
        ends = []
        for g in range(KT // 2):
            b = 4 + g
            for j in range(2):
                for t in range(TT):
                    i_ = pe.transpose(ps[:, b, (j * 2 + t) * P:(j * 2 + t + 1) * P], src(t, 2 * g + j), ident)
            m = T.inc(i_)
            view = ps[:, b, :].rearrange("p (k n) -> p k n", k=2)
            hs, ls = (xs[:, 2 * seq + q, 2 * g:2 * g + 2, :] for q in range(2))
            if shift is not None:
                w(dve, m)
                stv = stage[:, g, :].rearrange("p (k n) -> p k n", k=2)
                for k in range(2):
                    kk = 2 * g + k
                    i_ = dve.tensor_scalar(stv[:, k], view[:, k], scale[:, kk:kk + 1], shift[:, kk:kk + 1], ALU.mult, ALU.add)
                ends.append((V.inc(i_), stv, hs, ls, None))
            else:
                ends.append((m, view, hs, ls, scale))
        marks = []
        for g, (m, x, hs, ls, sc_) in enumerate(ends):
            w(act, m)
            if sc_ is None:
                i_ = act.activation(hs, x, ACT.Copy)
            else:
                for k in range(2):
                    i_ = act.activation(hs[:, k], x[:, k], ACT.Copy, scale=sc_[:, 2 * g + k:2 * g + k + 1])
            ma = A.inc(i_)
            w(dve, ma)
            if sc_ is None:
                i_ = dve.tensor_tensor(ls, x, hs.bitcast(F32), ALU.subtract)
            else:
                for k in range(2):
                    i_ = dve.scalar_tensor_tensor(ls[:, k], x[:, k], sc_[:, 2 * g + k:2 * g + k + 1], hs[:, k].bitcast(F32),
                                                  ALU.mult, ALU.subtract)
            marks.append((ma, V.inc(i_)))
        w(pe, *marks[1])
        x_rest.append(marks[3])

    def norm_split(src, seq, c, scale, shift=None):
        st, sq, xn, stage = c(8), c(D), c(TT, D), c(4, 512)
        settle()
        rstd_of(src, TT, D, st, sq)
        request_put_off()
        w(dve, V.now())
        for t in range(TT):
            V.inc(dve.tensor_scalar(xn[:, t, :], src[:, t, :], st[:, t:t + 1], None, ALU.mult))
        w(pe, V.now())
        to_split(lambda t, k: xn[:, t, k * P:(k + 1) * P], seq, stage, scale, shift)

    def add_product(wmat, nxt, gate=None, tmp=None):
        for n in range(2):
            m = chunk_tok((2 * n, 2 * n + 1))
            if n == 0:
                request(cols(wmat, CW))
            else:
                put_off.append(nxt)
            o = resid[:, :, n * CW:(n + 1) * CW]
            w(dve, m, V.now())
            if gate is None:
                V.inc(dve.tensor_tensor(o, o, ps[:, 2 * n:2 * n + 2, :], ALU.add))
            else:
                V.inc(dve.tensor_tensor(tmp, ps[:, 2 * n:2 * n + 2, :], bc(gate[:, n * CW:(n + 1) * CW], 1, TT), ALU.mult))
                w(dve, V.now())
                V.inc(dve.tensor_tensor(o, o, tmp, ALU.add))

    def narrow(src, raw_, halves, bank, n):
        w(act, V.now(), T.now())
        L.inc(act.dma_start(raw_, src.rearrange("(k p) n -> p k n", p=P)), 16)
        w(act, L.now())
        w(dve, L.now(), A.inc(act.activation(halves[:, 0], raw_, ACT.Copy)))
        w(pe, V.inc(dve.tensor_tensor(halves[:, 1], raw_, halves[:, 0].bitcast(F32), ALU.subtract)))
        w(pe, *(x_rest.pop() if x_rest else ()))
        for k in range(KT):
            if n == SEQ:
                rh, rl = xs[:, 0, k, :], xs[:, 1, k, :]
            else:
                rh, rl = xs[:, 0:4:2, k, :], xs[:, 1:4:2, k, :]
            i_ = mm3(ps[0:32, bank, 0:n], halves[:, 0, k, :], halves[:, 1, k, :], rh, rl, k == 0, k == KT - 1)
        return T.inc(i_)

    def ffn(w_up, w_down, nxt, conv=None, gate=None):
        settle()
        c = Carve(end=arena_n - 2 * FT * SEQ)
        tmp, val = c(2, 2, SEQ), c(2, 2, SEQ)
        yb, zb = (c(2, 4, SEQ), c(2, 4, SEQ)) if conv is not None else (None, None)
        prod = c(TT, CW)
        nv, na, ng = (4, 3, 1) if conv is not None else (2, 2, 0)

        def one(ci, par, after):
            b0 = 4 * par
            w(pe, V.back(nv), A.back(na))
            m = chunk_feat(range(b0, b0 + 4))
            two_ago = (V.back(nv), A.back(na))
            request(after)
            up = ps[:, b0 + 2:b0 + 4, 0:SEQ]
            if conv is None:
                w(act, m, *two_ago)
                A.inc(act.activation(tmp[:, par, :, :], ps[:, b0:b0 + 2, 0:SEQ], ACT.Silu))
            else:
                y, z = yb[:, par, :, :], zb[:, par, :, :]
                taps = ccur[:, par, :].rearrange("p (a t b) -> p a t b", a=2, t=4)
                w(pool, *two_ago)
                G.inc(pool.tensor_copy(taps, conv[:, :, :, bass.ds(ci * 2, 2)]))
                tap = [[taps[:, q // 2, t, q % 2:q % 2 + 1] for t in range(4)] for q in range(4)]
                w(act, m, G.now(), *two_ago)
                for q in range(4):
                    i_ = act.activation(y[:, q, :], ps[:, b0 + q, 0:SEQ], ACT.Identity, scale=tap[q][1], bias=tap[q][3])
                A.inc(i_)
                w(dve, A.now(), V.now())
                for q in range(4):
                    dve.scalar_tensor_tensor(z[:, q, 1:SEQ], ps[:, b0 + q, 0:SEQ - 1], tap[q][0],
                                             y[:, q, 1:SEQ], ALU.mult, ALU.add)
                V.inc(dve.tensor_copy(z[:, :, 0:1], y[:, :, 0:1]))
                w(dve, V.now())
                for q in range(4):
                    dve.scalar_tensor_tensor(y[:, q, 0:SEQ - 1], ps[:, b0 + q, 1:SEQ], tap[q][2],
                                             z[:, q, 0:SEQ - 1], ALU.mult, ALU.add)
                V.inc(dve.tensor_copy(y[:, :, SEQ - 1:SEQ], z[:, :, SEQ - 1:SEQ]))
                w(act, V.now())
                A.inc(act.activation(tmp[:, par, :, :], y[:, 0:2, :], ACT.Silu))
                up = y[:, 2:4, :]
            w(dve, A.now(), V.now())
            V.inc(dve.tensor_tensor(val[:, par, :, :], tmp[:, par, :, :], up, ALU.mult))
            w(act, V.now())
            hs = hid[:, 0, bass.ds(ci * 2, 2), :]
            A.inc(act.activation(hs, val[:, par, :, :], ACT.Copy))
            w(dve, A.now())
            V.inc(dve.tensor_tensor(hid[:, 1, bass.ds(ci * 2, 2), :], val[:, par, :, :], hs.bitcast(F32), ALU.subtract))

        with loop((N_FFC - 1) // 2, 2, dve=2 * nv, act=2 * na, pool=2 * ng) as i:
            one(i * 2, 0, gate_up(w_up, i * 2 + 1))
            one(i * 2 + 1, 1, gate_up(w_up, i * 2 + 2))
        splits = ((0, (HK, HK)), (8, (HK, HK)), (16, (HK, 2)))
        one(N_FFC - 1, 0, cols(w_down, 0, *splits[0]))
        w(pe, V.back(nv), A.back(na))
        for n in range(2):
            for j, (k0, nks) in enumerate(splits):
                if n == 0 and j == len(splits) - 1:
                    w(pe, V.now(), A.now())
                for s in range(2):
                    w(pe, hi_ok[s].now(), lo_ok[s].now())
                    for t in range(TT):
                        for k in range(nks[s]):
                            kk = k0 + s * HK + k
                            i_ = mm3(ps[:, 4 + 2 * n + t, :], hid[:, 0, kk, t * P:(t + 1) * P],
                                     hid[:, 1, kk, t * P:(t + 1) * P], whi[:, s, k, :], wlo[:, s, k, :],
                                     kk == 0, kk == FT - 1)
                    m = used[s].inc(i_)
                if j < 2:
                    request(cols(w_down, n * CW, *splits[j + 1]))
                elif n == 0:
                    request(cols(w_down, CW, *splits[0]))
                elif nxt is not None:
                    put_off.append(nxt)
            o = resid[:, :, n * CW:(n + 1) * CW]
            pv = ps[:, 4 + 2 * n:6 + 2 * n, :]
            w(dve, m, V.now())
            if gate is not None:
                V.inc(dve.tensor_tensor(prod, pv, bc(gate[:, n * CW:(n + 1) * CW], 1, TT), ALU.mult))
                w(dve, V.now())
                pv = prod
            V.inc(dve.tensor_tensor(o, o, pv, ALU.add))

    def head_norm_rope(x, nh, hd, nt, cos, sin, dst, bufs):
        sq, r, xn, a, b = bufs
        n = nt * nh
        g = sq[:, 0:n * hd]
        w(act, V.now(), G.now())
        A.inc(act.activation(g.rearrange("p (t m) -> p t m", t=nt), x, ACT.Square, scale=hd ** -0.5))
        w(dve, A.now())
        V.inc(dve.tensor_reduce(r[:, 0:n], g.rearrange("p (n d) -> p n d", d=hd), AX.X, ALU.add))
        w(act, V.now())
        rsqrt(r[:, 0:n], r[:, 0:n])
        w(dve, V.now(), G.now())
        xv = xn[:, 0:n * hd].rearrange("p (t h d) -> p t h d", t=nt, d=hd)
        for t in range(nt):
            i_ = dve.tensor_tensor(xv[:, t], x[:, t, :].rearrange("p (h d) -> p h d", d=hd),
                                   bc(r[:, t * nh:(t + 1) * nh], 2, hd), ALU.mult)
        V.inc(i_)
        done_psum = V.now()
        av, bv = (q[:, 0:n * hd].rearrange("p (t h d) -> p t h d", t=nt, d=hd) for q in (a, b))
        w_apart(pool, V.now())
        for t in range(nt):
            i_ = pool.tensor_tensor(av[:, t], xv[:, t], bc(cos[:, t, :], 1, nh), ALU.mult)
        G.inc(i_)
        w(dve, V.now())
        hh = 32
        for t in range(nt):
            for q in range(hd // 64):
                for s_ in range(2):
                    o0, i0 = q * 64 + s_ * hh, q * 64 + (1 - s_) * hh
                    i_ = dve.tensor_tensor(bv[:, t, :, o0:o0 + hh], xv[:, t, :, i0:i0 + hh],
                                           bc(sin[:, t, o0:o0 + hh], 1, nh), ALU.mult)
        V.inc(i_)
        w_apart(pool, V.now(), G.now())
        for t in range(nt):
            i_ = pool.tensor_tensor(dst(t), av[:, t], bv[:, t], ALU.add)
        G.inc(i_)
        return done_psum

    def layer_a(nxt):
        w_in, w_out = ins["a_w_in"][0], ins["a_w_out"][0]
        c = Carve()
        q_k = c(2, NG, TT, D)
        vv = c(NG, TT, D)
        keep = c.at
        tabs = c(2, NG, 2, TT, A_HD)
        gains = c(2, NG, A_HD)
        sq = c(1024)
        bufs = (sq, c(16), c(1024), c(1024), sq)
        load_row(gains.rearrange("p a b c -> p (a b c)"), "a_gains")
        w(pool, L.now())
        cosv = const("cos_a").rearrange("p (t d) -> p t d", t=TT)
        sinv = const("sin_a").rearrange("p (t d) -> p t d", t=TT)
        for j in range(2):
            for g in range(NG):
                for t in range(TT):
                    G.inc(pool.tensor_tensor(tabs[:, 0, g, j, t, :], cosv[:, t, :], gains[:, j, g, :], ALU.mult))
                    for s_ in range(2):
                        o, i_ = slice(s_ * 32, s_ * 32 + 32), slice(32 - s_ * 32, 64 - s_ * 32)
                        G.inc(pool.tensor_tensor(tabs[:, 1, g, j, t, o], sinv[:, t, o], gains[:, j, g, i_], ALU.mult))
        w(dve, G.now())

        def chunk(g, j, nxt_, ends):
            kind, half, gi = j // 2, j % 2, bass.ds(g, 1)
            b0 = 2 * (j % 4)
            w(pe, *ends[max(j - 1, 0)])
            m = chunk_tok((b0, b0 + 1))
            request(nxt_)
            w(act, m)
            w(dve, m)
            x = ps[:, b0:b0 + 2, :]
            flat = "p a t d -> p (a t) d"
            if kind < 2:
                head_norm_rope(
                    x, 8, A_HD, TT, tabs[:, 0, gi, kind, :, :].rearrange(flat), tabs[:, 1, gi, kind, :, :].rearrange(flat),
                    lambda t: q_k[:, kind, gi, t, half * CW:(half + 1) * CW].rearrange("p a (h d) -> p (a h) d", d=A_HD),
                    bufs)
            else:
                A.inc(act.activation(vv[:, gi, :, half * CW:(half + 1) * CW].rearrange(flat), x, ACT.Copy))
            ends.append((V.now(), A.now()))

        with loop(NG - 1, 6, act=2 * 4 + 2, dve=4 * 4, pool=2 * 4) as g:
            ends = [(V.now(), A.now())]
            for j in range(6):
                chunk(g, j, cols(w_in, g * (3 * D) + (j + 1) * CW), ends)
        ends = [(V.now(), A.now())]
        for j in range(6):
            chunk(NG - 1, j, cols(w_in, (NG - 1) * 3 * D + (j + 1) * CW) if j < 5 else cols(w_out, 0), ends)

        o = Carve(-TT * D, 0)(TT, D)
        c = Carve(-XS, -TT * D)
        stg = c(2, 6, P)
        kT = [c(6, P) for _ in range(2)]
        qz = [[c(6, P) for _ in range(2)] for _ in range(2)]
        c = Carve(start=keep)
        S, E, ET = (c(2, NG * SEQ) for _ in range(3))
        mask = c(TT, NG * SEQ)
        U = 8
        mx, ngm, l, rl = (c(U) for _ in range(4))
        settle()
        w(sp, T.now(), A.now(), V.now(), G.now())
        L.inc(sp.dma_start(mask.rearrange("p a b -> p (a b)"), ins["a_mask"]), 16)
        for z_ in qz:
            for h in range(2):
                V.inc(dve.memset(z_[h][64 - 64 * h:128 - 64 * h, :, :], 0.0))
        zeroed = V.now()
        scale = A_HD ** -0.5

        def columns(hp, off, n):
            return bass.ds(hp * P + off, n) if not isinstance(hp, int) else slice(hp * P + off, hp * P + off + n)

        def stage_pair(hp, *free):
            w_apart(pool, *free)
            for kind in range(2):
                for g in range(NG):
                    i_ = pool.tensor_copy(stg[:, kind, 2 * g:2 * g + 2, :], q_k[:, kind, g, :, columns(hp, 0, P)])
            return G.inc(i_)

        def transposed(kind, par, b, staged, *free):
            w(pe, staged, *free)
            for j in range(6):
                i_ = pe.transpose(ps[:, b + j // 4, (j % 4) * P:(j % 4 + 1) * P], stg[:, kind, j, :], ident)
            src = ps[:, b:b + 2, :].rearrange("p a b -> p (a b)")
            m = T.inc(i_)
            if kind:
                w(act, m)
                return A.inc(act.activation(kT[par].rearrange("p a b -> p (a b)"), src[:, 0:768], ACT.Copy))
            w(dve, m)
            for h in range(2):
                r = slice(64 * h, 64 * h + 64)
                i_ = dve.tensor_copy(qz[par][h][r].rearrange("p a b -> p (a b)"), src[r, 0:768])
            return V.inc(i_)

        def two_pairs(i, ready, last):
            ex, read, out, et = {0: ready["exp"]}, {0: ready["read"]}, {-2: ready["out"], -1: ready["out"]}, {}
            pair_ok, staged = {0: None, 1: None}, ready["staged"]
            bank_ok = {0: None, 1: None}

            def scores(u, after_pair=()):
                pr, h, t, par = u // 4 % 2, u // 2 % 2, u % 2, u % 2
                b = 4 + 2 * par
                w(pe, read.get(u - 2), ready["out"] if u < 2 else None, *after_pair)
                for g in range(NG):
                    i_ = pe.matmul(ps[:, b + g // 2, (g % 2) * SEQ:(g % 2 + 1) * SEQ], qz[pr][h][:, 2 * g + t, :],
                                   kT[pr][:, 2 * g:2 * g + 2, :], start=True, stop=True)
                w_apart(dve, T.inc(i_), ex.get(u - 2, ready["exp"]))
                n = u % U
                sc = ps[:, b:b + 2, :].rearrange("p a b -> p (a b)")[:, 0:NG * SEQ]
                read[u] = V.inc(dve.tensor_tensor_reduce(out=S[:, par, :], in0=sc, in1=mask[:, t, :], scale=1.0, scalar=-3e38,
                                                         op0=ALU.add, op1=ALU.max, accum_out=mx[:, n:n + 1]))
                w(dve, read[u])
                return V.inc(dve.tensor_scalar(ngm[:, n:n + 1], mx[:, n:n + 1], -scale, None, ALU.mult))

            def exponentials(u, m):
                par, n = u % 2, u % U
                w(act, m, T.now())
                ex[u] = A.inc(act.activation(E[:, par, :], S[:, par, :], ACT.Exp, bias=ngm[:, n:n + 1], scale=scale,
                                             accum_out=l[:, n:n + 1]))

            def transposes(u):
                par, n = u % 2, u % U
                b = 2 * par
                w(pe, ex[u], out[u - 2], bank_ok[par])
                for j in range(6):
                    i_ = pe.transpose(ps[:, b + j // 4, (j % 4) * P:(j % 4 + 1) * P], E[:, par, j * P:(j + 1) * P], ident)
                tm = T.inc(i_)
                w(act, tm)
                ma = A.inc(act.activation(ET[:, par, 0:512], ps[:, b, :], ACT.Copy))
                w(dve, tm, ex[u])
                mv = V.inc(dve.tensor_copy(ET[:, par, 512:768], ps[:, b + 1, 0:256]))
                et[u] = (ma, mv, V.inc(dve.reciprocal(rl[:, n:n + 1], l[:, n:n + 1])))

            def values(u):
                pr, h, t, par = u // 4, u // 2 % 2, u % 2, u % 2
                w(pe, *et[u][:2])
                po = ps[:, 2 * par + 1, 256:384]
                for j in range(6):
                    i_ = pe.matmul(po, ET[:, par, j * P:(j + 1) * P], vv[:, j // 2, j % 2, columns(i * 2 + pr, 0, P)],
                                   start=(j == 0), stop=(j == 5))
                w(dve, T.inc(i_), et[u][2])
                out[u] = V.inc(dve.tensor_scalar(o[:, t, columns(i * 2 + pr, 64 * h, 64)], po[:, 64 * h:64 * h + 64],
                                                 rl[:, u:u + 1], None, ALU.mult))

            for u in range(U):
                m = None
                if u + 1 < U or not last:
                    after_pair = (pair_ok[1], ready.get("k1")) if u + 1 == 4 else (pair_ok[0], ready.get("k0")) if u + 1 == U else ()
                    m = scores(u + 1, after_pair)
                transposes(u)
                if m is not None:
                    exponentials(u + 1, m)
                if u:
                    values(u - 1)
                if u in (1, 2) or (u in (5, 6) and not last):
                    kind, par_ = 0 if u in (1, 5) else 1, 1 if u < 4 else 0
                    b = 2 * ((u - 1) % 2)
                    ok = transposed(kind, par_, b, staged, out[u - 1])
                    bank_ok[(u - 1) % 2] = ok
                    if kind == 0:
                        pair_ok[par_] = ok
                    else:
                        ready[f"k{par_}"] = ok
                        if par_ == 1 and not last:
                            staged = stage_pair(i * 2 + 2, T.now())
                        elif par_ == 0:
                            staged = stage_pair(i * 2 + 3, T.now())
            values(U - 1)

        for kind in range(2):
            for g in range(NG):
                i_ = act.activation(stg[:, kind, 2 * g:2 * g + 2, :], q_k[:, kind, g, :, 0:P], ACT.Copy)
        m = A.inc(i_)
        mq = transposed(0, 0, 0, m, zeroed)
        mk = transposed(1, 0, 2, m)
        m = stage_pair(1, T.now())
        for g in range(NG):
            w(pe, mq, mk)
            i_ = pe.matmul(ps[:, 4 + g // 2, (g % 2) * SEQ:(g % 2 + 1) * SEQ], qz[0][0][:, 2 * g, :],
                           kT[0][:, 2 * g:2 * g + 2, :], start=True, stop=True)
        w_apart(dve, T.inc(i_), L.now())
        V.inc(dve.tensor_tensor_reduce(out=S[:, 0, :], in0=ps[:, 4:6, :].rearrange("p a b -> p (a b)")[:, 0:NG * SEQ],
                                       in1=mask[:, 0, :], scale=1.0, scalar=-3e38, op0=ALU.add, op1=ALU.max,
                                       accum_out=mx[:, 0:1]))
        w(dve, V.now())
        V.inc(dve.tensor_scalar(ngm[:, 0:1], mx[:, 0:1], -scale, None, ALU.mult))
        w(act, V.now())
        A.inc(act.activation(E[:, 0, :], S[:, 0, :], ACT.Exp, bias=ngm[:, 0:1], scale=scale, accum_out=l[:, 0:1]))

        def before():
            return {"exp": A.now(), "read": V.now(), "out": V.now(), "staged": G.now()}

        with loop(A_HEADS // 4 - 1, 0, pe=3 * U + 4, act=2 * U + 2, dve=5 * U + 2, pool=2) as i:
            two_pairs(i, before(), False)
        two_pairs(A_HEADS // 4 - 1, before(), True)

        settle()
        to_split(lambda t, k: o[:, t, k * P:(k + 1) * P], 0, None)
        add_product(w_out, nxt)

    def layer_b(nxt):
        w_in, w_out = ins["b_w_in"][0], ins["b_w_out"][0]
        QK, VW = GLA_HEADS * GLA_DK, GLA_HEADS * GLA_DV
        settle()
        c = Carve()
        qT, kT_ = c(GLA_HEADS, SEQ), c(GLA_HEADS, SEQ)
        v, r = c(TT, VW), c(TT, VW)
        la = c(2, GLA_HEADS * SEQ)
        wz = c(KT, 2 * GLA_RANK)
        zT = c(SEQ)
        wg = c(2, QK)
        gain = c(VW)
        t1, t2 = c(2, GLA_HEADS * SEQ), c(2, GLA_HEADS * SEQ)
        NB = GLA_HEADS * NCH
        e1, e2 = la, c(2, GLA_HEADS * SEQ)
        e3 = t1
        dec = c(2, NB)
        w(act, V.now(), T.now(), G.now())
        w(dve, A.now())
        w(act, V.inc(dve.memset(wg[0:32], 0.0)))
        L.inc(act.dma_start(wg[0:GLA_RANK, 0, :], ins["b_w_gate_f"][0]), 16)
        L.inc(act.dma_start(wg[GLA_RANK:32, 1, :], ins["b_w_gate_b"][0]), 16)
        load_row(gain, "b_out_norm")
        narrow(w_in[:, 2 * QK + 2 * VW:], wz, wzs[0], 0, SEQ)
        w(dve, T.now())
        V.inc(dve.tensor_copy(zT[0:32, :], ps[0:32, 0, 0:SEQ]))
        w(pe, V.now(), L.now())
        for d in range(2):
            for h in range(GLA_HEADS):
                i_ = pe.matmul(ps[:, 4 + 2 * d + h // 2, (h % 2) * SEQ:(h % 2 + 1) * SEQ],
                               wg[0:32, d, h * P:(h + 1) * P], zT[0:32, :], start=True, stop=True)
        gates = T.inc(i_)
        bias = vcol("gla_bias").rearrange("p (d h) -> p d h", d=2)

        def gate_steps():
            w(dve, gates)
            for d in range(2):
                i_ = dve.tensor_tensor(t1[:, d].rearrange("p (h n) -> p h n", h=4),
                                       ps[:, 4 + 2 * d:6 + 2 * d, :].rearrange("p b (h n) -> p (b h) n", h=2),
                                       bc(bias[:, d, :], 2, SEQ), ALU.add)
            w(act, V.inc(i_))
            yield
            A.inc(act.activation(t2, t1, ACT.Abs))
            w(act, A.now())
            A.inc(act.activation(t2, t2, ACT.Exp, scale=-1.0))
            yield
            w(act, A.now())
            ln = A.inc(act.activation(t2, t2, ACT.Ln, bias=1.0))
            w(dve, ln)
            m_ = V.inc(dve.tensor_scalar(t1, t1, 0.0, 1.0 / GLA_TAU, ALU.min, ALU.mult))
            w(dve, m_)
            V.inc(dve.scalar_tensor_tensor(la, t2, -1.0 / GLA_TAU, t1, ALU.mult, ALU.add))
            yield
            yield from sums()

        def sums():
            keepm = t1[:, 0, :]
            w(dve, V.now())
            V.inc(dve.memset(keepm, 1.0))
            w(dve, V.now())
            V.inc(dve.memset(keepm.rearrange("p (n c) -> p n c", c=CHUNK)[:, :, 0:1], 0.0))
            w(dve, V.now())
            V.inc(dve.tensor_tensor_scan(t2[:, 0, :], keepm, la[:, 0, :], 0.0, ALU.mult, ALU.add))
            V.inc(dve.tensor_tensor_scan(t2[:, 1, ::-1], keepm, la[:, 1, ::-1], 0.0, ALU.mult, ALU.add))
            yield
            w(dve, V.now())
            b4 = t2.rearrange("p d (n c) -> p d n c", c=CHUNK)
            e34 = e3.rearrange("p d (n c) -> p d n c", c=CHUNK)
            last = [b4[:, 0, :, CHUNK - 1], b4[:, 1, :, 0]]
            for d in range(2):
                i_ = dve.tensor_tensor(e34[:, d], bc(last[d], 2, CHUNK), b4[:, d], ALU.subtract)
            V.inc(i_)
            w(act, V.now())
            for d in range(2):
                act.activation(dec[:, d, :], last[d], ACT.Exp)
            act.activation(e1, t2, ACT.Exp)
            act.activation(e2, t2, ACT.Exp, scale=-1.0)
            A.inc(act.activation(e3, e3, ACT.Exp))

        steps = gate_steps()
        next(steps)
        m = chunk_feat(range(0, 4))
        request(cols(w_in, CW))
        w(act, m)
        A.inc(act.activation(qT, ps[:, 0:4, 0:SEQ], ACT.Copy, scale=GLA_DK ** -0.5))
        next(steps)
        w(pe, V.now())
        m = chunk_feat(range(4, 8))
        request(cols(w_in, 2 * CW))
        w(act, m)
        A.inc(act.activation(kT_, ps[:, 4:8, 0:SEQ], ACT.Copy))
        next(steps)
        read = A.now()
        for j in range(4):
            dst = (v, r)[j // 2]
            b0 = 2 * j
            w(pe, read)
            m = chunk_tok((b0, b0 + 1))
            request(cols(w_in, (3 + j) * CW) if j < 3 else cols(w_out, 0))
            w(act, m)
            o_ = dst[:, :, (j % 2) * CW:(j % 2 + 1) * CW]
            read = A.inc(act.activation(o_, ps[:, b0:b0 + 2, :], ACT.Copy if j < 2 else ACT.Silu))
            next(steps, None)
        o = c(TT, VW)
        qd, kd, ke = c(2, SEQ), c(2, SEQ), c(2, SEQ)
        kt = [c(2, TT, P) for _ in range(2)]
        AT = c(TT, P)
        S = c(2, NCH, GLA_DV)
        settle(dve, act, pe)
        V.inc(dve.memset(AT, 0.0))
        for q in range(2):
            V.inc(dve.memset(kt[q][64 - 64 * q:128 - 64 * q], 0.0))
        w(dve, V.now())
        mf, mb = const("gla_f").bitcast(I32), const("gla_b").bitcast(I32)
        with loop(GLA_HEADS, 0, pe=4 + TT, act=1, dve=2 + 2 + 2 * (NCH - 1) + TT) as h:
            hs = bass.ds(h * SEQ, SEQ)
            hv = bass.ds(h * GLA_DV, GLA_DV)
            w(dve, T.now(), A.now(), V.now())
            for d in range(2):
                e = [x[:, d, hs] for x in (e1, e2, e3)]
                qh, kh = (x[:, bass.ds(h, 1), :].rearrange("p a n -> p (a n)") for x in (qT, kT_))
                dve.tensor_tensor(qd[:, d, :], qh, e[0], ALU.mult)
                dve.tensor_tensor(kd[:, d, :], kh, e[1], ALU.mult)
                i_ = dve.tensor_tensor(ke[:, d, :], kh, e[2], ALU.mult)
                V.inc(i_)
            w(pe, V.now(), A.now())
            for d in range(2):
                for t in range(TT):
                    i_ = pe.transpose(ps[:, 0, (2 * d + t) * P:(2 * d + t + 1) * P], ke[:, d, t * P:(t + 1) * P], ident)
            w(act, T.inc(i_))
            for q in range(2):
                rr = slice(64 * q, 64 * q + 64)
                i_ = act.activation(kt[q][rr].rearrange("p a b c -> p (a b c)"), ps[rr, 0, :], ACT.Copy)
            A.inc(i_)
            for d in range(2):
                for t in range(TT):
                    i_ = pe.matmul(ps[:, 1, (2 * d + t) * P:(2 * d + t + 1) * P], kd[:, d, t * P:(t + 1) * P],
                                   qd[:, d, t * P:(t + 1) * P], start=True, stop=True)
            m = T.inc(i_)
            for d, mk in ((0, mf), (1, mb)):
                w_apart(dve, m, V.now())
                for t in range(TT):
                    i_ = dve.copy_predicated(AT[:, t, :], mk, ps[:, 1, (2 * d + t) * P:(2 * d + t + 1) * P])
                V.inc(i_)
            w(pe, A.now())
            kv = {}
            for d in range(2):
                for j in range(NCH - 1):
                    n = j if d == 0 else NCH - 1 - j
                    slot = ps[:, 2 + d * 2 + j // 2, (j % 2) * SEQ:(j % 2 + 1) * SEQ]
                    kv[d, j] = slot
                    i_ = pe.matmul(slot, kt[n % 2][:, d, n // 2, :], v[:, n // 2, hv], start=True, stop=True)
                w(dve, T.inc(i_))
                for j in range(NCH - 1):
                    n = j if d == 0 else NCH - 1 - j
                    to = n + 1 if d == 0 else n - 1
                    if j == 0:
                        i_ = dve.tensor_copy(S[:, d, to, :], kv[d, j])
                    else:
                        w(dve, V.now())
                        i_ = dve.scalar_tensor_tensor(S[:, d, to, :], S[:, d, n, :], dec[:, d, bass.ds(h * NCH + n, 1)],
                                                      kv[d, j], ALU.mult, ALU.add)
                    V.inc(i_)
            w(pe, V.now())
            for t in range(TT):
                po = ps[:, 6 + t, 0:GLA_DV]
                pe.matmul(po, AT[:, t, :], v[:, t, hv], start=True, stop=False)
                for q in range(2):
                    n = 2 * t + q
                    rows, cs = slice(64 * q, 64 * q + 64), slice(n * CHUNK, (n + 1) * CHUNK)
                    dirs = [d for d in range(2) if not (d == 0 and n == 0) and not (d == 1 and n == NCH - 1)]
                    for d in dirs:
                        i_ = pe.matmul(ps[rows, 6 + t, 0:GLA_DV], qd[:, d, cs], S[:, d, n, :], start=False,
                                       stop=(d == dirs[-1]))
                w(dve, T.inc(i_))
                V.inc(dve.tensor_copy(o[:, t, hv], po))
        settle(act, dve, pe)
        sq, st = e1.rearrange("p a b -> p (a b)"), dec.rearrange("p a b -> p (a b)")
        A.inc(act.activation(sq, o.rearrange("p a b -> p (a b)"), ACT.Square, scale=GLA_DV ** -0.5))
        w(dve, A.now())
        nh = TT * GLA_HEADS
        V.inc(dve.tensor_reduce(st[:, 0:nh], sq.rearrange("p (n d) -> p n d", d=GLA_DV), AX.X, ALU.add))
        w(act, V.now())
        w(dve, rsqrt(st[:, 0:nh], st[:, 0:nh]), L.now())
        o3 = o.rearrange("p a (n d) -> p (a n) d", d=GLA_DV)
        V.inc(dve.tensor_tensor(o3, o3, bc(st[:, 0:nh], 2, GLA_DV), ALU.mult))
        w(dve, V.now())
        V.inc(dve.tensor_tensor(o, o, bc(gain, 1, TT), ALU.mult))
        w(dve, V.now())
        V.inc(dve.tensor_tensor(o, o, r, ALU.mult))
        settle()
        to_split(lambda t, k: o[:, t, k * P:(k + 1) * P], 0, None)
        add_product(w_out, nxt)

    def modulation(nxt, bias, ctx):
        request_put_off()
        w_mod = ins["w_mod_2"][0]
        settle()
        c = Carve()
        sil, wide_c, rows = c(2, KT), c(KT, SEQ), c(2, CW)
        w(act, V.now())
        L.inc(act.dma_start(ctx, ins["ctx_2"][0].rearrange("(t p) d -> p t d", p=P)), 16)
        act.activation(sil[:, 0, :], vcol("c"), ACT.Silu)
        A.inc(act.activation(sil[:, 1, :], vcol("c_ctx"), ACT.Silu))
        w(dve, A.now())
        dve.tensor_copy(wide_c[:, :, 0:192], bc(sil[:, 0, :], 2, 192))
        V.inc(dve.tensor_copy(wide_c[:, :, 192:256], bc(sil[:, 1, :], 2, 64)))
        w(act, V.now())
        A.inc(act.activation(xs[:, 0, :, :], wide_c, ACT.Copy))
        w(dve, A.now(), L.now())
        V.inc(dve.tensor_tensor(xs[:, 1, :, :], wide_c, xs[:, 0, :, :].bitcast(F32), ALU.subtract))
        w(pe, V.now())
        ends = [None, None]
        for j in range(12):
            which, n = j // 2, j % 2
            b = j % 2
            w(pe, ends[b])
            m = chunk_tok((b,), (1,) if which < 2 else (0,))
            request(cols(w_mod, (j + 1) * CW) if j < 11 else nxt)
            brow = bias[:, which, n * CW:(n + 1) * CW]
            w(dve, m, V.now(), T.now())
            if which % 3 == 2:
                V.inc(dve.tensor_tensor(grow[:, which // 3, n * CW:(n + 1) * CW], ps[:, b, :], brow, ALU.add))
                ends[b] = V.now()
                continue
            V.inc(dve.tensor_tensor(rows[:, b, :], ps[:, b, :], brow, ALU.add))
            ends[b] = V.now()
            w(pe, V.now())
            for q in range(4):
                i_ = pe.transpose(ps[:, 2 + b, q * P:(q + 1) * P], rows[:, b, q * P:(q + 1) * P], ident)
            w(dve, T.inc(i_))
            v_ = (0, 1, None, 2, 3)[which]
            colv = ps[:, 2 + b, :].rearrange("p (q n) -> p q n", q=4)[:, :, 0:P:64]
            V.inc(dve.tensor_scalar(modcol[:, v_, 4 * n:4 * n + 4, :], colv, 1.0 if v_ % 2 else 0.0, None, ALU.add))
            ends[b] = V.now()

    def attention_2(akv_next, o):
        w_in = ins["w_in_2"][0]
        QW = 3616
        c = Carve(end=arena_n - 2048)
        k, v, q = c(NT2, KV2 * HD2), c(NT2, KV2 * HD2), c(TT, NH2 * HD2)
        tk, tq = c(2, NT2, HD2), c(2, TT, HD2)
        gk, gq = c(HD2), c(HD2)
        sq = c(1024)
        bufs = (sq, c(16), c(1024), c(1024), sq)
        kT = c(KV2, NT2 * P)
        settle(act)
        load_row(gk, "k_norm")
        load_row(gq, "q_norm")
        cosv = const("cos_2").rearrange("p (t d) -> p t d", t=TT)
        sinv = const("sin_2").rearrange("p (t d) -> p t d", t=TT)
        settle(pool)
        w(pool, L.now())
        for tab, gain in ((tk, gk), (tq, gq)):
            for t in range(TT):
                pool.tensor_tensor(tab[:, 0, t, :], cosv[:, t, :], gain, ALU.mult)
                for s_ in range(4):
                    o_, i_ = slice(s_ * 32, s_ * 32 + 32), slice((s_ ^ 1) * 32, (s_ ^ 1) * 32 + 32)
                    pool.tensor_tensor(tab[:, 1, t, o_], sinv[:, t, o_], gain[:, i_], ALU.mult)
        for t in range(TT, NT2):
            pool.tensor_copy(tk[:, 0, t, :], gk)
        G.inc(pool.memset(tk[:, 1, TT:NT2, :], 0.0))
        m = chunk_tok((0, 1, 2, 3), (0, 1, 2, 3))
        request(cols(w_in, QW))
        w(act, m)
        w(dve, m, G.now())
        head_norm_rope(ps[:, 0:4, 0:256], KV2, HD2, NT2, tk[:, 0], tk[:, 1],
                       lambda t: k[:, t, :].rearrange("p (h d) -> p h d", d=HD2), bufs)
        w(act, V.now())
        A.inc(act.activation(v, ps[:, 0:4, 256:512], ACT.Copy))
        for n in range(2):
            b0 = 4 + 2 * n
            m = chunk_tok((b0, b0 + 1))
            request(cols(w_in, QW + CW) if n == 0 else akv_next)
            w(act, m)
            w(dve, m)
            head_norm_rope(ps[:, b0:b0 + 2, :], 4, HD2, TT, tq[:, 0], tq[:, 1],
                           lambda t: q[:, t, n * CW:(n + 1) * CW].rearrange("p (h d) -> p h d", d=HD2), bufs)
        settle(pe)
        for g in range(KV2):
            for t in range(NT2):
                i_ = pe.transpose(ps[:, g, t * P:(t + 1) * P], k[:, t, g * HD2:(g + 1) * HD2], ident)
        w(dve, T.inc(i_))
        V.inc(dve.tensor_copy(kT, ps[:, 0:2, :]))
        c.at = 0 + NT2 * 512 + 2048
        stg, qT = c(TT, CW), c(TT, CW)
        E, ET = c(2, CW), c(2, CW)
        mx, ngm, l, rl = (c(8) for _ in range(4))
        assert c.at <= NT2 * 512 + 2048 + 1536 + 256 + 1024 * 3 + 16
        settle(act, dve)
        scale = HD2 ** -0.5
        with loop(KV2, 0, pe=1 + 8 * 3, act=1 + 8 * 1, dve=1 + 8 * 5) as g:
            gcols = bass.ds(g * CW, CW)
            w(act, T.now())
            A.inc(act.activation(stg, q[:, :, gcols], ACT.Copy))
            w(pe, A.now(), V.now())
            for t in range(TT):
                for h in range(GROUP2):
                    i_ = pe.transpose(ps[:, t, h * P:(h + 1) * P], stg[:, t, h * P:(h + 1) * P], ident)
            w(dve, T.inc(i_))
            V.inc(dve.tensor_copy(qT, ps[:, 0:2, :]))
            free = V.now()
            read, ex, et, out = {}, {}, {}, {}

            def scores(u):
                h, t, par = u // 2, u % 2, u % 2
                w(pe, free, ex.get(u - 2))
                i_ = pe.matmul(ps[:, 2 + par, :], qT[:, t, h * P:(h + 1) * P],
                               kT[:, bass.ds(g, 1), :].rearrange("p a n -> p (a n)"), start=True, stop=True)
                w(dve, T.inc(i_))
                m = V.inc(dve.tensor_reduce(mx[:, u:u + 1], ps[:, 2 + par, :], AX.X, ALU.max))
                w(dve, m)
                return V.inc(dve.tensor_scalar(ngm[:, u:u + 1], mx[:, u:u + 1], -scale, None, ALU.mult))

            def exponentials(u, m):
                w(act, m, T.now())
                ex[u] = A.inc(act.activation(E[:, u % 2, :], ps[:, 2 + u % 2, :], ACT.Exp, bias=ngm[:, u:u + 1],
                                             scale=scale, accum_out=l[:, u:u + 1]))

            def transposes(u):
                par = u % 2
                w(pe, ex[u], *et.get(u - 2, ()))
                for j in range(NT2):
                    i_ = pe.transpose(ps[:, 4 + par, j * P:(j + 1) * P], E[:, par, j * P:(j + 1) * P], ident)
                w(dve, T.inc(i_), ex[u])
                m = V.inc(dve.tensor_copy(ET[:, par, :], ps[:, 4 + par, :]))
                et[u] = (m, V.inc(dve.reciprocal(rl[:, u:u + 1], l[:, u:u + 1])))

            def values(u):
                h, t, par = u // 2, u % 2, u % 2
                w(pe, et[u][0], out.get(u - 2))
                for j in range(NT2):
                    i_ = pe.matmul(ps[:, 6 + par, 0:P], ET[:, par, j * P:(j + 1) * P], v[:, j, bass.ds(g * HD2, HD2)],
                                   start=(j == 0), stop=(j == NT2 - 1))
                w(dve, T.inc(i_), et[u][1])
                out[u] = V.inc(dve.tensor_scalar(o[:, t, bass.ds(g * CW + h * P, P)], ps[:, 6 + par, 0:P],
                                                 rl[:, u:u + 1], None, ALU.mult))

            exponentials(0, scores(0))
            for u in range(8):
                m = scores(u + 1) if u < 7 else None
                transposes(u)
                if m is not None:
                    exponentials(u + 1, m)
                if u:
                    values(u - 1)
            values(7)

    def gdn_rows(qkv, c):
        wz, zf, zl, a_log, dt = c(KT, 32), c(512), c(CW), c(16), c(16)
        sq = c(2, 2, CW)
        w(act, V.now())
        load_row(a_log, "a_log")
        load_row(dt, "dt_bias")
        w(pe, A.now(), V.now())
        w(dve, narrow(ins["w_in_2"][0][:, 3584:3616], wz, wzs[1], 6, 2 * SEQ))
        V.inc(dve.tensor_copy(zf[0:32, :], ps[0:32, 6, :]))
        pick = const("pick")
        free = [T.now()] * 2
        for g in range(8):
            w(act, free[g % 2])
            sq_ok = A.inc(act.activation(sq[:, g % 2], qkv[:, 2 * g:2 * g + 2, :], ACT.Square))
            w(pe, sq_ok)
            for j in range(2):
                n = 2 * g + j
                i_ = pe.matmul(ps[0:16, 7, :], pick[:, 15 - n:31 - n], sq[:, g % 2, j, :], start=(n == 0), stop=(n == 15))
            free[g % 2] = T.inc(i_)
        w(dve, free[1], V.now())
        w(pe, V.inc(dve.tensor_copy(zl[0:16, :], ps[0:16, 7, :])))
        return zf, zl, a_log, dt

    def gdn_inputs(qkv, nxt):
        w_in, c0 = ins["w_in_2"][0], 512
        settle()
        c = Carve(start=24 * 512, end=arena_n - 2048 - 512)
        y, z = c(4, 2, SEQ), c(4, 2, SEQ)
        taps_all = vcol("gdn_conv").rearrange("p (b t) -> p b t", t=3)

        def one(ci, par, after, ends, between=None):
            b0 = 4 * par
            w(pe, *ends)
            m = chunk_feat(range(b0, b0 + 4), both=True)
            request(after)
            if between is not None:
                between()
            taps = ccur[:, par, 0:12].rearrange("p (b t) -> p b t", t=3)
            w(pool, V.now(), A.now())
            G.inc(pool.tensor_copy(taps, taps_all[:, bass.ds(ci * 4, 4), :]))
            xq = ps[:, b0:b0 + 4, :].rearrange("p b (s n) -> p b s n", s=2)
            w(act, m, G.now(), V.now(), A.now())
            for q in range(4):
                i_ = act.activation(y[:, q], xq[:, q], ACT.Copy, scale=taps[:, q, 1:2])
            w(dve, A.inc(i_), V.now())
            for q in range(4):
                dve.scalar_tensor_tensor(z[:, q, :, 1:SEQ], xq[:, q, :, 0:SEQ - 1], taps[:, q, 0:1], y[:, q, :, 1:SEQ],
                                         ALU.mult, ALU.add)
            V.inc(dve.tensor_copy(z[:, :, :, 0:1], y[:, :, :, 0:1]))
            w(dve, V.now())
            for q in range(4):
                dve.scalar_tensor_tensor(y[:, q, :, 0:SEQ - 1], xq[:, q, :, 1:SEQ], taps[:, q, 2:3],
                                         z[:, q, :, 0:SEQ - 1], ALU.mult, ALU.add)
            V.inc(dve.tensor_copy(y[:, :, :, SEQ - 1:SEQ], z[:, :, :, SEQ - 1:SEQ]))
            w(act, V.now())
            A.inc(act.activation(qkv[:, bass.ds(ci * 4, 4), :], y.rearrange("p b s n -> p b (s n)"), ACT.Silu))

        with loop(2, 2, act=4, dve=4, pool=2) as i:
            for par in range(2):
                ends = (V.back(2), A.back(2))
                one(i * 2 + par, par, cols(w_in, c0 + (i * 2 + par + 1) * CW), ends)
        rows = []
        one(4, 0, cols(w_in, c0 + 5 * CW), (V.back(2), A.back(2)), lambda: rows.extend(gdn_rows(qkv, c)))
        one(5, 1, nxt, (V.back(2), A.back(2)))
        return rows

    def gdn_scalars(sc, c, zf, zl, a_log, dt):
        la, t1, t2 = c(NT2, 16), c(NT2, 16), c(NT2, 16)
        rn = c(NT2, 2, GDN_HEADS)
        settle(act, pe, dve)
        lens = ps[:, 6, 0:64].rearrange("p (t a h) -> p t a h", t=NT2, a=2)
        for t in range(NT2):
            i_ = pe.transpose(ps[:, 6, 16 * t:16 * t + 16], zl[0:16, t * P:(t + 1) * P], ident[0:16, 0:16])
        w(act, T.inc(i_))
        A.inc(act.activation(rn, lens, ACT.Sqrt, bias=eps_col))
        w(dve, A.now())
        rn_ok = V.inc(dve.reciprocal(rn, rn))
        w(pe, rn_ok)
        for t in range(NT2):
            i_ = pe.transpose(ps[:, 1, 32 * t:32 * t + 32], zf[0:32, t * P:(t + 1) * P], ident[0:32, 0:32])
        m = T.inc(i_)
        z = ps[:, 1, 0:128].rearrange("p (t n) -> p t n", t=NT2)
        kinds = sc.rearrange("p k t d h -> p k t (d h)")
        w(act, m)
        A.inc(act.activation(kinds[:, 9], z[:, :, 0:16], ACT.Sigmoid))
        w(dve, A.now())
        V.inc(dve.tensor_tensor(t1, z[:, :, 16:32], bc(dt, 1, NT2), ALU.add))
        w(act, V.now())
        A.inc(act.activation(t2, t1, ACT.Abs))
        w(act, A.now())
        A.inc(act.activation(t2, t2, ACT.Exp, scale=-1.0))
        act.activation(a_log, a_log, ACT.Exp)
        w(act, A.now())
        A.inc(act.activation(t2, t2, ACT.Ln, bias=1.0))
        w(dve, A.now())
        V.inc(dve.scalar_tensor_tensor(t1, t1, 0.0, t2, ALU.max, ALU.add))
        w(dve, V.now())
        V.inc(dve.scalar_tensor_tensor(la, t1, -1.0, bc(a_log, 1, NT2), ALU.mult, ALU.mult))
        w(pe, V.now())
        flat = la.rearrange("p t n -> p (t n)")
        for j, name in enumerate(("cum_f", "cum_b", "ones_bd", "even", "odd")):
            i_ = pe.matmul(ps[:, 2 + j, 0:64], const(name), flat, start=True, stop=True)
        m = T.inc(i_)
        w(dve, m)
        res = [ps[:, 2 + j, 0:64].rearrange("p (t d h) -> p t d h", t=NT2, d=2) for j in range(5)]
        for d in range(2):
            dve.tensor_copy(sc[:, 0, :, d, :], res[d][:, :, d, :])
            dve.tensor_copy(sc[:, 7, :, d, :], rn[:, :, 1, :])
            i_ = dve.tensor_scalar(sc[:, 8, :, d, :], rn[:, :, 0, :], GDN_D ** -0.5, None, ALU.mult)
        V.inc(i_)
        w(dve, V.now())
        V.inc(dve.tensor_tensor(t1, ps[:, 4, 0:64].rearrange("p (t n) -> p t n", t=NT2), kinds[:, 0], ALU.subtract))
        w(act, V.now())
        act.activation(kinds[:, 2], kinds[:, 0], ACT.Exp)
        act.activation(kinds[:, 3], t1, ACT.Exp)
        for q in range(2):
            i_ = act.activation(kinds[:, 5 + q], ps[:, 5 + q, 0:64].rearrange("p (t n) -> p t n", t=NT2), ACT.Exp)
        w(dve, A.inc(i_))
        V.inc(dve.tensor_tensor(kinds[:, 1], kinds[:, 9], kinds[:, 7], ALU.mult))
        w(dve, V.now())
        dve.tensor_tensor(kinds[:, 3], kinds[:, 3], kinds[:, 7], ALU.mult)
        V.inc(dve.scalar_tensor_tensor(kinds[:, 4], kinds[:, 1], -1.0, kinds[:, 2], ALU.mult, ALU.mult))
        w(dve, V.now())
        V.inc(dve.tensor_tensor(kinds[:, 2], kinds[:, 2], kinds[:, 8], ALU.mult))

    def gdn_heads(qkv, sc, o, lo, hi):
        NM = NT2 * 2
        hn = lo(NK, NT2 * 2)
        PTn, NTm, XT, X, Y = lo(2, TT, P), lo(2, NT2, P), lo(2, NT2, P), lo(2, NT2, P), lo(2, NT2, P)
        BT = [lo(2, NT2, P) for _ in range(2)]
        Ig, Ib = BT
        decT = Y
        hc = lo(NK, NT2 * 2)
        R, PT, PD, S, qst, dl = hi(2, NT2, P), hi(2, TT, P), hi(TT, P), hi(2, 4, P), hi(SEQ), lo(2, NT2, P)
        kn = hi(CW)
        Sc = hi(2, 2, P)
        half = [raw[:, q].rearrange("p a b -> p (a b)") for q in range(2)]
        four = "p (d t n) -> p d t n"
        kd = [half[q][:, 0:NM * P].rearrange(four, d=2, t=NT2) for q in range(2)]
        XTr = half[0][:, NM * P:].rearrange(four, d=2, t=NT2)
        kst, vst = half[1][:, NM * P:NM * P + CW], half[1][:, NM * P + CW:]
        rowed = lambda a: a.rearrange("p k (t d) -> p k d t", d=2)
        chunks = {0: [(1, 0, 0), (1, 0, 1), (1, 1, 0), (1, 1, 1), (0, 0, 0), (0, 0, 1), (0, 1, 0), (0, 1, 1)]}
        chunks[1] = chunks[0][3::-1] + chunks[0][:3:-1]
        settle()
        for e in (act, dve):
            w(e, hi_ok[0].now(), hi_ok[1].now(), lo_ok[0].now(), lo_ok[1].now())
        negs = (const("neg_f"), const("neg_b"))
        lev = [const(f"level{b}") for b in LEVELS]
        for q in range(2):
            i_ = dve.memset(kd[q][64 - 64 * q:128 - 64 * q], 0.0)
        V.inc(i_)
        hd = rowed(hn)
        hr = rowed(hc)

        def block(h, j):
            return qkv[:, bass.ds(h + 8 * j, 1) if not isinstance(h, int) else slice(h + 8 * j, h + 8 * j + 1), :].rearrange("p a n -> p (a n)")

        def column(h):
            c_ = bass.ds(h, 1) if not isinstance(h, int) else slice(h, h + 1)
            return sc.rearrange("p k t d h -> p k (t d) h")[:, :, :, c_].rearrange("p k n a -> p k (n a)")

        def prepare(h, ready):
            w(dve, *ready["hn free"])
            v0 = V.inc(dve.tensor_copy(hn, column(h)))
            w_apart(pool, v0, ready["BT free"])
            w_apart(act, v0, ready["BT free"])
            mk = A.inc(act.activation(kn, block(h, 1), ACT.Copy))
            ready["v"] = A.inc(act.activation(vst, block(h, 2), ACT.Copy))
            for d in range(2):
                for t in range(NT2):
                    if t < 2:
                        ig = pool.tensor_scalar(Ig[:, d, t, :], ident, hd[:, 0, d, t:t + 1], None, ALU.mult)
                    else:
                        ia = act.activation(Ig[:, d, t, :], ident, ACT.Copy, scale=hd[:, 0, d, t:t + 1])
            mg = (G.inc(ig), A.inc(ia))
            for d in range(2):
                for t in range(NT2):
                    if t < 1:
                        ig = pool.tensor_scalar(Ib[:, d, t, :], ident, hd[:, 1, d, t:t + 1], None, ALU.mult)
                    else:
                        ia = act.activation(Ib[:, d, t, :], ident, ACT.Copy, scale=hd[:, 1, d, t:t + 1])
            mi = (G.inc(ig), A.inc(ia))
            kh, qh = kn, block(h, 0)
            w(pe, ready["banks free"], mk)
            for t in range(NT2):
                pe.matmul(ps[:, 4, t * P:(t + 1) * P], kh[:, t * P:(t + 1) * P], kh[:, t * P:(t + 1) * P], start=True, stop=True)
            for t in range(TT):
                i_ = pe.matmul(ps[:, 5, t * P:(t + 1) * P], kh[:, t * P:(t + 1) * P], qh[:, t * P:(t + 1) * P], start=True, stop=True)
            mk = T.inc(i_)
            yield
            yield
            w(pe, *mg)
            for d in range(2):
                i_ = pe.matmul(ps[:, d, :], const("ones_bd"), Ig[:, d].rearrange("p t n -> p (t n)"), start=True, stop=True)
            mr = T.inc(i_)
            yield
            w(pe, *mi)
            for d in range(2):
                i_ = pe.matmul(ps[:, 2 + d, :], const("ones_bd"), Ib[:, d].rearrange("p t n -> p (t n)"), start=True, stop=True)
            mb = T.inc(i_)
            yield
            w(dve, mr)
            for d in range(2):
                for t in range(NT2):
                    i_ = dve.scalar_tensor_tensor(decT[:, d, t, :], ps[:, d, t * P:(t + 1) * P], hd[:, 0, d, t:t + 1],
                                                  negs[d], ALU.subtract, ALU.add)
                md = V.inc(i_)
                w(act, md)
                me = A.inc(act.activation(decT[:, d], decT[:, d], ACT.Exp))
                yield
            for d in range(2):
                w(dve, me, mk)
                for t in range(NT2):
                    if t == 2:
                        yield
                    kq = ps[:, 5, t * P:(t + 1) * P]
                    if t < TT:
                        dve.scalar_tensor_tensor(PTn[:, d, t], kq, hd[:, 7, d, t:t + 1], decT[:, d, t], ALU.mult, ALU.mult)
                    i_ = dve.scalar_tensor_tensor(NTm[:, d, t], ps[:, 4, t * P:(t + 1) * P], hd[:, 7, d, t:t + 1],
                                                  decT[:, d, t], ALU.mult, ALU.mult)
                mn = ready["mn"] = V.inc(i_)
                yield
            w(dve, mn, mb)
            for d in range(2):
                mn = V.inc(dve.tensor_tensor(NTm[:, d], NTm[:, d], ps[:, 2 + d, :].rearrange("p (t n) -> p t n", t=NT2), ALU.mult))
                yield
            bt_ok = {}

            def level_part(j, free):
                w(pool, mn, free)
                bt_ok[j] = G.inc(pool.tensor_tensor(BT[(j - 1) % 2], NTm, lev0_bc(lev[j]), ALU.mult))

            w(dve, mn, mb)
            v1 = V.inc(dve.tensor_tensor(XT, NTm, lev0_bc(lev[0]), ALU.mult))
            level_part(1, mb)
            yield
            w(dve, v1)
            v1 = V.inc(dve.tensor_tensor(XT, lev0_bc(ident), XT, ALU.subtract))
            level_part(2, mb)
            yield
            xt_ok = [v1, v1]
            for j in range(1, len(LEVELS)):
                bt = BT[(j - 1) % 2]
                x_ok, y_ok = [None, None], [None, None]
                for d in range(2):
                    w(pe, xt_ok[d])
                    for t in range(NT2):
                        i_ = pe.transpose(ps[:, d, t * P:(t + 1) * P], XT[:, d, t, :], ident)
                    w(act, T.inc(i_))
                    x_ok[d] = A.inc(act.activation(X[:, d].rearrange("p t n -> p (t n)"), ps[:, d, :], ACT.Copy))
                    yield
                for d in range(2):
                    w(pe, x_ok[d], bt_ok[j])
                    for t in range(NT2):
                        i_ = pe.matmul(ps[:, 2 + d, t * P:(t + 1) * P], bt[:, d, t, :], X[:, d, t, :], start=True, stop=True)
                    mt = T.inc(i_)
                    w(act, mt)
                    y_ok[d] = A.inc(act.activation(Y[:, d].rearrange("p t n -> p (t n)"), ps[:, 2 + d, :], ACT.Copy))
                    yield
                if j + 2 < len(LEVELS):
                    level_part(j + 2, mt)
                if j + 1 == len(LEVELS):
                    w(dve, ready["rec"])
                for d in range(2):
                    w(pe, y_ok[d])
                    for t in range(NT2):
                        i_ = pe.matmul(ps[:, 4 + d, t * P:(t + 1) * P], Y[:, d, t, :], XT[:, d, t, :], start=True, stop=True)
                    w(dve, T.inc(i_))
                    to = XT if j + 1 < len(LEVELS) else XTr
                    xt_ok[d] = V.inc(dve.tensor_tensor(to[:, d].rearrange("p t n -> p (t n)"), XT[:, d].rearrange("p t n -> p (t n)"),
                                                       ps[:, 4 + d, :], ALU.subtract))
                    yield
            ready["XTr"] = xt_ok[1]
            ready["BT free"] = mt
            ready["banks free"] = xt_ok[1]

        def operands(h, ready):
            w_apart(act, ready["out"])
            act.activation(kst, block(h, 1), ACT.Copy)
            ready["kst"] = A.inc(act.activation(qst, block(h, 0)[:, 0:SEQ], ACT.Copy))
            w(dve, ready["out"], ready["mn"])
            dve.tensor_copy(PT, PTn)
            mc = V.inc(dve.tensor_copy(hc, hn))
            ready["hn free"] = (mc,)
            w(pe, ready["v"], ready["out"])
            for t in range(NT2):
                pe.transpose(ps[:, 6, t * P:(t + 1) * P], kn[:, t * P:(t + 1) * P], ident)
                i_ = pe.transpose(ps[:, 7, t * P:(t + 1) * P], vst[:, t * P:(t + 1) * P], ident)
            mt = T.inc(i_)
            yield
            w(dve, mt, mc)
            for d in range(2):
                for q in range(2):
                    rw = slice(64 * q, 64 * q + 64)
                    dve.tensor_tensor(kd[q][rw, d], ps[rw, 6, :].rearrange("p (t n) -> p t n", t=NT2), bc(hr[rw, 3, d, :], 2, P), ALU.mult)
                i_ = dve.tensor_tensor(R[:, d], ps[:, 7, :].rearrange("p (t n) -> p t n", t=NT2), bc(hr[:, 9, d, :], 2, P), ALU.mult)
            ready["R"] = V.inc(i_)
            yield

        def state_at(d, n):
            return S[:, d, n, :] if n < 4 else Sc[:, d, n - 4, :]

        def recur(h, ready):
            s_ok = [ready["R"]] * 2
            r_ok = [ready["R"]] * 2
            slot = [None, None]
            d_ok = [None, None]
            for st in range(8):
                where = []
                for d in range(2):
                    seq, tl, q = chunks[d][st]
                    t = 2 * seq + tl
                    nx = (5, 4, 5, None, None, None, None, None)[st]
                    if 3 <= st < 7:
                        nx = 2 * chunks[d][st + 1][1] + chunks[d][st + 1][2]
                    where.append((t, q, slice(64 * q, 64 * q + 64), nx))
                if st:
                    for d in range(2):
                        t, q, rw, nx = where[d]
                        w(pe, s_ok[d], ready["kst"])
                        i_ = pe.matmul(ps[:, 6 + d, 0:P], kst[:, t * P:(t + 1) * P], state_at(d, slot[d]), start=True, stop=True)
                        w(dve, T.inc(i_), r_ok[d])
                        r_ok[d] = V.inc(dve.scalar_tensor_tensor(R[rw, d, t, :], ps[rw, 6 + d, 0:P], hr[rw, 4, d, t:t + 1],
                                                                 R[rw, d, t, :], ALU.mult, ALU.add))
                    yield
                for d in range(2):
                    t, q, rw, nx = where[d]
                    w(pe, r_ok[d], ready["XTr"])
                    i_ = pe.matmul(ps[:, 6 + d, P:2 * P], XTr[:, d, t, :], R[:, d, t, :], start=True, stop=True)
                    w(act, T.inc(i_))
                    d_ok[d] = A.inc(act.activation(dl[:, d, t, :], ps[:, 6 + d, P:2 * P], ACT.Copy))
                yield
                if st < 7:
                    for d in range(2):
                        t, q, rw, nx = where[d]
                        w(pe, d_ok[d])
                        i_ = pe.matmul(ps[:, 6 + d, 2 * P:3 * P], kd[q][:, d, t, :], dl[:, d, t, :], start=True, stop=True)
                        w(dve, T.inc(i_), s_ok[d])
                        if st == 0:
                            s_ok[d] = V.inc(dve.tensor_copy(state_at(d, nx), ps[:, 6 + d, 2 * P:3 * P]))
                        else:
                            s_ok[d] = V.inc(dve.scalar_tensor_tensor(state_at(d, nx), state_at(d, slot[d]), hr[:, 5 + q, d, t:t + 1],
                                                                     ps[:, 6 + d, 2 * P:3 * P], ALU.mult, ALU.add))
                        slot[d] = nx
                    yield
            w(pe, d_ok[0], d_ok[1], s_ok[0], s_ok[1])
            for t in range(TT):
                for d in range(2):
                    i_ = pe.matmul(ps[:, 6, t * P:(t + 1) * P], PT[:, d, t, :], dl[:, d, t, :], start=(d == 0), stop=(d == 1))
            w(act, T.inc(i_))
            for t in range(TT):
                i_ = act.activation(PD[:, t], ps[:, 6, t * P:(t + 1) * P], ACT.Copy, scale=hr[:, 8, 0, t:t + 1])
            ma = A.inc(i_)
            yield
            for d in range(2):
                for t in range(TT):
                    for q in range(2):
                        i_ = pe.matmul(ps[64 * q:64 * q + 64, 7, (2 * d + t) * P:(2 * d + t + 1) * P],
                                       qst[:, (2 * t + q) * CHUNK:(2 * t + q + 1) * CHUNK], S[:, d, 2 * t + q, :], start=True, stop=True)
            mt = T.inc(i_)
            yield
            w(dve, mt, ma)
            for d in range(2):
                if d:
                    w(dve, md)
                for t in range(TT):
                    c_ = bass.ds(h * P, P) if not isinstance(h, int) else slice(h * P, h * P + P)
                    dst = PD[:, t, :] if d == 0 else o[:, t, c_]
                    i_ = dve.scalar_tensor_tensor(dst, ps[:, 7, (2 * d + t) * P:(2 * d + t + 1) * P], hr[:, 2, d, t:t + 1],
                                                  PD[:, t, :], ALU.mult, ALU.add)
                md = V.inc(i_)
            ready["out"] = md
            ready["rec"] = md
            yield

        def braid(a, b):
            a, b = iter(a), iter(b)
            while any([next(x, "end") is None for x in (a, b)]):
                pass

        def after(first, second):
            yield from first
            yield from second

        def done():
            return {"hn free": (V.now(), A.now(), G.now()), "BT free": T.now(), "banks free": V.now(), "rec": V.now(),
                    "out": V.now(), "mn": V.now(), "R": V.now(), "XTr": V.now(), "kst": A.now()}

        ready = done()
        for _ in after(prepare(0, ready), operands(0, ready)):
            pass
        with loop(GDN_HEADS - 1, 0, **GDN_PER) as h:
            ready = done()
            braid(prepare(h + 1, ready), after(recur(h, ready), operands(h + 1, ready)))
        for _ in recur(GDN_HEADS - 1, done()):
            pass
        settle(sp)

    def lev0_bc(m):
        return bc(bc(m, 1, NT2), 1, 2)

    def layer_c(nxt, ctx):
        w_in = ins["w_in_2"][0]
        settle()
        w(act, L.now())
        w(dve, L.now())
        norm_split(ctx, 1, Carve(), modcol[:, 1, :, 1], modcol[:, 0, :, 1])
        norm_split(resid, 0, Carve(), modcol[:, 1, :, 0], modcol[:, 0, :, 0])
        attn = Carve(start=arena_n - 2048)(TT, D)
        attention_2(cols(w_in, 512), attn)
        Z0 = 4640
        c = Carve()
        qkv = c(24, CW)
        rows = gdn_inputs(qkv, cols(w_in, Z0))
        gdn = c(TT, D)
        sc = c(NK, NT2, 2, GDN_HEADS)
        gdn_scalars(sc, Carve(start=c.at, end=24 * CW + 4096), *rows)
        gdn_heads(qkv, sc, gdn, Carve(c.at, arena_n - 2048), Carve(-XS // 2, 0))
        settle()
        c = Carve()
        z, gt = c(TT, D), c(TT, 2 * D)
        y = c(TT, D)
        sq = c(TT * D)
        st = c(16)
        gain = c(GDN_D)
        assert c.at <= 24 * CW
        load_row(gain, "gdn_norm")
        reads = [A.now()] * 4
        for j in range(6):
            b0 = 2 * (j % 4)
            w(pe, reads[j - 4] if j >= 4 else None)
            m = chunk_tok((b0, b0 + 1))
            request(cols(w_in, Z0 + (j + 1) * CW) if j < 5 else cols(ins["w_pa_2"][0], 0))
            w(act, m)
            dst = z[:, :, j * CW:(j + 1) * CW] if j < 2 else gt[:, :, (j - 2) * CW:(j - 1) * CW]
            A.inc(act.activation(dst, ps[:, b0:b0 + 2, :], ACT.Silu if j < 2 else ACT.Sigmoid))
            reads.append(A.now())
        nh = TT * GDN_HEADS
        A.inc(act.activation(sq, gdn.rearrange("p t n -> p (t n)"), ACT.Square, scale=GDN_D ** -0.5))
        w(dve, A.now())
        V.inc(dve.tensor_reduce(st[:, 0:nh], sq.rearrange("p (n d) -> p n d", d=GDN_D), AX.X, ALU.add))
        w(act, V.now())
        w(dve, rsqrt(st[:, 0:nh], st[:, 0:nh]), L.now())
        o3 = gdn.rearrange("p t (h d) -> p (t h) d", d=GDN_D)
        V.inc(dve.tensor_tensor(o3, o3, bc(st[:, 0:nh], 2, GDN_D), ALU.mult))
        w(dve, V.now())
        V.inc(dve.tensor_tensor(o3, o3, bc(gain, 1, nh), ALU.mult))
        w(dve, V.now())
        V.inc(dve.tensor_tensor(gdn, gdn, z, ALU.mult))
        settle()
        to_split(lambda t, k: attn[:, t, k * P:(k + 1) * P], 0, None)
        settle()
        to_split(lambda t, k: gdn[:, t, k * P:(k + 1) * P], 1, None)
        after = [cols(ins["w_pa_2"][0], CW), cols(ins["w_pd_2"][0], 0), cols(ins["w_pd_2"][0], CW), cols(ins["w_out_2"][0], 0)]
        prod = sq.rearrange("p (t n) -> p t n", t=TT)
        for j in range(4):
            n, br = j % 2, j // 2
            b0 = 2 * j
            m = chunk_tok((b0, b0 + 1), (0, 1) if br == 0 else (2, 3))
            request(after[j])
            yo, g_ = y[:, :, n * CW:(n + 1) * CW], gt[:, :, j * CW:(j + 1) * CW]
            w(dve, m, V.now(), A.now())
            if br == 0:
                V.inc(dve.tensor_tensor(yo, ps[:, b0:b0 + 2, :], g_, ALU.mult))
            else:
                pr = prod[:, :, 0:CW]
                V.inc(dve.tensor_tensor(pr, ps[:, b0:b0 + 2, :], g_, ALU.mult))
                w(dve, V.now())
                V.inc(dve.tensor_tensor(yo, yo, pr, ALU.add))
        settle()
        to_split(lambda t, k: y[:, t, k * P:(k + 1) * P], 0, None)
        add_product(ins["w_out_2"][0], nxt, gate=grow[:, 0, :], tmp=z[:, :, 0:CW])



    assert const_at["ident"] == (0, P)
    F.inc(act.dma_start(resid[:, :, :], ins["x"][0].rearrange("(t p) d -> p t d", p=P)), 16)
    F.inc(act.dma_start(cst[:, 0:P], ins["consts"][:, 0:P]), 16)
    F.inc(act.dma_start(vec[:, :], ins["vecs"]), 16)
    L.inc(act.dma_start(cst[:, P:], ins["consts"][:, P:]), 16)
    request(cols(ins["a_w_in"][0], 0))
    V.inc(dve.memset(unused[:, :], 0.0))
    V.inc(dve.memset(eps_col, EPS))
    w(pool, V.now())
    for e in (pe, act, dve, pool):
        w(e, F.now(), V.now())
    a_norm = vcol("attn_norm").rearrange("p (l k) -> p l k", k=KT)
    f_norm = vcol("ffn_norm").rearrange("p (l k) -> p l k", k=KT)

    def finish(src):
        settle(sp)
        stored.inc(sp.dma_start(out[0].rearrange("(t p) d -> p t d", p=P), src), 16)
        w(sp, stored.now())

    first_gu = [gate_up(ins["ffn_w_gate_up"][i], 0) for i in range(2)]
    norm_split(resid, 0, Carve(), a_norm[:, 0, :])
    layer_a(first_gu[0])
    norm_split(resid, 0, Carve(), f_norm[:, 0, :])
    ffn(ins["ffn_w_gate_up"][0], ins["ffn_w_down"][0], cols(ins["b_w_in"][0], 0))
    norm_split(resid, 0, Carve(), a_norm[:, 1, :])
    layer_b(first_gu[1])
    norm_split(resid, 0, Carve(), f_norm[:, 1, :])
    mod_bias = Carve(start=7936, end=arena_n - 2 * FT * SEQ)(6, D)
    load_row(mod_bias.rearrange("p a b -> p (a b)"), "b_mod")
    ffn(ins["ffn_w_gate_up"][1], ins["ffn_w_down"][1], cols(ins["w_mod_2"][0], 0))
    ctx = Carve(start=7936 + 6 * D)(TT, D)
    modulation(cols(ins["w_in_2"][0], 0), mod_bias, ctx)
    layer_c(gate_up(ins["w_up_2"][0], 0), ctx)
    norm_split(resid, 0, Carve(), modcol[:, 3, :, 0], modcol[:, 2, :, 0])
    conv = vcol("ffn_conv").rearrange("p (a t n) -> p a t n", a=2, t=4)
    ffn(ins["w_up_2"][0], ins["w_down_2"][0], None, conv, grow[:, 1, :])
    settle()
    c = Carve()
    st, sq, o, gain = c(8), c(D), c(TT, D), c(D)
    load_row(gain, "final_norm")
    rstd_of(resid, TT, D, st, sq)
    w(dve, V.now(), L.now())
    for t in range(TT):
        V.inc(dve.scalar_tensor_tensor(o[:, t, :], resid[:, t, :], st[:, t:t + 1], gain, ALU.mult, ALU.mult))
    finish(o)




def pack(parts):
    at, n = {}, 0
    for name, a in parts:
        at[name] = (n, n + a.shape[-1])
        n += a.shape[-1]
    return np.ascontiguousarray(np.concatenate([a for _, a in parts], -1)), at


def by_partition(v):
    a = np.asarray(v)
    a = a.reshape(-1, a.shape[-1] // P, P)
    return np.ascontiguousarray(a.reshape(-1, P).T)


_WEIGHTS = ["x", "a_w_in", "a_w_out", "b_w_in", "b_w_gate_f", "b_w_gate_b", "b_w_out", "ffn_w_gate_up",
            "ffn_w_down", "ctx_2", "w_mod_2", "w_in_2", "w_pa_2", "w_pd_2", "w_out_2", "w_up_2", "w_down_2"]


def kernel(**inputs):
    import concourse.bacc as bacc
    from concourse.bass_utils import run_bass_kernel_spmd

    g = {k: np.asarray(v) for k, v in inputs.items()}
    consts, const_at = pack(list(constants().items()))
    conv = np.concatenate([g["ffn_conv_w_2"][0], g["ffn_conv_b_2"]], 0)
    conv = conv.reshape(4, 2, FT, P).transpose(3, 1, 0, 2).reshape(P, -1)
    gdn_conv = g["conv_qkv_w_2"][0].reshape(3, 24, P).transpose(2, 1, 0).reshape(P, -1)
    vecs, vec_at = pack([
        ("attn_norm", by_partition(g["attn_norm"])), ("ffn_norm", by_partition(g["ffn_norm"])),
        ("gla_bias", by_partition(np.concatenate([g["b_gate_bias_f"], g["b_gate_bias_b"]], 0))),
        ("c", by_partition(g["c_2"])), ("c_ctx", by_partition(g["c_ctx_2"][None])),
        ("ffn_conv", conv), ("gdn_conv", gdn_conv)])
    rows, row_at = pack([(n, g[s].reshape(-1)) for n, s in (
        ("b_out_norm", "b_out_norm"), ("q_norm", "q_norm_w_2"), ("k_norm", "k_norm_w_2"), ("a_log", "a_log_2"),
        ("dt_bias", "dt_bias_2"), ("gdn_norm", "gdn_norm_w_2"), ("final_norm", "final_norm_w_2"), ("b_mod", "b_mod_2"))]
        + [("a_gains", np.concatenate([g["a_q_norm"], g["a_k_norm"]], 0).reshape(-1))])
    arrays = {n: np.ascontiguousarray(g[n]) for n in _WEIGHTS}
    arrays.update(consts=consts, vecs=vecs, rows=rows, a_mask=attention_masks())

    nc = bacc.Bacc("TRN2", target_bir_lowering=False, num_devices=1)
    ins = {n: nc.dram_tensor(f"in_{n}", a.shape, F32, kind="ExternalInput").ap() for n, a in arrays.items()}
    out = nc.dram_tensor("out", (1, SEQ, D), F32, kind="ExternalOutput").ap()
    build(nc, ins, out, const_at, vec_at, row_at)
    r = run_bass_kernel_spmd(nc, [{f"in_{n}": a for n, a in arrays.items()}], core_ids=[0])
    return r.results[0]["out"]
```
